# Optimizing a Trainium2 kernel written in Bass

```python
import jax, jax.numpy as jnp
from jax import lax
import numpy as np

D_MODEL = 1024
BATCH = 1
SEQ = 512
DEPTH = 1

PLE_DIM = 256
GRID_W = 64
ATTN_HEAD_DIM = 64
ATTN_HEADS = (D_MODEL // 2) // ATTN_HEAD_DIM
ATTN_KV_HEADS = ATTN_HEADS // 4
RET_HEAD_DIM = 128
RET_HEADS = (D_MODEL // 2) // RET_HEAD_DIM
ATTN_Q_W = ATTN_HEADS * ATTN_HEAD_DIM
ATTN_KV_W = ATTN_KV_HEADS * ATTN_HEAD_DIM
RET_W = RET_HEADS * RET_HEAD_DIM
IN_SPLITS = (ATTN_Q_W, ATTN_KV_W, ATTN_KV_W, RET_W, RET_W, RET_W, RET_W, D_MODEL, D_MODEL)
IN_W = ATTN_Q_W + 2 * ATTN_KV_W + 4 * RET_W + 2 * D_MODEL
D_FF = 4 * D_MODEL
Q_BLOCK = 128
RET_CHUNK = 128
ROPE_THETA = 10000.0
NORM_EPS = 1e-6
GN_EPS = 1e-5

kernel_name = "hybrid_gqa_retention_gated_encoder"

def rms_norm(x, gain):
    x32 = x.astype(jnp.float32)
    y = x32 * lax.rsqrt(jnp.mean(x32 * x32, axis=-1, keepdims=True) + NORM_EPS)
    return (y * gain.astype(jnp.float32)).astype(x.dtype)

def axial_rope_tables(seq_len, head_dim):
    rows = seq_len // GRID_W
    n_axis = head_dim // 4
    freqs = ROPE_THETA ** (-jnp.arange(n_axis, dtype=jnp.float32) / n_axis)
    row = jnp.repeat(jnp.arange(rows, dtype=jnp.float32), GRID_W)
    col = jnp.tile(jnp.arange(GRID_W, dtype=jnp.float32), rows)
    ang = jnp.concatenate([row[:, None] * freqs, col[:, None] * freqs], axis=-1)
    return jnp.cos(ang), jnp.sin(ang)

def apply_rope(x, cos, sin):
    x32 = x.astype(jnp.float32)
    x1, x2 = jnp.split(x32, 2, axis=-1)
    c = cos[None, :, None, :]
    s = sin[None, :, None, :]
    return jnp.concatenate([x1 * c - x2 * s, x1 * s + x2 * c], axis=-1).astype(x.dtype)

def gqa_attention(q, k, v):
    b, s, _, hd = q.shape
    g = ATTN_HEADS // ATTN_KV_HEADS
    nb = s // Q_BLOCK
    qb = q.reshape(b, nb, Q_BLOCK, ATTN_KV_HEADS, g, hd).transpose(1, 0, 3, 4, 2, 5)
    kt = k.transpose(0, 2, 1, 3)
    vt = v.transpose(0, 2, 1, 3)
    scale = hd ** -0.5

    def block(qi):
        sc = jnp.einsum('bkgqd,bksd->bkgqs', qi, kt).astype(jnp.float32) * scale
        pr = jax.nn.softmax(sc, axis=-1).astype(vt.dtype)
        return jnp.einsum('bkgqs,bksd->bkgqd', pr, vt)

    o = lax.map(block, qb)
    return o.transpose(1, 0, 4, 2, 3, 5).reshape(b, s, ATTN_HEADS * hd)

def retention_direction(q, k, v, log_gamma, include_diag):
    b, h, s, dk = q.shape
    dv = v.shape[-1]
    c = RET_CHUNK
    nc = s // c
    qc = q.reshape(b, h, nc, c, dk)
    kc = k.reshape(b, h, nc, c, dk)
    vc = v.reshape(b, h, nc, c, dv)
    pos = jnp.arange(c, dtype=jnp.float32)
    lg = log_gamma[:, None]
    diff = pos[:, None] - pos[None, :]
    mask = (diff >= 0) if include_diag else (diff > 0)
    dmask = jnp.where(mask[None], jnp.exp(lg[:, :, None] * jnp.maximum(diff, 0.0)[None]), 0.0)
    scores = jnp.einsum('bhnid,bhnjd->bhnij', qc, kc) * dmask[None, :, None]
    y = jnp.einsum('bhnij,bhnje->bhnie', scores, vc)
    k_dec = jnp.exp(lg * (c - 1 - pos))
    kv = jnp.einsum('bhnjd,bhnje->nbhde', kc * k_dec[None, :, None, :, None], vc)
    chunk_decay = jnp.exp(log_gamma * c)[None, :, None, None]

    def step(state, kv_n):
        return state * chunk_decay + kv_n, state

    _, prev = lax.scan(step, jnp.zeros((b, h, dk, dv), jnp.float32), kv)
    q_dec = jnp.exp(lg * (pos + 1.0))
    y = y + jnp.einsum('bhnid,nbhde->bhnie', qc * q_dec[None, :, None, :, None], prev)
    return y.reshape(b, h, s, dv)

def bidirectional_retention(q, k, v, decay_logit):
    log_g = jax.nn.log_sigmoid(decay_logit.astype(jnp.float32))
    qt = q.astype(jnp.float32).transpose(0, 2, 1, 3) * (RET_HEAD_DIM ** -0.5)
    kt = k.astype(jnp.float32).transpose(0, 2, 1, 3)
    vt = v.astype(jnp.float32).transpose(0, 2, 1, 3)
    fwd = retention_direction(qt, kt, vt, log_g[0], True)
    flip = lambda a: jnp.flip(a, axis=2)
    bwd = flip(retention_direction(flip(qt), flip(kt), flip(vt), log_g[1], False))
    return fwd + bwd

def hybrid_layer(x, p_i, mix_norm, w_in, attn_q_norm, attn_k_norm, ret_decay_logit, ret_norm_gain,
                 w_attn_o, w_ret_o, w_out, mlp_norm, w_up, w_down, ple_norm, w_ple_gate, w_ple,
                 rope_a, rope_r):
    b, s, _ = x.shape
    dt = x.dtype
    h = rms_norm(x, mix_norm)
    proj = h @ w_in
    split_idx = [int(i) for i in np.cumsum(IN_SPLITS)[:-1]]
    aq, ak, av, rq, rk, rv, rg, gate_a, gate_r = jnp.split(proj, split_idx, axis=-1)

    aq = rms_norm(aq.reshape(b, s, ATTN_HEADS, ATTN_HEAD_DIM), attn_q_norm)
    ak = rms_norm(ak.reshape(b, s, ATTN_KV_HEADS, ATTN_HEAD_DIM), attn_k_norm)
    av = av.reshape(b, s, ATTN_KV_HEADS, ATTN_HEAD_DIM)
    aq = apply_rope(aq, *rope_a)
    ak = apply_rope(ak, *rope_a)
    attn_out = gqa_attention(aq, ak, av).astype(dt) @ w_attn_o

    rq = apply_rope(rq.reshape(b, s, RET_HEADS, RET_HEAD_DIM), *rope_r)
    rk = apply_rope(rk.reshape(b, s, RET_HEADS, RET_HEAD_DIM), *rope_r)
    rv = rv.reshape(b, s, RET_HEADS, RET_HEAD_DIM)
    ry = bidirectional_retention(rq, rk, rv, ret_decay_logit)
    mu = jnp.mean(ry, axis=-1, keepdims=True)
    var = jnp.mean(jnp.square(ry - mu), axis=-1, keepdims=True)
    ry = ((ry - mu) * lax.rsqrt(var + GN_EPS)).transpose(0, 2, 1, 3).reshape(b, s, RET_W)
    ry = ry * ret_norm_gain.astype(jnp.float32) * jax.nn.silu(rg.astype(jnp.float32))
    ret_out = ry.astype(dt) @ w_ret_o

    merged = jax.nn.sigmoid(gate_a) * attn_out + jax.nn.sigmoid(gate_r) * ret_out
    x = x + merged @ w_out

    hm = rms_norm(x, mlp_norm)
    x = x + jnp.square(jax.nn.relu(hm @ w_up)) @ w_down

    gate = jax.nn.sigmoid(rms_norm(x, ple_norm) @ w_ple_gate)
    x = x + gate * (p_i.astype(dt) @ w_ple)
    return x

def setup_inputs(seed: int = 0) -> dict:
    key = jax.random.key(seed)
    ks = jax.random.split(key, 20)
    f32 = jnp.float32

    def w(k, shape, fan_in):
        return jax.random.normal(k, shape, f32) * (fan_in ** -0.5)

    def gain(k, shape):
        return 1.0 + 0.05 * jax.random.normal(k, shape, f32)

    gamma0 = 1.0 - 2.0 ** (-5.0 - jnp.arange(RET_HEADS, dtype=f32))
    logit0 = jnp.log(gamma0) - jnp.log1p(-gamma0)
    decay_logit = logit0[None, None, :] + 0.05 * jax.random.normal(ks[5], (DEPTH, 2, RET_HEADS), f32)

    return {
        "x": jax.random.normal(ks[0], (BATCH, SEQ, D_MODEL), f32),
        "p": jax.random.normal(ks[1], (DEPTH, BATCH, SEQ, PLE_DIM), f32),
        "mix_norm": gain(ks[2], (DEPTH, D_MODEL)),
        "w_in": w(ks[3], (DEPTH, D_MODEL, IN_W), D_MODEL),
        "attn_q_norm": gain(ks[4], (DEPTH, ATTN_HEAD_DIM)),
        "attn_k_norm": gain(ks[6], (DEPTH, ATTN_HEAD_DIM)),
        "ret_decay_logit": decay_logit,
        "ret_norm_gain": gain(ks[7], (DEPTH, RET_W)),
        "w_attn_o": w(ks[8], (DEPTH, ATTN_Q_W, D_MODEL), ATTN_Q_W),
        "w_ret_o": w(ks[9], (DEPTH, RET_W, D_MODEL), RET_W),
        "w_out": w(ks[10], (DEPTH, D_MODEL, D_MODEL), D_MODEL),
        "mlp_norm": gain(ks[11], (DEPTH, D_MODEL)),
        "w_up": w(ks[12], (DEPTH, D_MODEL, D_FF), D_MODEL),
        "w_down": w(ks[13], (DEPTH, D_FF, D_MODEL), D_FF),
        "ple_norm": gain(ks[14], (DEPTH, D_MODEL)),
        "w_ple_gate": w(ks[15], (DEPTH, D_MODEL, D_MODEL), D_MODEL),
        "w_ple": w(ks[16], (DEPTH, PLE_DIM, D_MODEL), PLE_DIM),
        "final_norm": gain(ks[17], (D_MODEL,)),
    }

def reference(x, p, mix_norm, w_in, attn_q_norm, attn_k_norm, ret_decay_logit, ret_norm_gain,
              w_attn_o, w_ret_o, w_out, mlp_norm, w_up, w_down, ple_norm, w_ple_gate, w_ple,
              final_norm):
    seq_len = x.shape[1]
    rope_a = axial_rope_tables(seq_len, ATTN_HEAD_DIM)
    rope_r = axial_rope_tables(seq_len, RET_HEAD_DIM)
    for i in range(DEPTH):
        x = hybrid_layer(x, p[i], mix_norm[i], w_in[i], attn_q_norm[i], attn_k_norm[i],
                         ret_decay_logit[i], ret_norm_gain[i], w_attn_o[i], w_ret_o[i], w_out[i],
                         mlp_norm[i], w_up[i], w_down[i], ple_norm[i], w_ple_gate[i], w_ple[i],
                         rope_a, rope_r)
    return rms_norm(x, final_norm)


_drawn_inputs = setup_inputs


def setup_inputs(seed=0):
    import zlib

    import numpy as np

    out = dict(_drawn_inputs(seed))
    spreads = {}
    factors = {'attn_q_norm': 8.0, 'attn_k_norm': 8.0, 'ret_norm_gain': 3.557, 'ple_norm': 27.29}
    for name, (base, spread) in spreads.items():
        noise = np.random.default_rng([zlib.crc32(name.encode()), seed]).standard_normal(out[name].shape)
        drawn = base * np.exp(spread * noise) if base else spread * noise
        out[name] = __import__('jax').numpy.asarray(drawn.astype(out[name].dtype))
    for name, factor in factors.items():
        out[name] = (out[name] * factor).astype(out[name].dtype)
    return out
```

```python
from contextlib import ExitStack, contextmanager

import concourse.bass as bass
from concourse import mybir

ALU = mybir.AluOpType
ACT = mybir.ActivationFunctionType
AX = mybir.AxisListType
F32 = mybir.dt.float32
F32R = mybir.dt.float32r
I32 = mybir.dt.int32

P = 128
D = 1024
SEQ = 512
PLE = 256
FF = 4 * D
C = 512
NT = SEQ // P
KD = D // P
HD = 64
NH = 8
KV = 2
RHD = 128
RH = 4
NORM_EPS = 1e-6
GN_EPS = 1e-5
RING = 4
SLAB = 1024

S_PLE0 = 0
S_AQ = S_PLE0 + 1
S_AKV = S_AQ + 4
S_PLE1 = S_AKV + 2
S_RET = S_PLE1 + 1
S_GATE = S_RET + 16
S_AO = S_GATE + 16
S_RO = S_AO + 4
S_OUT = S_RO + 4
S_UP0 = S_OUT + 8
S_MLP = S_UP0 + 4
S_DOWN7 = S_MLP + 7 * 8
S_PG = S_DOWN7 + 4
SLABS = S_PG + 8
NF = FF // C

T_ID = 0
T_CA = T_ID + P
T_SA = T_CA + NT * HD // 2
T_CR = T_SA + NT * HD // 2
T_SR = T_CR + NT * RHD // 2
T_END = T_SR + NT * RHD // 2
DELTA = SEQ + (NT - 1) * P


class Mark:

    def __init__(self, sem):
        self.sem, self.base, self.local = sem, 0, 0

    @property
    def value(self):
        return self.base + self.local

    def up(self):
        self.local += 1
        return self.value


@contextmanager
def counted(engine, count, marks):
    start = {m: m.value for m in marks}
    with engine.Fori(0, count) as i:
        for m, per in marks.items():
            m.base, m.local = i * per + start[m], 0
        yield i
        for m, per in marks.items():
            assert m.local == per, (m.sem, m.local, per)
    for m, per in marks.items():
        m.base, m.local = start[m] + count * per, 0


def build(nc, slabs, x_in, p_in, tables, delta_in, norms, q_gain, k_gain, ret_gain, fin_gain,
          decay, ple_spill, out):
    ctx = ExitStack()
    with ctx:
        sem = lambda name: ctx.enter_context(nc.semaphore(name))
        sb = lambda n, w, dt=F32: ctx.enter_context(nc.sbuf_tensor(n, [P, w], dt))

        ops = sb("ops", 24576, F32R)
        fp = sb("fp", 4096 + 8192 + 8192 + 2048 + 2048 + 896)
        tab = sb("tab", T_END)
        gains = sb("gains", 24 + HD + HD + RH * RHD + 2 * RH)
        rope_tmp = sb("rope_tmp", 512)
        small = sb("small", 256)
        ps = [ctx.enter_context(nc.psum_tensor(f"bank{b}", [P, C], F32)) for b in range(8)]

        def region(t, a, n):
            return t[:, a:a + n]

        w_hi = region(ops, 0, 4096).rearrange("p (s n) -> p s n", s=RING)
        w_lo = region(ops, 4096, 4096).rearrange("p (s n) -> p s n", s=RING)
        R1, R2 = 8192, 16384
        r1_hi = region(ops, R1, 4096).rearrange("p (k n) -> p k n", n=C)
        r1_lo = region(ops, R1 + 4096, 4096).rearrange("p (k n) -> p k n", n=C)
        xt_hi = region(ops, R2, 4096).rearrange("p (k n) -> p k n", n=C)
        xt_lo = region(ops, R2 + 4096, 4096).rearrange("p (k n) -> p k n", n=C)
        pt_hi = region(ops, R2, 1024).rearrange("p (k n) -> p k n", n=C)
        pt_lo = region(ops, R2 + 1024, 1024).rearrange("p (k n) -> p k n", n=C)
        q_st = region(ops, R2, 1024).rearrange("p (h n) -> p h n", h=2)
        k_st = region(ops, R2 + 1024, 2048).rearrange("p (g s n) -> p g s n", g=KV, s=2)
        v_st = region(ops, R2 + 3072, 1024).rearrange("p (g t n) -> p g t n", g=KV, t=NT)
        prt_hi = region(ops, R2 + 4096, 2048).rearrange("p (k n) -> p k n", n=C)
        prt_lo = region(ops, R2 + 6144, 2048).rearrange("p (k n) -> p k n", n=C)
        rq_t = region(ops, R2, 1024).rearrange("p (s n) -> p s n", s=2)
        rk_t = region(ops, R2 + 1024, 1024).rearrange("p (s n) -> p s n", s=2)
        rv_st = region(ops, R2 + 2048, 1024).rearrange("p (t n) -> p t n", t=NT)
        at_hi, at_lo = prt_hi, prt_lo
        ry_hi = region(ops, R2, 2048).rearrange("p (k n) -> p k n", n=C)
        ry_lo = region(ops, R2 + 2048, 2048).rearrange("p (k n) -> p k n", n=C)

        f32 = lambda ap: ap.bitcast(F32)

        raw = region(fp, 0, 4096).rearrange("p (s n) -> p s n", s=RING)
        RR, GG = 4096, 12288
        ret = region(fp, RR, 8192).rearrange("p (c t n) -> p c t n", c=4, t=NT)
        x0 = region(fp, RR, 4096).rearrange("p (t n) -> p t n", t=NT)
        ple_w = region(fp, RR + 4096, 4096).rearrange("p (t n) -> p t n", t=NT)
        merged = region(fp, RR, 4096).rearrange("p (m n) -> p m n", n=C)
        xs = region(fp, RR + 4096, 4096).rearrange("p (t n) -> p t n", t=NT)
        ple_r = region(fp, RR, 4096).rearrange("p (t n) -> p t n", t=NT)
        gate = region(fp, GG, 8192).rearrange("p (m n) -> p m n", n=C)
        q_raw = region(fp, GG, 2048).rearrange("p (t n) -> p t n", t=NT)
        k_raw = region(fp, GG + 2048, 512).rearrange("p (t n) -> p t n", t=NT)
        p_sb = region(fp, GG + 4096, 1024).rearrange("p (t n) -> p t n", t=NT)
        squares = region(fp, GG + 5120, 1024)
        q_sq = region(fp, GG + 6144, 512).rearrange("p (t n) -> p t n", t=NT)
        q_rot = region(fp, GG + 6656, 512).rearrange("p (t n) -> p t n", t=NT)
        k_rot = region(fp, GG + 7168, 512).rearrange("p (t n) -> p t n", t=NT)
        stage = region(fp, GG, 2048).rearrange("p (m n) -> p m n", n=C)
        fin_g = region(fp, GG + 2048, 1024)
        squares2 = region(fp, GG + 3072, 1024)
        out_sb = region(fp, GG + 4096, 4096).rearrange("p (t n) -> p t n", t=NT)
        sig = region(fp, GG + 4096, 4096).rearrange("p (c t n) -> p c t n", c=2, t=NT)
        PP = GG + 8192
        prob = region(fp, PP, 2048).rearrange("p (t n) -> p t n", t=NT)
        sc_f = region(fp, PP, 1024).rearrange("p (b n) -> p b n", b=2)
        r_rot = region(fp, PP, 1024).rearrange("p (c t n) -> p c t n", c=2, t=NT)
        delta = region(fp, PP + 1024, DELTA)
        ot = region(fp, PP + 2048, 2048).rearrange("p (k n) -> p k n", n=C)
        mask = region(fp, PP + 4096, DELTA)
        ident = tab[:, T_ID:T_ID + P]
        cos_a = tab[:, T_CA:T_SA].rearrange("p (t d) -> p t d", t=NT)
        sin_a = tab[:, T_SA:T_CR].rearrange("p (t d) -> p t d", t=NT)
        cos_r = tab[:, T_CR:T_SR].rearrange("p (t d) -> p t d", t=NT)
        sin_r = tab[:, T_SR:T_END].rearrange("p (t d) -> p t d", t=NT)
        mix_g, mlp_g, ple_g = gains[:, 0:8], gains[:, 8:16], gains[:, 16:24]
        qg = gains[:, 24:88]
        kg = gains[:, 88:152]
        rg_g = gains[:, 152:664]
        dec = gains[:, 664:672]
        ss = small[:, 0:4]
        rstd = small[:, 4:8]
        inv_ms = small[:, 8:12]
        hss = small[:, 12:20]
        hr = small[:, 20:28]
        nwt = small[:, 28:44]
        mx = small[:, 44:48]
        nb = small[:, 48:52]
        den = small[:, 52:56]
        rden = small[:, 56:60]
        lg = small[:, 60:68]
        lt = small[:, 68:116].rearrange("p (a n) -> p a n", n=8)
        bst = small[:, 116:140].rearrange("p (t n) -> p t n", t=NT)
        mv = small[:, 140:148].rearrange("p (t n) -> p t n", t=NT)
        rvar = small[:, 148:152]
        otmp = rope_tmp[:, :]

        s_slab = [sem(f"slab_landed{n}") for n in range(RING)]
        s_hi = sem("slab_hi_made")
        s_lo = sem("slab_lo_made")
        s_used = sem("slab_used")
        s_fill = [sem(f"bank{b}_filled") for b in range(8)]
        s_drain = [sem(f"bank{b}_drained") for b in range(8)]
        s_ahi = sem("operand_hi_made")
        s_p = sem("p_landed")
        s_x = [sem(f"x_landed{t}") for t in range(NT)]
        s_tab = sem("tables_landed")
        s_dlt = sem("delta_landed")
        s_xr = sem("residual_landed")
        s_spill = sem("ple_spilled")
        s_pler = sem("ple_reloaded")
        s_fin = sem("final_gain_landed")
        s_out = sem("out_stored")
        s_ss = sem("squares_summed")
        s_xn = sem("x_normalised")
        s_rope = sem("roped")
        s_shift = sem("row_max_ready")
        s_prob = sem("probs_ready")
        s_otmp = sem("lo_half_copied")
        s_vst = sem("v_split")
        s_sct = sem("scores_split")
        s_mexp = sem("mask_exponent")
        s_mask = sem("mask_ready")
        s_dexp = sem("decay_exponent")
        s_du = sem("decay_exp_done")
        s_osp = sem("attention_out_split")
        s_rgs = sem("ret_gate_sigmoid")
        s_gs = sem("gate_sigmoid")
        s_ry = sem("ret_out_ready")
        s_mg = sem("merged_summed")
        s_mgs = sem("merged_split")
        s_xf = sem("x_final")
        s_hid = sem("hidden_squared")
        s_hids = sem("hidden_split")
        s_rs = sem("row_scale_ready")
        s_psig = sem("ple_gate_sigmoid")
        s_fo = sem("final_ready")
        s_dve = sem("dve_steps")
        s_act = sem("act_steps")

        LOW = [0, 1, 2, 3]
        HIGH = [4, 5, 6, 7]

        block = ctx.enter_context(nc.Block())

        @block.sync
        def _(sp):
            sp.dma_start(p_sb, p_in.rearrange("(t p) n -> p t n", p=P)).then_inc(s_p, 16)
            sp.dma_start(raw[:, 0, :], slabs[0]).then_inc(s_slab[0], 16)
            for t in range(NT):
                sp.dma_start(x0[:, t, :], x_in[t * P:(t + 1) * P, :]).then_inc(s_x[t], 16)
            for n in range(1, RING):
                sp.dma_start(raw[:, n, :], slabs[n]).then_inc(s_slab[n], 16)
            with sp.Fori(1, SLABS // RING) as i:
                for n in range(RING):
                    sp.wait_ge(s_lo, (i - 1) * RING + n + 1)
                    sp.dma_start(raw[:, n, :], slabs[bass.ds(i * RING + n, 1)].rearrange("a p n -> (a p) n"))\
                      .then_inc(s_slab[n], 16)

        @block.gpsimd
        def _(pool):
            with pool.Fori(0, SLABS // RING) as i:
                for n in range(RING):
                    pool.wait_ge(s_hi, i * RING + n + 1)
                    pool.tensor_tensor(w_lo[:, n, :], raw[:, n, :], f32(w_hi[:, n, :]), ALU.subtract)\
                        .then_inc(s_lo, 1)

        @block.tensor
        def _(pe):
            fill = [Mark(s_fill[b]) for b in range(8)]

            def begin(b):
                n = fill[b].up()
                if not (isinstance(n, int) and n == 1):
                    pe.wait_ge(s_drain[b], n - 1)

            def slab_start(s):
                pe.wait_ge(s_lo, s + 1)
                return not (isinstance(s, int) and s == 0)

            def three(bank, a_hi, a_lo, b_hi, b_lo, first, last, used, done):
                m = pe.matmul(bank, a_hi, b_hi, start=first, stop=False)
                if used:
                    m.then_inc(s_used, 1)
                pe.matmul(bank, a_hi, b_lo, start=False, stop=False)
                m = pe.matmul(bank, a_lo, b_hi, start=False, stop=last)
                if done is not None:
                    m.then_inc(s_fill[done], 1)

            def tile(s, j, kk, banks, x_hi, x_lo, k, k_end, tokens, n=C):
                used = slab_start(s) if kk == 0 else False
                cols = slice(kk * n, (kk + 1) * n)
                first, last = k == 0, k == k_end - 1
                for m, b in enumerate(banks):
                    if first:
                        begin(b)
                    wc = slice(kk * n + m * P, kk * n + (m + 1) * P)
                    xc = slice(m * P, (m + 1) * P)
                    done = b if last else None
                    if tokens:
                        three(ps[b][:, 0:n], x_hi[:, k, xc], x_lo[:, k, xc], w_hi[:, j, cols], w_lo[:, j, cols],
                              first, last, used and m == 0, done)
                    else:
                        three(ps[b][:, :], w_hi[:, j, wc], w_lo[:, j, wc], x_hi[:, k, :], x_lo[:, k, :],
                              first, last, used and m == 0, done)

            def slab(s, j, banks, x_hi, x_lo, k0, k_end, tokens, n=C):
                for kk in range(SLAB // n):
                    tile(s, j, kk, banks, x_hi, x_lo, k0 + kk, k_end, tokens, n)

            def turn(b, src):
                begin(b)
                for n in range(4):
                    m = pe.transpose(ps[b][:, n * P:(n + 1) * P], src(n), ident)
                m.then_inc(s_fill[b], 1)

            def turn_x(src, k0, banks):
                for n, b in enumerate(banks):
                    turn(b, lambda t, k=k0 + n: src[:, t, k * P:(k + 1) * P])

            pe.wait_ge(s_tab, 16 * 6)
            pe.wait_ge(s_p, 16)
            turn_x(p_sb, 0, [4, 5])
            for b in (4, 5):
                pe.wait_ge(s_drain[b], fill[b].value)
            slab(S_PLE0, 0, LOW, pt_hi, pt_lo, 0, 2, True)

            pe.wait_ge(s_xn, NT)
            turn_x(x0, 0, HIGH)
            turn_x(x0, 4, HIGH)
            for j in range(4):
                for b in (HIGH[2 * j % 4], HIGH[(2 * j + 1) % 4]):
                    pe.wait_ge(s_drain[b], fill[b].value - (1 if j < 2 else 0))
                slab(S_AQ + j, (S_AQ + j) % RING, LOW, r1_hi, r1_lo, 2 * j, KD, True)
            for j in range(2):
                slab(S_AKV + j, (S_AKV + j) % RING, HIGH, r1_hi, r1_lo, 4 * j, KD, True, n=2 * KV * HD)
            slab(S_PLE1, S_PLE1 % RING, LOW, pt_hi, pt_lo, 0, 2, True)
            pe.wait_ge(s_rope, 2)
            turn(5, lambda t: k_rot[:, t, :])

            prob_m = Mark(s_prob)

            def scores(e, g):
                for qt in range(NT):
                    b = HIGH[qt]
                    begin(b)
                    lhs = q_st[:, e, qt * P:(qt + 1) * P]
                    pe.matmul(ps[b][:, :], lhs, k_st[:, g, 0, :], start=True, stop=False)
                    pe.matmul(ps[b][:, :], lhs, k_st[:, g, 1, :], start=False, stop=True).then_inc(s_fill[b], 1)

            def turn_probs():
                for kt in range(NT):
                    b = HIGH[kt]
                    begin(b)
                    for qt in range(NT):
                        if kt == 0:
                            pe.wait_ge(s_prob, prob_m.up())
                        m = pe.transpose(ps[b][:, qt * P:(qt + 1) * P], prob[:, qt, kt * P:(kt + 1) * P], ident)
                    m.then_inc(s_fill[b], 1)

            def values(g):
                ready = [fill[HIGH[kt]].value for kt in range(NT)]
                begin(7)
                for kt in range(NT):
                    if kt < 3:
                        pe.wait_ge(s_drain[HIGH[kt]], ready[kt])
                    pe.matmul(ps[7][:, :], v_st[:, g, kt, :], prt_hi[:, kt, :], start=(kt == 0), stop=False)
                    m = pe.matmul(ps[7][:, :], v_st[:, g, kt, :], prt_lo[:, kt, :], start=False, stop=(kt == 3))
                m.then_inc(s_fill[7], 1)

            rope_m = Mark(s_rope)
            rope_m.local = 1

            def attention(s0, pair, g):
                def half(n):
                    j = n // 2
                    tile(s0 + j, j, n % 2, LOW, r1_hi, r1_lo, n, KD, True)
                pe.wait_ge(s_rope, rope_m.up())
                turn(4, lambda t: q_rot[:, t, :])
                q_ready = fill[4].value
                half(0)
                pe.wait_ge(s_drain[4], q_ready)
                scores(0, g)
                half(1)
                half(2)
                turn_probs()
                half(3)
                values(g)
                half(4)
                scores(1, g)
                half(5)
                half(6)
                turn_probs()
                half(7)
                values(g)

            pe.wait_ge(s_drain[5], fill[5].value)
            at_marks = {fill[0]: 1, fill[1]: 1, fill[2]: 1, fill[3]: 1, fill[4]: 5, fill[5]: 4, fill[6]: 4,
                        fill[7]: 6, prob_m: 8, rope_m: 1}
            for g in range(KV):
                with counted(pe, 2, at_marks) as i:
                    attention(S_RET + 8 * g + i * 4, 2 * g + i, g)

            vst_m, sct_m = Mark(s_vst), Mark(s_sct)
            rr_m = Mark(s_rope)
            rr_m.local = rope_m.value
            re_marks = {fill[0]: 1, fill[1]: 1, fill[2]: 1, fill[3]: 1, fill[4]: 2, fill[5]: 2, fill[6]: 2,
                        fill[7]: 2, vst_m: 1, sct_m: 4, rr_m: 2}
            with counted(pe, RH, re_marks) as u:
                s0 = S_GATE + u * 4

                def half(n):
                    tile(s0 + n // 2, n // 2, n % 2, LOW, r1_hi, r1_lo, n, KD, False)
                half(0)
                half(1)
                half(2)
                for b, c in ((4, 0), (5, 1)):
                    pe.wait_ge(s_rope, rr_m.up())
                    turn(b, lambda t, c=c: r_rot[:, c, t, :])
                ready = [fill[4].value, fill[5].value]
                half(3)
                pe.wait_ge(s_drain[4], ready[0])
                pe.wait_ge(s_drain[5], ready[1])
                for jt, b in enumerate((6, 7, 4, 5)):
                    begin(b)
                    kc = slice(jt * P, (jt + 1) * P)
                    three(ps[b][:, :], rk_t[:, 0, kc], rk_t[:, 1, kc], rq_t[:, 0, :], rq_t[:, 1, :],
                          True, True, False, b)
                half(4)
                half(5)
                pe.wait_ge(s_vst, vst_m.up())
                for b in (6, 7):
                    begin(b)
                    for e in range(2):
                        it = 2 * (b - 6) + e
                        for jt in range(NT):
                            if it == 0:
                                pe.wait_ge(s_sct, sct_m.up())
                            ic = slice(it * P, (it + 1) * P)
                            o = ps[b][:, e * 256:(e + 1) * 256]
                            pe.matmul(o, prt_hi[:, jt, ic], rv_st[:, jt, :], start=(jt == 0), stop=False)
                            m = pe.matmul(o, prt_lo[:, jt, ic], rv_st[:, jt, :], start=False, stop=(jt == 3))
                    m.then_inc(s_fill[b], 1)
                half(6)
                half(7)

            def project(s, banks, x_hi, x_lo, k_end, tokens, ready=None):
                for j in range(k_end // 2):
                    if ready:
                        ready(2 * j)
                    slab(s + j, (s + j) % RING, banks, x_hi, x_lo, 2 * j, k_end, tokens)

            project(S_AO, LOW, at_hi, at_lo, 4, False, lambda k: pe.wait_ge(s_osp, k + 2))
            pe.wait_ge(s_ry, NT)
            for k in range(4):
                turn(HIGH[k], lambda t, k=k: ret[:, 0, t, k * P:(k + 1) * P])
            project(S_AO + 2, LOW, at_hi, at_lo, 4, False)
            for b in HIGH:
                pe.wait_ge(s_drain[b], fill[b].value)
            project(S_RO, HIGH, ry_hi, ry_lo, 4, False)
            project(S_RO + 2, LOW, ry_hi, ry_lo, 4, False)

            project(S_OUT, HIGH, r1_hi, r1_lo, KD, True, lambda k: pe.wait_ge(s_mgs, k + 2))

            def chunk_and_turn(s, x_hi, x_lo, k_end):
                for j in range(k_end // 2):
                    if j == k_end // 2 - 1:
                        for b in HIGH:
                            pe.wait_ge(s_drain[b], fill[b].value)
                        turn_x(xs, 0, HIGH)
                    slab(s + j, (s + j) % RING, LOW, x_hi, x_lo, 2 * j, k_end, True)

            def chunk_from_turns(s, tokens):
                for j in range(4):
                    for n in (2 * j, 2 * j + 1):
                        if n == 2:
                            for b in LOW:
                                pe.wait_ge(s_drain[b], fill[b].value)
                            turn_x(xs, 4, LOW)
                        if n == 0:
                            for b in HIGH:
                                pe.wait_ge(s_drain[b], fill[b].value)
                        if n >= 4:
                            pe.wait_ge(s_drain[LOW[n - 4]], fill[LOW[n - 4]].value)
                        tile(s + j, j, n % 2, HIGH, xt_hi, xt_lo, n, KD, tokens)

            chunk_and_turn(S_OUT + 4, r1_hi, r1_lo, KD)
            chunk_from_turns(S_UP0, False)

            hid_m = Mark(s_hids)

            def down(s, slot, banks, first):
                for j in range(2):
                    if first:
                        for _ in range(2):
                            hid_m.up()
                        pe.wait_ge(s_hids, hid_m.value)
                    slab(s + j, slot + j, banks, r1_hi, r1_lo, 2 * j, 4, True)

            mlp_marks = {hid_m: 4}
            for b in LOW:
                mlp_marks[fill[b]] = 2
            for b in HIGH:
                mlp_marks[fill[b]] = 1
            with counted(pe, NF - 1, mlp_marks) as f:
                s0 = S_MLP + f * 8
                for j in range(4):
                    slab(s0 + j, j, LOW, xt_hi, xt_lo, 2 * j, KD, False)
                down(s0 + 4, 0, HIGH, True)
                down(s0 + 6, 2, LOW, False)
            down(S_DOWN7, 0, HIGH, True)
            chunk_and_turn(S_DOWN7 + 2, r1_hi, r1_lo, 4)

            chunk_from_turns(S_PG, True)
            project(S_PG + 4, LOW, xt_hi, xt_lo, KD, True)

        @block.scalar
        def _(act):
            fill = [Mark(s_fill[b]) for b in range(8)]
            ahi = Mark(s_ahi)
            steps = Mark(s_act)

            def ahead(s, slot):
                s3, n = s + 3, (slot + 3) % RING
                turn_of = s3 // RING + 1 if isinstance(s3, int) else None
                act.wait_ge(s_slab[n], 16 * turn_of)
                if not (isinstance(s, int) and s < 1):
                    act.wait_ge(s_used, s)
                act.activation(w_hi[:, n, :], raw[:, n, :], ACT.Copy).then_inc(s_hi, 1)

            def ahead_in(base, i, per, j, slot):
                n = (slot + 3) % RING
                q = (base + j + 3) // RING + 1
                act.wait_ge(s_slab[n], (i * (per // RING) + q) * 16)
                act.wait_ge(s_used, i * per + (base + j))
                act.activation(w_hi[:, n, :], raw[:, n, :], ACT.Copy).then_inc(s_hi, 1)

            def filled(b):
                act.wait_ge(s_fill[b], fill[b].up())

            def skip(b):
                fill[b].up()

            def hi(dst, src, scale=1.0):
                ahi.up()
                return act.activation(dst, src, ACT.Copy, scale=scale).then_inc(s_ahi, 1)

            def drained(b, ins):
                ins.then_inc(s_drain[b], 1)

            act.dma_start(tab[:, :], tables).then_inc(s_tab, 16)
            act.dma_start(gains[:, 0:24], norms).then_inc(s_tab, 16)
            act.dma_start(qg, q_gain.partition_broadcast(P)).then_inc(s_tab, 16)
            act.dma_start(kg, k_gain.partition_broadcast(P)).then_inc(s_tab, 16)
            act.dma_start(rg_g, ret_gain.partition_broadcast(P)).then_inc(s_tab, 16)
            act.dma_start(dec, decay.partition_broadcast(P)).then_inc(s_tab, 16)

            act.wait_ge(s_slab[0], 16)
            act.activation(w_hi[:, 0, :], raw[:, 0, :], ACT.Copy).then_inc(s_hi, 1)
            for k, b in ((0, 4), (1, 5)):
                filled(b)
                hi(pt_hi[:, k, :], ps[b][:, :])
            for t in range(NT):
                act.wait_ge(s_x[t], 16)
                if t:
                    act.wait_ge(s_ss, t)
                act.activation(squares, x0[:, t, :], ACT.Square, accum_out=ss[:, t:t + 1]).then_inc(s_ss, 1)
            act.wait_ge(s_dexp, 1)
            act.activation(lt[:, 1, :], lt[:, 0, :], ACT.Exp).then_inc(s_du, 1)
            for n in (1, 2):
                act.wait_ge(s_slab[n], 16)
                act.activation(w_hi[:, n, :], raw[:, n, :], ACT.Copy).then_inc(s_hi, 1)
            ahead(0, 0)
            for t in range(NT):
                filled(t)
                if t % 2 == 0:
                    drained(t, act.copy(ple_w[:, t, 0:C], ps[t][:, :]))
            act.wait_ge(s_tab, 16 * 6)
            for k in range(KD):
                filled(HIGH[k % 4])
                hi(r1_hi[:, k, :], ps[HIGH[k % 4]][:, :], scale=mix_g[:, k:k + 1])
            for j in range(4):
                ahead(S_AQ + j, (S_AQ + j) % RING)
            for t in range(NT):
                filled(t)
                if t % 2 == 0:
                    drained(t, act.copy(q_raw[:, t, :], ps[t][:, :]))
            for j in range(2):
                ahead(S_AKV + j, (S_AKV + j) % RING)
            for t in range(NT):
                b = HIGH[t]
                filled(b)
                act.copy(k_raw[:, t, :], ps[b][:, 0:P]).then_inc(s_act, 1)
                steps.up()
                hi(v_st[:, :, t, 0:HD], ps[b][:, P:2 * P].rearrange("p (g d) -> p g d", g=KV))
            ahead(S_PLE1, S_PLE1 % RING)
            for t in range(NT):
                filled(t)
                if t % 2 == 0:
                    drained(t, act.copy(ple_w[:, t, C:2 * C], ps[t][:, :]))
            for t in range(NT):
                act.wait_ge(s_drain[t], 3)
            act.dma_start(ple_spill, region(fp, RR + 4096, 4096)).then_inc(s_spill, 16)
            filled(5)
            hi(k_st[0:HD, 0, 0, :], ps[5][0:HD, :])
            hi(k_st[HD:P, 1, 0, :], ps[5][HD:P, :])
            act.copy(k_st[HD:P, 0, 0, :], ps[5][0:HD, :]).then_inc(s_act, 1)
            act.copy(k_st[0:HD, 1, 0, :], ps[5][HD:P, :]).then_inc(s_act, 1)
            steps.local += 2

            shift_m = Mark(s_shift)

            def soft():
                for qt in range(NT):
                    b = HIGH[qt]
                    filled(b)
                    act.wait_ge(s_shift, shift_m.up())
                    drained(b, act.activation(prob[:, qt, :], ps[b][:, :], ACT.Exp, bias=nb[:, qt:qt + 1],
                                              scale=HD ** -0.5, accum_out=den[:, qt:qt + 1]))

            def split_probs():
                for kt in range(NT):
                    filled(HIGH[kt])
                    hi(prt_hi[:, kt, :], ps[HIGH[kt]][:, :])

            def low_half():
                filled(7)
                act.copy(otmp[0:HD, :], ps[7][HD:P, :]).then_inc(s_otmp, 1)

            def drain_ret(c):
                for t in range(NT):
                    filled(t)
                    if t % 2 == 0:
                        drained(t, act.copy(ret[:, bass.ds(c, 1), t, :].rearrange("p a n -> p (a n)"), ps[t][:, :]))

            at_marks = {fill[0]: 1, fill[1]: 1, fill[2]: 1, fill[3]: 1, fill[4]: 5, fill[5]: 4, fill[6]: 4,
                        fill[7]: 6, ahi: 10, shift_m: 8}
            act.wait_ge(s_spill, 16)
            for g in range(KV):
                with counted(act, 2, at_marks) as i:
                    base = S_RET + 8 * g
                    filled(4)
                    hi(q_st[0:HD, 0, :], ps[4][0:HD, :])
                    hi(q_st[HD:P, 1, :], ps[4][HD:P, :])
                    ahead_in(base, i, 4, 0, 0)
                    soft()
                    ahead_in(base, i, 4, 1, 1)
                    split_probs()
                    low_half()
                    ahead_in(base, i, 4, 2, 2)
                    soft()
                    ahead_in(base, i, 4, 3, 3)
                    split_probs()
                    drain_ret(2 * g + i)
                    low_half()

            act.dma_start(delta, delta_in).then_inc(s_dlt, 16)
            mexp_m = Mark(s_mexp)
            re_marks = {fill[0]: 1, fill[1]: 1, fill[2]: 1, fill[3]: 1, fill[4]: 2, fill[5]: 2, fill[6]: 2,
                        fill[7]: 2, ahi: 7, mexp_m: 1}
            with counted(act, RH, re_marks) as u:
                ahead_in(S_GATE, u, 4, 0, 0)
                hi(rv_st[:, :, 0:P], ret[:, 2, :, bass.ds(u * P, P)])
                act.wait_ge(s_mexp, mexp_m.up())
                act.activation(mask, mask, ACT.Exp).then_inc(s_mask, 1)
                ahead_in(S_GATE, u, 4, 1, 1)
                for b, dst in ((4, rq_t), (5, rk_t)):
                    filled(b)
                    hi(dst[:, 0, :], ps[b][:, :])
                ahead_in(S_GATE, u, 4, 2, 2)
                for jt, b in enumerate((6, 7, 4, 5)):
                    skip(b)
                    act.wait_ge(s_drain[b], fill[b].value)
                    hi(prt_hi[:, jt, :], sc_f[:, jt % 2, :])
                ahead_in(S_GATE, u, 4, 3, 3)
                for b in (6, 7):
                    filled(b)
                    act.copy(otmp[:, (b - 6) * 256:(b - 5) * 256].rearrange("p (e n) -> p e n", e=2),
                             ps[b][:, :].rearrange("p (e s n) -> p e s n", e=2, s=2)[:, :, 1, :]).then_inc(s_otmp, 1)
                for m in LOW:
                    filled(m)
                    drained(m, act.copy(gate[:, bass.ds(u * 4 + m, 1), :].rearrange("p a n -> p (a n)"),
                                        ps[m][:, :]))

            for k in range(4):
                hi(at_hi[:, k, :], ot[:, k, :])
            for t in range(NT):
                act.activation(ret[:, 1, t, :], ret[:, 3, t, :], ACT.Sigmoid).then_inc(s_rgs, 1)
            for b in LOW:
                act.wait_ge(s_drain[b], fill[b].value)
            for j in range(2):
                ahead(S_AO + j, (S_AO + j) % RING)
                for m in range(4 * j, 4 * j + 4):
                    act.activation(gate[:, m, :], gate[:, m, :], ACT.Sigmoid).then_inc(s_gs, 1)
            for b in LOW:
                skip(b)
            for k in range(4):
                filled(HIGH[k])
                hi(ry_hi[:, k, :], ps[HIGH[k]][:, :])
            act.wait_ge(s_rgs, NT)
            act.wait_ge(s_ry, NT)
            act.dma_start(xs, x_in.rearrange("(t p) n -> p t n", p=P)).then_inc(s_xr, 16)
            for j in range(2):
                ahead(S_AO + 2 + j, (S_AO + 2 + j) % RING)
            for m in range(8, 16):
                act.activation(gate[:, m, :], gate[:, m, :], ACT.Sigmoid).then_inc(s_gs, 1)
            for b in LOW:
                skip(b)
            for j in range(4):
                ahead(S_RO + j, (S_RO + j) % RING)
                for m in ((0, 1, 2, 3) if j == 1 else (4, 5, 6, 7) if j == 3 else ()):
                    skip(HIGH[m] if j == 1 else LOW[m - 4])
                    act.wait_ge(s_mg, m + 1)
                    hi(r1_hi[:, m, :], merged[:, m, :])
            for b in HIGH:
                skip(b)
            for j in range(4):
                ahead(S_OUT + j, (S_OUT + j) % RING)
            act.wait_ge(s_mgs, 8)
            act.dma_start(region(fp, RR, 4096), ple_spill).then_inc(s_pler, 16)
            def split_turned(k0, banks, gain):
                for n, b in enumerate(banks):
                    filled(b)
                    hi(xt_hi[:, k0 + n, :], ps[b][:, :], scale=gain[:, k0 + n:k0 + n + 1])

            def row_squares(first_sum):
                for t in range(NT):
                    if t or first_sum:
                        act.wait_ge(s_ss, first_sum + t)
                    act.activation(squares2, xs[:, t, :], ACT.Square, accum_out=ss[:, t:t + 1]).then_inc(s_ss, 1)

            for j in range(4):
                if j == 3:
                    split_turned(0, HIGH, mlp_g)
                ahead(S_OUT + 4 + j, j)
            for b in LOW:
                skip(b)
            for j in range(4):
                ahead(S_UP0 + j, (S_UP0 + j) % RING)
                if j == 1:
                    split_turned(4, LOW, mlp_g)
                if j == 2:
                    row_squares(NT)

            def relus(banks):
                for m, b in enumerate(banks):
                    filled(b)
                    drained(b, act.activation(stage[:, m, :], ps[b][:, :], ACT.Relu))

            hid_m = Mark(s_hid)

            def split_hidden():
                for m in range(4):
                    act.wait_ge(s_hid, hid_m.up())
                    hi(r1_hi[:, m, :], stage[:, m, :])

            relus(HIGH)
            mlp_marks = {fill[b]: 2 for b in LOW}
            mlp_marks.update({fill[b]: 1 for b in HIGH})
            mlp_marks.update({ahi: 4, hid_m: 4})
            with counted(act, NF - 1, mlp_marks) as f:
                ahead_in(S_MLP, f, 8, 0, 0)
                split_hidden()
                for j in range(1, 4):
                    ahead_in(S_MLP, f, 8, j, j)
                act.wait_ge(s_hids, f * 4 + 4)
                relus(LOW)
                for j in range(4, 8):
                    ahead_in(S_MLP, f, 8, j, j % RING)
                for b in HIGH + LOW:
                    filled(b)
            split_hidden()
            act.dma_start(fin_g, fin_gain.partition_broadcast(P)).then_inc(s_fin, 16)
            for j in range(4):
                if j == 3:
                    for b in HIGH:
                        skip(b)
                    split_turned(0, HIGH, ple_g)
                ahead(S_DOWN7 + j, j)
            for b in LOW:
                skip(b)
            for j in range(4):
                ahead(S_PG + j, j)
                if j == 1:
                    split_turned(4, LOW, ple_g)
                if j == 2:
                    row_squares(2 * NT)
            ahead(S_PG + 4, 0)
            act.wait_ge(s_rs, 1)
            for c, banks in ((0, HIGH), (1, LOW)):
                for t in range(NT):
                    filled(banks[t])
                    drained(banks[t], act.activation(sig[:, c, t, :], ps[banks[t]][:, :], ACT.Sigmoid,
                                                     scale=rstd[:, t:t + 1]))
            for t in range(NT):
                act.wait_ge(s_xf, t + 1)
                act.wait_ge(s_ss, 3 * NT + t)
                act.activation(squares2, xs[:, t, :], ACT.Square, accum_out=ss[:, t:t + 1]).then_inc(s_ss, 1)
            for t in range(NT):
                act.wait_ge(s_fo, t + 1)
                act.dma_start(out[t * P:(t + 1) * P, :], out_sb[:, t, :]).then_inc(s_out, 16)
            act.wait_ge(s_out, 16 * NT)

        @block.vector
        def _(dve):
            fill = [Mark(s_fill[b]) for b in range(8)]
            ahi = Mark(s_ahi)
            steps = Mark(s_dve)
            roped = Mark(s_rope)

            def filled(b):
                dve.wait_ge(s_fill[b], fill[b].up())

            def skip(b):
                fill[b].up()

            def step(ins):
                ins.then_inc(s_dve, 1)
                steps.up()

            def settle():
                dve.wait_ge(s_dve, steps.value)

            def carry_waits():
                step(dve.memset(small[:, 152:153], 0.0))

            def lo(dst, src, hi_part):
                dve.wait_ge(s_ahi, ahi.up())
                return dve.tensor_tensor(dst, src, f32(hi_part), ALU.subtract)

            def rsqrt(dst, src):
                n = dst.shape[-1]
                t = nwt[:, 0:n]
                step(dve.tensor_scalar(dst.bitcast(I32), src.bitcast(I32), -0.5, 1597463007.0, ALU.mult, ALU.add))
                settle()
                for _ in range(4):
                    step(dve.tensor_tensor(t, dst, dst, ALU.mult))
                    settle()
                    step(dve.scalar_tensor_tensor(t, t, -0.5, src, ALU.mult, ALU.mult))
                    settle()
                    step(dve.scalar_tensor_tensor(dst, t, 1.5, dst, ALU.add, ALU.mult))
                    settle()

            def rope(o1, o2, x1, x2, cos, sin, shape):
                n = 1
                for v in shape[1:]:
                    n *= v
                def buf(k):
                    v = rope_tmp[:, k * n:(k + 1) * n]
                    if len(shape) == 4:
                        return v.rearrange("p (t h d) -> p t h d", t=shape[1], h=shape[2])
                    return v.rearrange("p (t d) -> p t d", t=shape[1])
                a, b = buf(0), buf(1)
                step(dve.tensor_tensor(a, x1, sin, ALU.mult))
                step(dve.tensor_tensor(b, x2, sin, ALU.mult))
                step(dve.tensor_tensor(o1, x1, cos, ALU.mult))
                step(dve.tensor_tensor(o2, x2, cos, ALU.mult))
                settle()
                step(dve.tensor_tensor(o1, o1, b, ALU.subtract))
                return dve.tensor_tensor(o2, o2, a, ALU.add)

            def heads_ready(dst, v, gain):
                dv = dst.rearrange("p t (h d) -> p t h d", h=2)
                hv = v.rearrange("p t (h d) -> p t h d", h=2)
                step(dve.tensor_tensor(q_sq, v, v, ALU.mult))
                settle()
                step(dve.tensor_reduce(hss, q_sq.rearrange("p t (h d) -> p (t h) d", h=2), AX.X, ALU.add))
                settle()
                step(dve.tensor_scalar(hss, hss, 1.0 / HD, NORM_EPS, ALU.mult, ALU.add))
                settle()
                rsqrt(hr, hss)
                r = hr.rearrange("p (t h) -> p t h", h=2).unsqueeze(3).to_broadcast([P, NT, 2, HD])
                step(dve.tensor_tensor(hv, hv, r, ALU.mult))
                settle()
                g = gain.unsqueeze(1).unsqueeze(1).to_broadcast([P, NT, 2, HD])
                step(dve.tensor_tensor(hv, hv, g, ALU.mult))
                settle()
                half = HD // 2
                c = cos_a.unsqueeze(2).to_broadcast([P, NT, 2, half])
                s = sin_a.unsqueeze(2).to_broadcast([P, NT, 2, half])
                rope(dv[:, :, :, 0:half], dv[:, :, :, half:HD], hv[:, :, :, 0:half], hv[:, :, :, half:HD], c, s, [P, NT, 2, half]).then_inc(s_rope, 1)
                dve.wait_ge(s_rope, roped.up())

            dve.wait_ge(s_tab, 16 * 6)
            step(dve.tensor_scalar(lt[:, 2, :], dec, -1.0, None, ALU.mult))
            settle()
            dve.tensor_tensor(lt[:, 0, :], dec, lt[:, 2, :], ALU.min).then_inc(s_dexp, 1)

            for k, b in ((0, 4), (1, 5)):
                filled(b)
                lo(pt_lo[:, k, :], ps[b][:, :], pt_hi[:, k, :]).then_inc(s_drain[b], 1)
            dve.wait_ge(s_ss, NT)
            step(dve.tensor_scalar(inv_ms, ss, 1.0 / D, NORM_EPS, ALU.mult, ALU.add))
            settle()
            rsqrt(rstd, inv_ms)
            for t in range(NT):
                dve.tensor_scalar(x0[:, t, :], x0[:, t, :], rstd[:, t:t + 1], None, ALU.mult).then_inc(s_xn, 1)
            for t in range(NT):
                filled(t)
                if t % 2:
                    dve.tensor_copy(ple_w[:, t, 0:C], ps[t][:, :]).then_inc(s_drain[t], 1)
            def split_turned(dst_lo, dst_hi, k0, banks, gain):
                for n, b in enumerate(banks):
                    filled(b)
                    dve.wait_ge(s_ahi, ahi.up())
                    dve.scalar_tensor_tensor(dst_lo[:, k0 + n, :], ps[b][:, :], gain[:, k0 + n:k0 + n + 1],
                                             f32(dst_hi[:, k0 + n, :]), ALU.mult, ALU.subtract)\
                       .then_inc(s_drain[b], 1)
            split_turned(r1_lo, r1_hi, 0, HIGH, mix_g)
            split_turned(r1_lo, r1_hi, 4, HIGH, mix_g)

            dve.wait_ge(s_du, 1)
            u_, w_, s_, q_ = lt[:, 1, :], lt[:, 2, :], lt[:, 3, :], lt[:, 4, :]
            step(dve.tensor_scalar(w_, u_, 2.0, None, ALU.add))
            settle()
            step(dve.reciprocal(w_, w_))
            settle()
            step(dve.tensor_tensor(s_, u_, w_, ALU.mult))
            settle()
            step(dve.tensor_tensor(w_, s_, s_, ALU.mult))
            settle()
            step(dve.tensor_scalar(q_, w_, 1.0 / 17, None, ALU.mult))
            settle()
            for n in (15, 13, 11, 9, 7, 5, 3):
                step(dve.scalar_tensor_tensor(q_, q_, 1.0 / n, w_, ALU.add, ALU.mult))
                settle()
            step(dve.scalar_tensor_tensor(q_, q_, 1.0, s_, ALU.add, ALU.mult))
            step(dve.tensor_scalar(w_, dec, 0.0, None, ALU.min))
            settle()
            step(dve.scalar_tensor_tensor(lg, q_, -2.0, w_, ALU.mult, ALU.add))
            settle()
            step(dve.tensor_scalar(lg[:, RH:2 * RH], lg[:, RH:2 * RH], -1.0, None, ALU.mult))

            for t in range(NT):
                filled(t)
                if t % 2:
                    dve.tensor_copy(q_raw[:, t, :], ps[t][:, :]).then_inc(s_drain[t], 1)
            for t in range(NT):
                dve.wait_ge(s_drain[t], 2)
            heads_ready(q_rot, q_raw[:, :, 0:P], qg)
            a_steps = 0
            for t in range(NT):
                b = HIGH[t]
                filled(b)
                a_steps += 1
                dve.wait_ge(s_act, a_steps)
                lo(v_st[:, :, t, HD:P], ps[b][:, P:2 * P].rearrange("p (g d) -> p g d", g=KV), v_st[:, :, t, 0:HD])\
                    .then_inc(s_drain[b], 1)
            for t in range(NT):
                filled(t)
                if t % 2:
                    dve.tensor_copy(ple_w[:, t, C:2 * C], ps[t][:, :]).then_inc(s_drain[t], 1)
            heads_ready(k_rot, k_raw, kg)
            filled(5)
            dve.wait_ge(s_act, a_steps + 2)
            for g, rows, other in ((0, slice(0, HD), slice(HD, P)), (1, slice(HD, P), slice(0, HD))):
                dve.wait_ge(s_ahi, ahi.up())
                step(dve.tensor_tensor(k_st[rows, g, 1, :], ps[5][rows, :], f32(k_st[rows, g, 0, :]), ALU.subtract))
                ins = dve.tensor_tensor(k_st[other, g, 1, :], ps[5][rows, :], f32(k_st[rows, g, 0, :]), ALU.subtract)
                if g == 0:
                    step(ins)
            ins.then_inc(s_drain[5], 1)

            otmp_m = Mark(s_otmp)

            def soft():
                n0 = []
                for qt in range(NT):
                    b = HIGH[qt]
                    filled(b)
                    step(dve.tensor_reduce(mx[:, qt:qt + 1], ps[b][:, :], AX.X, ALU.max))
                    settle()
                    dve.tensor_scalar(nb[:, qt:qt + 1], mx[:, qt:qt + 1], -(HD ** -0.5), None, ALU.mult)\
                       .then_inc(s_shift, 1)
                    n0.append(fill[b].value)
                for qt in range(NT):
                    dve.wait_ge(s_drain[HIGH[qt]], n0[qt])
                    step(dve.reciprocal(rden[:, qt:qt + 1], den[:, qt:qt + 1]))
                    settle()
                    dve.tensor_scalar(prob[:, qt, :], prob[:, qt, :], rden[:, qt:qt + 1], None, ALU.mult)\
                       .then_inc(s_prob, 1)

            def split_probs():
                for kt in range(NT):
                    b = HIGH[kt]
                    filled(b)
                    lo(prt_lo[:, kt, :], ps[b][:, :], prt_hi[:, kt, :]).then_inc(s_drain[b], 1)

            def join(pair, rows):
                filled(7)
                dve.wait_ge(s_otmp, otmp_m.up())
                dve.tensor_tensor(ot[rows, bass.ds(pair, 1), :].rearrange("p a n -> p (a n)"),
                                  ps[7][0:HD, :], otmp[0:HD, :], ALU.add).then_inc(s_drain[7], 1)

            def drain_ret(c):
                for t in range(NT):
                    filled(t)
                    if t % 2:
                        dve.tensor_copy(ret[:, bass.ds(c, 1), t, :].rearrange("p a n -> p (a n)"), ps[t][:, :])\
                           .then_inc(s_drain[t], 1)

            def attention(g, pair, last):
                filled(4)
                dve.wait_ge(s_ahi, ahi.up())
                step(dve.tensor_tensor(q_st[HD:P, 0, :], ps[4][0:HD, :], f32(q_st[0:HD, 0, :]), ALU.subtract))
                dve.wait_ge(s_ahi, ahi.up())
                settle()
                dve.tensor_tensor(q_st[0:HD, 1, :], ps[4][HD:P, :], f32(q_st[HD:P, 1, :]), ALU.subtract)\
                   .then_inc(s_drain[4], 1)
                soft()
                split_probs()
                join(pair, slice(0, HD))
                soft()
                split_probs()
                drain_ret(pair)
                join(pair, slice(HD, P))
                if not last:
                    dve.wait_ge(s_drain[7], fill[7].value)
                    heads_ready(q_rot, q_raw[:, :, bass.ds((pair + 1) * P, P)], qg)

            HEADS_STEPS = 3 + 13 + 2 + 5
            at_marks = {fill[0]: 1, fill[1]: 1, fill[2]: 1, fill[3]: 1, fill[4]: 5, fill[5]: 4, fill[6]: 4,
                        fill[7]: 6, ahi: 10, otmp_m: 2, roped: 1, steps: 1 + 16 + HEADS_STEPS}
            with counted(dve, 2, at_marks) as i:
                attention(0, i, False)
            attention(1, 2, False)
            attention(1, 3, True)

            for b in LOW:
                dve.wait_ge(s_drain[b], fill[b].value)
            dve.wait_ge(s_drain[7], fill[7].value)
            dve.wait_ge(s_dlt, 16)
            mask_m = Mark(s_mask)
            re_marks = {fill[0]: 1, fill[1]: 1, fill[2]: 1, fill[3]: 1, fill[4]: 2, fill[5]: 2, fill[6]: 2,
                        fill[7]: 2, ahi: 7, otmp_m: 2, mask_m: 1, roped: 2,
                        steps: 2 + 10 + 4 + 4 + 2 + 1 + 13 + 4 + 2}
            with counted(dve, RH, re_marks) as u:
                hc = bass.ds(u * P, P)
                half = RHD // 2
                step(dve.tensor_scalar(mask, delta, 0.0, lg[:, bass.ds(u, 1)], ALU.max, ALU.mult))
                step(dve.tensor_scalar(region(fp, PP, DELTA), delta, 0.0, lg[:, bass.ds(u + RH, 1)], ALU.min, ALU.mult))
                settle()
                dve.tensor_tensor(mask, mask, region(fp, PP, DELTA), ALU.add).then_inc(s_mexp, 1)
                dve.wait_ge(s_mexp, u + 1)
                for c in (0, 1):
                    v = ret[:, c, :, :]
                    ins = rope(r_rot[:, c, :, 0:half], r_rot[:, c, :, half:RHD], v[:, :, bass.ds(u * P, half)], v[:, :, bass.ds(u * P + half, half)], cos_r, sin_r,
                               [P, NT, half])
                    ins.then_inc(s_rope, 1)
                    dve.wait_ge(s_rope, roped.up())
                lo(rv_st[:, :, P:2 * P], ret[:, 2, :, hc], rv_st[:, :, 0:P]).then_inc(s_vst, 1)
                for b, dst in ((4, rq_t), (5, rk_t)):
                    filled(b)
                    lo(dst[:, 1, :], ps[b][:, :], dst[:, 0, :]).then_inc(s_drain[b], 1)
                dve.wait_ge(s_mask, mask_m.up())
                def finish(jt):
                    lo(prt_lo[:, jt, :], sc_f[:, jt % 2, :], prt_hi[:, jt, :]).then_inc(s_sct, 1)
                for jt, b in enumerate((6, 7, 4, 5)):
                    filled(b)
                    if jt >= 2:
                        dve.wait_ge(s_sct, u * 4 + jt - 1)
                    dve.scalar_tensor_tensor(sc_f[:, jt % 2, :], ps[b][:, :], RHD ** -0.5,
                                             mask[:, (NT - 1 - jt) * P:(NT - 1 - jt) * P + C], ALU.mult, ALU.mult)\
                       .then_inc(s_drain[b], 1)
                    if jt >= 1:
                        finish(jt - 1)
                finish(3)
                for b in (6, 7):
                    filled(b)
                    dve.wait_ge(s_otmp, otmp_m.up())
                    dve.tensor_tensor(ret[:, 0, 2 * (b - 6):2 * (b - 6) + 2, hc],
                                      ps[b][:, :].rearrange("p (e s n) -> p e s n", e=2, s=2)[:, :, 0, :],
                                      otmp[:, (b - 6) * 256:(b - 5) * 256].rearrange("p (e n) -> p e n", e=2),
                                      ALU.add).then_inc(s_drain[b], 1)
                for b in (6, 7):
                    dve.wait_ge(s_drain[b], fill[b].value)
                carry_waits()
                for t in range(NT):
                    step(dve.bn_stats(bst[:, t, :], ret[:, 0, t, hc]))
                settle()
                carry_waits()
                for t in range(NT):
                    step(dve.bn_aggr(mv[:, t, :], bst[:, t, :]))
                settle()
                step(dve.tensor_scalar(rvar, mv[:, :, 1], GN_EPS, None, ALU.add))
                settle()
                rsqrt(rstd, rvar)
                for t in range(NT):
                    step(dve.tensor_scalar(ret[:, 0, t, hc], ret[:, 0, t, hc], mv[:, t, 0:1], rstd[:, t:t + 1],
                                           ALU.subtract, ALU.mult))
                settle()
                gb = rg_g[:, hc].unsqueeze(1).to_broadcast([P, NT, RHD])
                step(dve.tensor_tensor(ret[:, 0, :, hc], ret[:, 0, :, hc], gb, ALU.mult))
                settle()
                step(dve.tensor_tensor(ret[:, 0, :, hc], ret[:, 0, :, hc], ret[:, 3, :, hc], ALU.mult))
                for m in LOW:
                    skip(m)

            settle()
            for k in range(4):
                lo(at_lo[:, k, :], ot[:, k, :], at_hi[:, k, :]).then_inc(s_osp, 1)
            for t in range(NT):
                dve.wait_ge(s_rgs, t + 1)
                dve.tensor_tensor(ret[:, 0, t, :], ret[:, 0, t, :], ret[:, 1, t, :], ALU.mult).then_inc(s_ry, 1)
            def attn_branch(ms):
                for m in ms:
                    b = LOW[m % 4]
                    filled(b)
                    dve.wait_ge(s_gs, m + 1)
                    dve.tensor_tensor(gate[:, m, :], ps[b][:, :], gate[:, m, :], ALU.mult).then_inc(s_drain[b], 1)

            attn_branch(range(4))
            for k in range(4):
                filled(HIGH[k])
                lo(ry_lo[:, k, :], ps[HIGH[k]][:, :], ry_hi[:, k, :]).then_inc(s_drain[HIGH[k]], 1)
            attn_branch(range(4, 8))
            for b in LOW:
                dve.wait_ge(s_drain[b], fill[b].value)

            def merge(m, b):
                filled(b)
                dve.wait_ge(s_gs, 8 + m + 1)
                dve.tensor_tensor(gate[:, 8 + m, :], ps[b][:, :], gate[:, 8 + m, :], ALU.mult)\
                   .then_inc(s_drain[b], 1)
                dve.wait_ge(s_drain[b], fill[b].value)
                dve.tensor_tensor(merged[:, m, :], gate[:, m, :], gate[:, 8 + m, :], ALU.add).then_inc(s_mg, 1)

            def merge_lo(m):
                lo(r1_lo[:, m, :], merged[:, m, :], r1_hi[:, m, :]).then_inc(s_mgs, 1)
            for m in range(8):
                merge(m, m % 4 + (4 if m < 4 else 0))
                if m:
                    merge_lo(m - 1)
            merge_lo(7)

            def add_columns(c, banks):
                for t in range(NT):
                    b = banks[t]
                    filled(b)
                    xc = xs[:, t, c * C:(c + 1) * C]
                    dve.tensor_tensor(xc, xc, ps[b][:, :], ALU.add).then_inc(s_drain[b], 1)

            dve.wait_ge(s_xr, 16)
            add_columns(0, HIGH)
            split_turned(xt_lo, xt_hi, 0, HIGH, mlp_g)
            add_columns(1, LOW)
            split_turned(xt_lo, xt_hi, 4, LOW, mlp_g)
            dve.wait_ge(s_ss, 2 * NT)
            step(dve.tensor_scalar(inv_ms, ss, 1.0 / D, NORM_EPS, ALU.mult, ALU.add))
            settle()
            step(dve.reciprocal(inv_ms, inv_ms))
            settle()

            def square(banks):
                for m, b in enumerate(banks):
                    skip(b)
                    dve.wait_ge(s_drain[b], fill[b].value)
                    dve.tensor_tensor(stage[:, m, :], stage[:, m, :], stage[:, m, :], ALU.mult).then_inc(s_hid, 1)

            def split_hidden():
                for m in range(4):
                    lo(r1_lo[:, m, :], stage[:, m, :], r1_hi[:, m, :]).then_inc(s_hids, 1)

            def add_scaled(c, banks):
                for t in range(NT):
                    b = banks[t]
                    filled(b)
                    xc = xs[:, t, c * C:(c + 1) * C]
                    dve.scalar_tensor_tensor(xc, ps[b][:, :], inv_ms[:, t:t + 1], xc, ALU.mult, ALU.add)\
                       .then_inc(s_drain[b], 1)

            square(HIGH)
            mlp_marks = {fill[b]: 2 for b in LOW}
            mlp_marks.update({fill[b]: 1 for b in HIGH})
            mlp_marks.update({ahi: 4})
            with counted(dve, NF - 1, mlp_marks) as f:
                split_hidden()
                square(LOW)
                add_scaled(0, HIGH)
                add_scaled(1, LOW)
            split_hidden()
            add_scaled(0, HIGH)
            split_turned(xt_lo, xt_hi, 0, HIGH, ple_g)
            add_scaled(1, LOW)
            split_turned(xt_lo, xt_hi, 4, LOW, ple_g)
            dve.wait_ge(s_ss, 3 * NT)
            step(dve.tensor_scalar(inv_ms, ss, 1.0 / D, NORM_EPS, ALU.mult, ALU.add))
            settle()
            rsqrt(rstd, inv_ms)
            dve.nop().then_inc(s_rs, 1)
            dve.wait_ge(s_pler, 16)
            for c, banks in ((0, HIGH), (1, LOW)):
                for t in range(NT):
                    b = banks[t]
                    skip(b)
                    dve.wait_ge(s_drain[b], fill[b].value)
                    xc = xs[:, t, c * C:(c + 1) * C]
                    sg = sig[:, c, t, :]
                    step(dve.tensor_tensor(sg, sg, ple_r[:, t, c * C:(c + 1) * C], ALU.mult))
                    settle()
                    ins = dve.tensor_tensor(xc, xc, sg, ALU.add)
                    if c:
                        ins.then_inc(s_xf, 1)
                    else:
                        step(ins)
            dve.wait_ge(s_fin, 16)
            dve.wait_ge(s_ss, 4 * NT)
            step(dve.tensor_scalar(inv_ms, ss, 1.0 / D, NORM_EPS, ALU.mult, ALU.add))
            settle()
            rsqrt(rstd, inv_ms)
            for t in range(NT):
                dve.scalar_tensor_tensor(out_sb[:, t, :], xs[:, t, :], rstd[:, t:t + 1], fin_g, ALU.mult, ALU.mult)\
                   .then_inc(s_fo, 1)


def shape_tables():
    import numpy as np

    def rope(head_dim):
        n = head_dim // 4
        freqs = np.float32(10000.0) ** (-np.arange(n, dtype=np.float32) / np.float32(n))
        pos = np.arange(SEQ)
        row, col = (pos // 64).astype(np.float32), (pos % 64).astype(np.float32)
        ang = np.concatenate([row[:, None] * freqs, col[:, None] * freqs], axis=-1).astype(np.float32)
        tiles = lambda a: a.reshape(NT, P, -1).transpose(1, 0, 2).reshape(P, -1)
        return tiles(np.cos(ang)), tiles(np.sin(ang))

    tables = np.concatenate([np.eye(P, dtype=np.float32), *rope(HD), *rope(RHD)], axis=1).astype(np.float32)
    delta = (np.arange(DELTA)[None, :] - (NT - 1) * P - np.arange(P)[:, None]).astype(np.float32)
    return tables, delta


def slabs_of(w, width):
    per = SLAB // width
    k = w.shape[0] // P
    return w.reshape(k // per, per, P, width).transpose(0, 2, 1, 3).reshape(k // per, P, SLAB)


def pack(w_in, w_attn_o, w_ret_o, w_out, w_up, w_down, w_ple_gate, w_ple):
    import numpy as np

    a = NH * HD
    kv = 2 * KV * HD
    cols = lambda w, c: slabs_of(w[:, c:c + C], C)
    parts = [cols(w_ple, 0), cols(w_in, 0), slabs_of(w_in[:, a:a + kv], kv), cols(w_ple, C)]
    parts += [cols(w_in, a + kv + n * C) for n in range(8)]
    parts += [cols(w, n * C) for w in (w_attn_o, w_ret_o, w_out) for n in range(2)]
    parts += [cols(w_up, 0)]
    for f in range(NF):
        if f + 1 < NF:
            parts.append(cols(w_up, (f + 1) * C))
        parts += [cols(w_down[f * C:(f + 1) * C], n * C) for n in range(2)]
    parts += [cols(w_ple_gate, n * C) for n in range(2)]
    return np.concatenate(parts)


def kernel(**inputs):
    import numpy as np
    import concourse.bacc as bacc
    from concourse.bass_utils import run_bass_kernel_spmd

    a = {k: np.asarray(v) for k, v in inputs.items()}
    tables, delta = shape_tables()
    norms = np.concatenate([a[n][0].reshape(KD, P).T for n in ("mix_norm", "mlp_norm", "ple_norm")], axis=1)
    arrays = {
        "slabs": pack(*(a[n][0] for n in ("w_in", "w_attn_o", "w_ret_o", "w_out", "w_up", "w_down",
                                          "w_ple_gate", "w_ple"))),
        "x": a["x"][0], "p": a["p"][0, 0], "tables": tables, "delta": delta, "norms": norms,
        "q_gain": a["attn_q_norm"][0], "k_gain": a["attn_k_norm"][0], "ret_gain": a["ret_norm_gain"][0],
        "final_gain": a["final_norm"], "decay": a["ret_decay_logit"][0].reshape(-1),
    }
    arrays = {f"in_{k}": np.ascontiguousarray(v) for k, v in arrays.items()}
    nc = bacc.Bacc("TRN2", target_bir_lowering=False, num_devices=1)
    args = [nc.dram_tensor(k, v.shape, F32, kind="ExternalInput").ap() for k, v in arrays.items()]
    args.append(nc.dram_tensor("ple_spill", [P, 4096], F32).ap())
    args.append(nc.dram_tensor("out_x", [SEQ, D], F32, kind="ExternalOutput").ap())
    build(nc, *args)
    r = run_bass_kernel_spmd(nc, [arrays], core_ids=[0])
    return r.results[0]["out_x"].reshape(1, SEQ, D)
```

```python
from contextlib import ExitStack, contextmanager

import concourse.bass as bass
from concourse import mybir

ALU = mybir.AluOpType
ACT = mybir.ActivationFunctionType
AX = mybir.AxisListType
F32 = mybir.dt.float32
F32R = mybir.dt.float32r
I32 = mybir.dt.int32

P = 128
D = 1024
SEQ = 512
PLE = 256
FF = 4 * D
C = 512
NT = SEQ // P
KD = D // P
HD = 64
NH = 8
KV = 2
RHD = 128
RH = 4
NORM_EPS = 1e-6
GN_EPS = 1e-5
RING = 4
SLAB = 1024

S_PLE0 = 0
S_AKV = S_PLE0 + 1
S_AQ = S_AKV + 2
S_PLE1 = S_AQ + 4
S_RET = S_PLE1 + 1
S_GATE = S_RET + 16
S_AO = S_GATE + 16
S_RO = S_AO + 4
S_OUT = S_RO + 4
S_UP0 = S_OUT + 8
S_MLP = S_UP0 + 4
S_DOWN7 = S_MLP + 7 * 8
S_PG = S_DOWN7 + 4
SLABS = S_PG + 8
NF = FF // C

T_ID = 0
T_CA = T_ID + P
T_SA = T_CA + NT * HD // 2
T_CR = T_SA + NT * HD // 2
T_SR = T_CR + NT * RHD // 2
T_END = T_SR + NT * RHD // 2
DELTA = SEQ + (NT - 1) * P


class Mark:

    def __init__(self, sem):
        self.sem, self.base, self.local = sem, 0, 0

    @property
    def value(self):
        return self.base + self.local

    def up(self):
        self.local += 1
        return self.value


@contextmanager
def counted(engine, count, marks):
    start = {m: m.value for m in marks}
    with engine.Fori(0, count) as i:
        for m, per in marks.items():
            m.base, m.local = i * per + start[m], 0
        yield i
        for m, per in marks.items():
            assert m.local == per, (m.sem, m.local, per)
    for m, per in marks.items():
        m.base, m.local = start[m] + count * per, 0


def build(nc, slabs, x_in, p_in, tables, delta_in, norms, q_gain, k_gain, ret_gain, fin_gain,
          decay, ple_spill, out):
    ctx = ExitStack()
    with ctx:
        sem = lambda name: ctx.enter_context(nc.semaphore(name))
        sb = lambda n, w, dt=F32: ctx.enter_context(nc.sbuf_tensor(n, [P, w], dt))

        ops = sb("ops", 24576, F32R)
        fp = sb("fp", 4096 + 8192 + 8192 + 2048 + 2048 + 896)
        tab = sb("tab", T_END)
        gains = sb("gains", 24 + HD + HD + RH * RHD + 2 * RH)
        rope_tmp = sb("rope_tmp", 512)
        mtmp = sb("mtmp", P)[:, :]
        scale_t = sb("scale_t", C)[:, :]
        small = sb("small", 256)
        ps = [ctx.enter_context(nc.psum_tensor(f"bank{b}", [P, C], F32)) for b in range(8)]

        def region(t, a, n):
            return t[:, a:a + n]

        w_hi = region(ops, 0, 4096).rearrange("p (s n) -> p s n", s=RING)
        w_lo = region(ops, 4096, 4096).rearrange("p (s n) -> p s n", s=RING)
        R1, R2 = 8192, 16384
        r1_hi = region(ops, R1, 4096).rearrange("p (k n) -> p k n", n=C)
        r1_lo = region(ops, R1 + 4096, 4096).rearrange("p (k n) -> p k n", n=C)
        xt_hi = region(ops, R2, 4096).rearrange("p (k n) -> p k n", n=C)
        xt_lo = region(ops, R2 + 4096, 4096).rearrange("p (k n) -> p k n", n=C)
        pt_hi = region(ops, R2 + 4096, 1024).rearrange("p (k n) -> p k n", n=C)
        pt_lo = region(ops, R2 + 5120, 1024).rearrange("p (k n) -> p k n", n=C)
        q_st = region(ops, R2, 1024).rearrange("p (h n) -> p h n", h=2)
        k_st = region(ops, R2 + 1024, 2048).rearrange("p (g s n) -> p g s n", g=KV, s=2)
        v_st = region(ops, R2 + 3072, 1024).rearrange("p (g t n) -> p g t n", g=KV, t=NT)
        prt_hi = region(ops, R2 + 4096, 2048).rearrange("p (k n) -> p k n", n=C)
        prt_lo = region(ops, R2 + 6144, 2048).rearrange("p (k n) -> p k n", n=C)
        rq_t = region(ops, R2, 1024).rearrange("p (s n) -> p s n", s=2)
        rk_t = region(ops, R2 + 1024, 1024).rearrange("p (s n) -> p s n", s=2)
        rv_st = region(ops, R2 + 2048, 1024).rearrange("p (t n) -> p t n", t=NT)
        at_hi, at_lo = prt_hi, prt_lo
        ry_hi = region(ops, R2, 2048).rearrange("p (k n) -> p k n", n=C)
        ry_lo = region(ops, R2 + 2048, 2048).rearrange("p (k n) -> p k n", n=C)

        f32 = lambda ap: ap.bitcast(F32)

        raw = region(fp, 0, 4096).rearrange("p (s n) -> p s n", s=RING)
        RR, GG = 4096, 12288
        ret = region(fp, RR, 8192).rearrange("p (c t n) -> p c t n", c=4, t=NT)
        x0 = region(fp, RR, 4096).rearrange("p (t n) -> p t n", t=NT)
        ple_w = region(fp, RR + 4096, 4096).rearrange("p (t n) -> p t n", t=NT)
        merged = region(fp, RR, 4096).rearrange("p (m n) -> p m n", n=C)
        xs = region(fp, RR + 4096, 4096).rearrange("p (t n) -> p t n", t=NT)
        ple_r = region(fp, RR, 4096).rearrange("p (t n) -> p t n", t=NT)
        gate = region(fp, GG, 8192).rearrange("p (m n) -> p m n", n=C)
        q_raw = region(fp, GG, 2048).rearrange("p (t n) -> p t n", t=NT)
        k_raw = region(fp, GG + 2048, 512).rearrange("p (t n) -> p t n", t=NT)
        p_sb = region(fp, GG + 4096, 1024).rearrange("p (t n) -> p t n", t=NT)
        squares = region(fp, GG + 5120, 1024)
        otmp_a = squares[:, 0:C]
        q_sq = region(fp, GG + 6144, 512).rearrange("p (t n) -> p t n", t=NT)
        q_rot = region(fp, GG + 6656, 512).rearrange("p (t n) -> p t n", t=NT)
        k_rot = region(fp, GG + 7168, 512).rearrange("p (t n) -> p t n", t=NT)
        stage = region(fp, GG, 2048).rearrange("p (m n) -> p m n", n=C)
        fin_g = region(fp, GG + 2048, 1024)
        squares2 = region(fp, GG + 3072, 1024)
        out_sb = region(fp, 0, 4096).rearrange("p (t n) -> p t n", t=NT)
        sig = region(fp, GG + 4096, 4096).rearrange("p (c t n) -> p c t n", c=2, t=NT)
        PP = GG + 8192
        prob = region(fp, PP, 2048).rearrange("p (t n) -> p t n", t=NT)
        sc_f = region(fp, PP, 1024).rearrange("p (b n) -> p b n", b=2)
        r_rot = region(fp, PP, 1024).rearrange("p (c t n) -> p c t n", c=2, t=NT)
        delta = region(fp, PP + 1024, DELTA)
        ot = region(fp, PP + 2048, 2048).rearrange("p (k n) -> p k n", n=C)
        mask = region(fp, PP + 4096, DELTA)
        ident = tab[:, T_ID:T_ID + P]
        cos_a = tab[:, T_CA:T_SA].rearrange("p (t d) -> p t d", t=NT)
        sin_a = tab[:, T_SA:T_CR].rearrange("p (t d) -> p t d", t=NT)
        cos_r = tab[:, T_CR:T_SR].rearrange("p (t d) -> p t d", t=NT)
        sin_r = tab[:, T_SR:T_END].rearrange("p (t d) -> p t d", t=NT)
        mix_g, mlp_g, ple_g = gains[:, 0:8], gains[:, 8:16], gains[:, 16:24]
        qg = gains[:, 24:88]
        kg = gains[:, 88:152]
        rg_g = gains[:, 152:664]
        dec = gains[:, 664:672]
        ss = small[:, 0:4]
        rstd = small[:, 4:8]
        inv_ms = small[:, 8:12]
        hss = small[:, 12:20]
        hr = small[:, 20:28]
        nwt = small[:, 28:44]
        mx = small[:, 44:48]
        nb = small[:, 48:52]
        den = small[:, 52:56]
        rden = small[:, 56:60]
        lg = small[:, 60:68]
        lt = small[:, 68:116].rearrange("p (a n) -> p a n", n=8)
        bst = small[:, 116:140].rearrange("p (t n) -> p t n", t=NT)
        mv = small[:, 140:148].rearrange("p (t n) -> p t n", t=NT)
        rvar = small[:, 148:152]
        row_r = small[:, 153:157]
        ss2 = small[:, 157:165]
        otmp = rope_tmp[:, :]

        s_slab = [sem(f"slab_landed{n}") for n in range(RING)]
        s_hi = sem("slab_hi_made")
        s_lo = sem("slab_lo_made")
        s_used = sem("slab_used")
        s_fill = [sem(f"bank{b}_filled") for b in range(8)]
        s_drain = [sem(f"bank{b}_drained") for b in range(8)]
        s_ahi = sem("operand_hi_made")
        s_p = sem("p_landed")
        s_x = [sem(f"x_landed{t}") for t in range(NT)]
        s_tab = sem("tables_landed")
        s_dlt = sem("delta_landed")
        s_xr = sem("residual_landed")
        s_spill = sem("ple_spilled")
        s_pler = sem("ple_reloaded")
        s_fin = sem("final_gain_landed")
        s_out = sem("out_stored")
        s_ss = sem("squares_summed")
        s_rr = sem("row_rms_ready")
        s_gr = sem("gates_scaled")
        s_id = sem("identity_landed")
        s_rope = sem("roped")
        s_shift = sem("row_max_ready")
        s_prob = sem("probs_ready")
        s_otmp = sem("lo_half_copied")
        s_vst = sem("v_split")
        s_sct = sem("scores_split")
        s_mexp = sem("mask_exponent")
        s_mask = sem("mask_ready")
        s_dexp = sem("decay_exponent")
        s_du = sem("decay_exp_done")
        s_osp = sem("attention_out_split")
        s_rgs = sem("ret_gate_sigmoid")
        s_gs = sem("gate_sigmoid")
        s_ry = sem("ret_out_ready")
        s_mg = sem("merged_summed")
        s_mgs = sem("merged_split")
        s_xf = sem("x_final")
        s_hid = sem("hidden_squared")
        s_hids = sem("hidden_split")
        s_rs = sem("row_scale_ready")
        s_psig = sem("ple_gate_sigmoid")
        s_fo = sem("final_ready")
        s_dve = sem("dve_steps")
        s_act = sem("act_steps")

        LOW = [0, 1, 2, 3]
        HIGH = [4, 5, 6, 7]

        block = ctx.enter_context(nc.Block())

        @block.sync
        def _(sp):
            sp.dma_start(p_sb, p_in.rearrange("(t p) n -> p t n", p=P)).then_inc(s_p, 16)
            sp.dma_start(raw[:, 0, :], slabs[0]).then_inc(s_slab[0], 16)
            for t in range(NT):
                sp.dma_start(x0[:, t, :], x_in[t * P:(t + 1) * P, :]).then_inc(s_x[t], 16)
            for n in range(1, RING):
                sp.dma_start(raw[:, n, :], slabs[n]).then_inc(s_slab[n], 16)
            with sp.Fori(1, SLABS // RING) as i:
                for n in range(RING):
                    sp.wait_ge(s_lo, (i - 1) * RING + n + 1)
                    sp.dma_start(raw[:, n, :], slabs[bass.ds(i * RING + n, 1)].rearrange("a p n -> (a p) n"))\
                      .then_inc(s_slab[n], 16)

        @block.gpsimd
        def _(pool):
            with pool.Fori(0, SLABS // RING) as i:
                for n in range(RING):
                    pool.wait_ge(s_hi, i * RING + n + 1)
                    pool.tensor_tensor(w_lo[:, n, :], raw[:, n, :], f32(w_hi[:, n, :]), ALU.subtract)\
                        .then_inc(s_lo, 1)

        @block.tensor
        def _(pe):
            fill = [Mark(s_fill[b]) for b in range(8)]

            def begin(b):
                n = fill[b].up()
                if not (isinstance(n, int) and n == 1):
                    pe.wait_ge(s_drain[b], n - 1)

            def slab_start(s):
                pe.wait_ge(s_lo, s + 1)
                return not (isinstance(s, int) and s == 0)

            def three(bank, a_hi, a_lo, b_hi, b_lo, first, last, used, done):
                m = pe.matmul(bank, a_hi, b_hi, start=first, stop=False)
                if used:
                    m.then_inc(s_used, 1)
                pe.matmul(bank, a_hi, b_lo, start=False, stop=False)
                m = pe.matmul(bank, a_lo, b_hi, start=False, stop=last)
                if done is not None:
                    m.then_inc(s_fill[done], 1)

            def tile(s, j, kk, banks, x_hi, x_lo, k, k_end, tokens, n=C):
                used = slab_start(s) if kk == 0 else False
                cols = slice(kk * n, (kk + 1) * n)
                first, last = k == 0, k == k_end - 1
                for m, b in enumerate(banks):
                    if first:
                        begin(b)
                    wc = slice(kk * n + m * P, kk * n + (m + 1) * P)
                    xc = slice(m * P, (m + 1) * P)
                    done = b if last else None
                    if tokens:
                        three(ps[b][:, 0:n], x_hi[:, k, xc], x_lo[:, k, xc], w_hi[:, j, cols], w_lo[:, j, cols],
                              first, last, used and m == 0, done)
                    else:
                        three(ps[b][:, :], w_hi[:, j, wc], w_lo[:, j, wc], x_hi[:, k, :], x_lo[:, k, :],
                              first, last, used and m == 0, done)

            def slab(s, j, banks, x_hi, x_lo, k0, k_end, tokens, n=C):
                for kk in range(SLAB // n):
                    tile(s, j, kk, banks, x_hi, x_lo, k0 + kk, k_end, tokens, n)

            def turn(b, src):
                begin(b)
                for n in range(4):
                    m = pe.transpose(ps[b][:, n * P:(n + 1) * P], src(n), ident)
                m.then_inc(s_fill[b], 1)

            def turn_x(src, k0, banks):
                for n, b in enumerate(banks):
                    turn(b, lambda t, k=k0 + n: src[:, t, k * P:(k + 1) * P])

            pe.wait_ge(s_id, 16)
            pe.wait_ge(s_p, 16)
            turn_x(p_sb, 0, [4, 5])
            for b in (4, 5):
                pe.wait_ge(s_drain[b], fill[b].value)
            slab(S_PLE0, 0, LOW, pt_hi, pt_lo, 0, 2, True)

            for t in range(NT):
                pe.wait_ge(s_x[t], 16)
            turn_x(x0, 0, HIGH)
            turn_x(x0, 4, HIGH)
            before = [fill[b].value - 1 for b in HIGH]
            for k in range(KD):
                b = HIGH[k % 4]
                pe.wait_ge(s_drain[b], before[k % 4] + (k >= 4))
                tile(S_AKV + k // 4, (S_AKV + k // 4) % RING, k % 4, LOW, r1_hi, r1_lo, k, KD, True, n=2 * KV * HD)
            for j in range(4):
                if j == 3:
                    begin(2)
                    for t in range(NT):
                        m = pe.matmul(ps[2][:, t * P:(t + 1) * P], row_r[:, t:t + 1].to_broadcast([P, P]), ident,
                                      start=True, stop=True)
                    m.then_inc(s_fill[2], 1)
                    pe.wait_ge(s_rope, 1)
                    turn(3, lambda t: k_rot[:, t, :])
                slab(S_AQ + j, (S_AQ + j) % RING, HIGH, r1_hi, r1_lo, 2 * j, KD, True)
            slab(S_PLE1, S_PLE1 % RING, LOW, pt_hi, pt_lo, 0, 2, True)

            prob_m = Mark(s_prob)

            def scores(e, g):
                for qt in range(NT):
                    b = HIGH[qt]
                    begin(b)
                    lhs = q_st[:, e, qt * P:(qt + 1) * P]
                    pe.matmul(ps[b][:, :], lhs, k_st[:, g, 0, :], start=True, stop=False)
                    pe.matmul(ps[b][:, :], lhs, k_st[:, g, 1, :], start=False, stop=True).then_inc(s_fill[b], 1)

            def turn_probs():
                for kt in range(NT):
                    b = HIGH[kt]
                    begin(b)
                    for qt in range(NT):
                        if kt == 0:
                            pe.wait_ge(s_prob, prob_m.up())
                        m = pe.transpose(ps[b][:, qt * P:(qt + 1) * P], prob[:, qt, kt * P:(kt + 1) * P], ident)
                    m.then_inc(s_fill[b], 1)

            def values(g):
                ready = [fill[HIGH[kt]].value for kt in range(NT)]
                begin(7)
                for kt in range(NT):
                    if kt < 3:
                        pe.wait_ge(s_drain[HIGH[kt]], ready[kt])
                    pe.matmul(ps[7][:, :], v_st[:, g, kt, :], prt_hi[:, kt, :], start=(kt == 0), stop=False)
                    m = pe.matmul(ps[7][:, :], v_st[:, g, kt, :], prt_lo[:, kt, :], start=False, stop=(kt == 3))
                m.then_inc(s_fill[7], 1)

            rope_m = Mark(s_rope)
            rope_m.local = 1

            def attention(s0, pair, g):
                def half(n):
                    j = n // 2
                    tile(s0 + j, j, n % 2, LOW, r1_hi, r1_lo, n, KD, True)
                pe.wait_ge(s_rope, rope_m.up())
                turn(4, lambda t: q_rot[:, t, :])
                q_ready = fill[4].value
                half(0)
                pe.wait_ge(s_drain[4], q_ready)
                scores(0, g)
                half(1)
                half(2)
                turn_probs()
                half(3)
                values(g)
                half(4)
                scores(1, g)
                half(5)
                half(6)
                turn_probs()
                half(7)
                values(g)

            at_marks = {fill[0]: 1, fill[1]: 1, fill[2]: 1, fill[3]: 1, fill[4]: 5, fill[5]: 4, fill[6]: 4,
                        fill[7]: 6, prob_m: 8, rope_m: 1}
            for g in range(KV):
                with counted(pe, 2, at_marks) as i:
                    attention(S_RET + 8 * g + i * 4, 2 * g + i, g)

            vst_m, sct_m = Mark(s_vst), Mark(s_sct)
            rr_m = Mark(s_rope)
            rr_m.local = rope_m.value
            re_marks = {fill[0]: 1, fill[1]: 1, fill[2]: 1, fill[3]: 1, fill[4]: 2, fill[5]: 2, fill[6]: 2,
                        fill[7]: 2, vst_m: 1, sct_m: 4, rr_m: 2}
            with counted(pe, RH, re_marks) as u:
                s0 = S_GATE + u * 4

                def half(n):
                    tile(s0 + n // 2, n // 2, n % 2, LOW, r1_hi, r1_lo, n, KD, False)
                half(0)
                half(1)
                half(2)
                for b, c in ((4, 0), (5, 1)):
                    pe.wait_ge(s_rope, rr_m.up())
                    turn(b, lambda t, c=c: r_rot[:, c, t, :])
                ready = [fill[4].value, fill[5].value]
                half(3)
                pe.wait_ge(s_drain[4], ready[0])
                pe.wait_ge(s_drain[5], ready[1])
                for jt, b in enumerate((6, 7, 4, 5)):
                    begin(b)
                    kc = slice(jt * P, (jt + 1) * P)
                    three(ps[b][:, :], rk_t[:, 0, kc], rk_t[:, 1, kc], rq_t[:, 0, :], rq_t[:, 1, :],
                          True, True, False, b)
                half(4)
                half(5)
                pe.wait_ge(s_vst, vst_m.up())
                for b in (6, 7):
                    begin(b)
                    for e in range(2):
                        it = 2 * (b - 6) + e
                        for jt in range(NT):
                            if it == 0:
                                pe.wait_ge(s_sct, sct_m.up())
                            ic = slice(it * P, (it + 1) * P)
                            o = ps[b][:, e * 256:(e + 1) * 256]
                            pe.matmul(o, prt_hi[:, jt, ic], rv_st[:, jt, :], start=(jt == 0), stop=False)
                            m = pe.matmul(o, prt_lo[:, jt, ic], rv_st[:, jt, :], start=False, stop=(jt == 3))
                    m.then_inc(s_fill[b], 1)
                half(6)
                half(7)

            def project(s, banks, x_hi, x_lo, k_end, tokens, ready=None):
                for j in range(k_end // 2):
                    if ready:
                        ready(2 * j)
                    slab(s + j, (s + j) % RING, banks, x_hi, x_lo, 2 * j, k_end, tokens)

            project(S_AO, LOW, at_hi, at_lo, 4, False, lambda k: pe.wait_ge(s_osp, k + 2))
            project(S_AO + 2, HIGH, at_hi, at_lo, 4, False)
            pe.wait_ge(s_ry, NT)
            for k in range(4):
                turn(LOW[k], lambda t, k=k: ret[:, 0, t, k * P:(k + 1) * P])
            for k in range(4):
                pe.wait_ge(s_drain[LOW[k]], fill[LOW[k]].value)
                tile(S_RO + k // 2, (S_RO + k // 2) % RING, k % 2, HIGH, ry_hi, ry_lo, k, 4, False)
            project(S_RO + 2, LOW, ry_hi, ry_lo, 4, False)

            project(S_OUT, HIGH, r1_hi, r1_lo, KD, True, lambda k: pe.wait_ge(s_mgs, k + 2))

            def chunk_and_turn(s, x_hi, x_lo, k_end):
                for j in range(k_end // 2):
                    if j == k_end // 2 - 1:
                        for b in HIGH:
                            pe.wait_ge(s_drain[b], fill[b].value)
                        turn_x(xs, 0, HIGH)
                    slab(s + j, (s + j) % RING, LOW, x_hi, x_lo, 2 * j, k_end, True)

            def chunk_from_turns(s, tokens):
                for j in range(4):
                    for n in (2 * j, 2 * j + 1):
                        if n == 2:
                            for b in LOW:
                                pe.wait_ge(s_drain[b], fill[b].value)
                            turn_x(xs, 4, LOW)
                        if n == 0:
                            for b in HIGH:
                                pe.wait_ge(s_drain[b], fill[b].value)
                        if n >= 4:
                            pe.wait_ge(s_drain[LOW[n - 4]], fill[LOW[n - 4]].value)
                        tile(s + j, j, n % 2, HIGH, xt_hi, xt_lo, n, KD, tokens)

            chunk_and_turn(S_OUT + 4, r1_hi, r1_lo, KD)
            chunk_from_turns(S_UP0, False)

            hid_m = Mark(s_hids)

            def down(s, slot, banks, first, h_hi=r1_hi, h_lo=r1_lo):
                for j in range(2):
                    if first:
                        for _ in range(2):
                            hid_m.up()
                        pe.wait_ge(s_hids, hid_m.value)
                    slab(s + j, slot + j, banks, h_hi, h_lo, 2 * j, 4, True)

            mlp_marks = {hid_m: 4}
            for b in LOW:
                mlp_marks[fill[b]] = 2
            for b in HIGH:
                mlp_marks[fill[b]] = 1
            with counted(pe, NF - 1, mlp_marks) as f:
                s0 = S_MLP + f * 8
                for j in range(4):
                    slab(s0 + j, j, LOW, xt_hi, xt_lo, 2 * j, KD, False)
                down(s0 + 4, 0, HIGH, True)
                down(s0 + 6, 2, LOW, False)
            down(S_DOWN7, 0, HIGH, True, xt_hi[:, 4:8, :], xt_lo[:, 4:8, :])
            chunk_and_turn(S_DOWN7 + 2, xt_hi[:, 4:8, :], xt_lo[:, 4:8, :], 4)

            chunk_from_turns(S_PG, True)
            for t, b in enumerate(LOW):
                begin(b)
                for k in range(KD):
                    j = k // 2
                    used = slab_start(S_PG + 4 + j) if t == 0 and k % 2 == 0 else False
                    cols = slice(k % 2 * C, (k % 2 + 1) * C)
                    tc = slice(t * P, (t + 1) * P)
                    three(ps[b][:, :], xt_hi[:, k, tc], xt_lo[:, k, tc], w_hi[:, j, cols], w_lo[:, j, cols],
                          k == 0, k == KD - 1, used, b if k == KD - 1 else None)

        @block.scalar
        def _(act):
            fill = [Mark(s_fill[b]) for b in range(8)]
            ahi = Mark(s_ahi)
            steps = Mark(s_act)

            def ahead(s, slot):
                s3, n = s + 3, (slot + 3) % RING
                turn_of = s3 // RING + 1 if isinstance(s3, int) else None
                act.wait_ge(s_slab[n], 16 * turn_of)
                if not (isinstance(s, int) and s < 1):
                    act.wait_ge(s_used, s)
                act.activation(w_hi[:, n, :], raw[:, n, :], ACT.Copy).then_inc(s_hi, 1)

            def ahead_in(base, i, per, j, slot):
                n = (slot + 3) % RING
                q = (base + j + 3) // RING + 1
                act.wait_ge(s_slab[n], (i * (per // RING) + q) * 16)
                act.wait_ge(s_used, i * per + (base + j))
                act.activation(w_hi[:, n, :], raw[:, n, :], ACT.Copy).then_inc(s_hi, 1)

            def filled(b):
                act.wait_ge(s_fill[b], fill[b].up())

            def skip(b):
                fill[b].up()

            def hi(dst, src, scale=1.0):
                ahi.up()
                return act.activation(dst, src, ACT.Copy, scale=scale).then_inc(s_ahi, 1)

            def drained(b, ins):
                ins.then_inc(s_drain[b], 1)

            act.dma_start(ident, tables[:, T_ID:T_ID + P]).then_inc(s_id, 16)
            act.dma_start(tab[:, T_CA:T_END], tables[:, T_CA:T_END]).then_inc(s_tab, 16)
            act.dma_start(gains[:, 0:24], norms).then_inc(s_tab, 16)
            act.dma_start(qg, q_gain.partition_broadcast(P)).then_inc(s_tab, 16)
            act.dma_start(kg, k_gain.partition_broadcast(P)).then_inc(s_tab, 16)
            act.dma_start(rg_g, ret_gain.partition_broadcast(P)).then_inc(s_tab, 16)
            act.dma_start(dec, decay.partition_broadcast(P)).then_inc(s_tab, 16)

            def first_hi(n):
                act.wait_ge(s_slab[n], 16)
                act.activation(w_hi[:, n, :], raw[:, n, :], ACT.Copy).then_inc(s_hi, 1)

            def x_squares(t):
                act.wait_ge(s_x[t], 16)
                if t:
                    act.wait_ge(s_ss, t)
                act.activation(squares, x0[:, t, :], ACT.Square, accum_out=ss[:, t:t + 1]).then_inc(s_ss, 1)

            def turned_hi(k):
                filled(HIGH[k % 4])
                hi(r1_hi[:, k, :], ps[HIGH[k % 4]][:, :], scale=mix_g[:, k:k + 1])

            first_hi(0)
            for k, b in ((0, 4), (1, 5)):
                filled(b)
                hi(pt_hi[:, k, :], ps[b][:, :])
            first_hi(1)
            for t in range(NT - 1):
                x_squares(t)
            act.wait_ge(s_tab, 16 * 6)
            for k in range(4):
                turned_hi(k)
            for t in range(NT):
                filled(t)
                if t % 2 == 0:
                    drained(t, act.copy(ple_w[:, t, 0:C], ps[t][:, :]))
            first_hi(2)
            for k in range(4, KD):
                turned_hi(k)
            x_squares(NT - 1)
            ahead(0, 0)
            act.wait_ge(s_dexp, 1)
            act.activation(lt[:, 1, :], lt[:, 0, :], ACT.Exp).then_inc(s_du, 1)
            for j in range(2):
                ahead(S_AKV + j, (S_AKV + j) % RING)
            act.wait_ge(s_rr, 1)
            for t in range(NT):
                filled(t)
                act.activation(k_raw[:, t, :], ps[t][:, 0:P], ACT.Copy, scale=row_r[:, t:t + 1]).then_inc(s_act, 1)
                steps.up()
                hi(v_st[:, :, t, 0:HD], ps[t][:, P:2 * P].rearrange("p (g d) -> p g d", g=KV), scale=row_r[:, t:t + 1])
            for j in range(3):
                ahead(S_AQ + j, (S_AQ + j) % RING)
            filled(2)
            drained(2, act.copy(scale_t, ps[2][:, :]))
            filled(3)
            hi(k_st[0:HD, 0, 0, :], ps[3][0:HD, :])
            hi(k_st[HD:P, 1, 0, :], ps[3][HD:P, :])
            act.copy(k_st[HD:P, 0, 0, :], ps[3][0:HD, :]).then_inc(s_act, 1)
            act.copy(k_st[0:HD, 1, 0, :], ps[3][HD:P, :]).then_inc(s_act, 1)
            steps.local += 2
            ahead(S_AQ + 3, (S_AQ + 3) % RING)
            for t in range(NT):
                b = HIGH[t]
                filled(b)
                if t % 2 == 0:
                    drained(b, act.activation(q_raw[:, t, :], ps[b][:, :], ACT.Copy, scale=row_r[:, t:t + 1]))
            ahead(S_PLE1, S_PLE1 % RING)
            for t in range(NT):
                filled(t)
                if t % 2 == 0:
                    drained(t, act.copy(ple_w[:, t, C:2 * C], ps[t][:, :]))
            for t in range(NT):
                act.wait_ge(s_drain[t], fill[t].value)
            act.dma_start(ple_spill, region(fp, RR + 4096, 4096)).then_inc(s_spill, 16)

            shift_m = Mark(s_shift)

            def soft():
                for qt in range(NT):
                    b = HIGH[qt]
                    filled(b)
                    act.wait_ge(s_shift, shift_m.up())
                    drained(b, act.activation(prob[:, qt, :], ps[b][:, :], ACT.Exp, bias=nb[:, qt:qt + 1],
                                              scale=HD ** -0.5, accum_out=den[:, qt:qt + 1]))

            def split_probs():
                for kt in range(NT):
                    filled(HIGH[kt])
                    hi(prt_hi[:, kt, :], ps[HIGH[kt]][:, :])

            def low_half():
                filled(7)
                act.copy(otmp_a[0:HD, :], ps[7][HD:P, :]).then_inc(s_otmp, 1)

            def drain_ret(c):
                for t in range(NT):
                    filled(t)
                    if t % 2 == 0:
                        drained(t, act.activation(ret[:, bass.ds(c, 1), t, :].rearrange("p a n -> p (a n)"),
                                                  ps[t][:, :], ACT.Copy, scale=row_r[:, t:t + 1]))

            at_marks = {fill[0]: 1, fill[1]: 1, fill[2]: 1, fill[3]: 1, fill[4]: 5, fill[5]: 4, fill[6]: 4,
                        fill[7]: 6, ahi: 10, shift_m: 8}
            for g in range(KV):
                if g:
                    act.wait_ge(s_spill, 16)
                with counted(act, 2, at_marks) as i:
                    base = S_RET + 8 * g
                    filled(4)
                    hi(q_st[0:HD, 0, :], ps[4][0:HD, :])
                    hi(q_st[HD:P, 1, :], ps[4][HD:P, :])
                    ahead_in(base, i, 4, 0, 0)
                    soft()
                    ahead_in(base, i, 4, 1, 1)
                    split_probs()
                    low_half()
                    ahead_in(base, i, 4, 2, 2)
                    soft()
                    ahead_in(base, i, 4, 3, 3)
                    split_probs()
                    drain_ret(2 * g + i)
                    low_half()

            act.dma_start(delta, delta_in).then_inc(s_dlt, 16)
            mexp_m = Mark(s_mexp)
            re_marks = {fill[0]: 1, fill[1]: 1, fill[2]: 1, fill[3]: 1, fill[4]: 2, fill[5]: 2, fill[6]: 2,
                        fill[7]: 2, ahi: 7, mexp_m: 1}
            with counted(act, RH, re_marks) as u:
                ahead_in(S_GATE, u, 4, 0, 0)
                hi(rv_st[:, :, 0:P], ret[:, 2, :, bass.ds(u * P, P)])
                act.wait_ge(s_mexp, mexp_m.up())
                diag = (NT - 1) * P
                act.activation(mask[:, 0:diag], delta[:, 0:diag], ACT.Exp, scale=lg[:, bass.ds(u + RH, 1)])
                act.activation(mask[:, diag + P:DELTA], delta[:, diag + P:DELTA], ACT.Exp, scale=lg[:, bass.ds(u, 1)])
                act.activation(mask[:, diag:diag + P], mask[:, diag:diag + P], ACT.Exp).then_inc(s_mask, 1)
                ahead_in(S_GATE, u, 4, 1, 1)
                for b, dst in ((4, rq_t), (5, rk_t)):
                    filled(b)
                    hi(dst[:, 0, :], ps[b][:, :])
                ahead_in(S_GATE, u, 4, 2, 2)
                for jt, b in enumerate((6, 7, 4, 5)):
                    skip(b)
                    act.wait_ge(s_drain[b], fill[b].value)
                    hi(prt_hi[:, jt, :], sc_f[:, jt % 2, :])
                ahead_in(S_GATE, u, 4, 3, 3)
                for b in (6, 7):
                    filled(b)
                    act.copy(otmp[:, (b - 6) * 256:(b - 5) * 256].rearrange("p (e n) -> p e n", e=2),
                             ps[b][:, :].rearrange("p (e s n) -> p e s n", e=2, s=2)[:, :, 1, :]).then_inc(s_otmp, 1)
                for m in LOW:
                    filled(m)
                    drained(m, act.copy(gate[:, bass.ds(u * 4 + m, 1), :].rearrange("p a n -> p (a n)"),
                                        ps[m][:, :]))

            for k in range(4):
                hi(at_hi[:, k, :], ot[:, k, :])
            for t in range(NT):
                act.activation(ret[:, 1, t, :], ret[:, 3, t, :], ACT.Sigmoid).then_inc(s_rgs, 1)
            for j in range(2):
                ahead(S_AO + j, (S_AO + j) % RING)
                act.wait_ge(s_gr, j + 1)
                for m in range(4 * j, 4 * j + 4):
                    act.activation(gate[:, m, :], gate[:, m, :], ACT.Sigmoid).then_inc(s_gs, 1)
            for b in LOW + HIGH:
                skip(b)
            ahead(S_AO + 2, (S_AO + 2) % RING)
            act.wait_ge(s_gr, 4)
            for m in range(8, 12):
                act.activation(gate[:, m, :], gate[:, m, :], ACT.Sigmoid).then_inc(s_gs, 1)
            ahead(S_AO + 3, (S_AO + 3) % RING)
            for m in range(12, 16):
                act.activation(gate[:, m, :], gate[:, m, :], ACT.Sigmoid).then_inc(s_gs, 1)
            for k in range(4):
                filled(LOW[k])
                hi(ry_hi[:, k, :], ps[LOW[k]][:, :])
            act.wait_ge(s_rgs, NT)
            act.wait_ge(s_ry, NT)
            act.dma_start(xs, x_in.rearrange("(t p) n -> p t n", p=P)).then_inc(s_xr, 16)
            for j in range(4):
                ahead(S_RO + j, (S_RO + j) % RING)
                for m in ((0, 1, 2, 3) if j == 1 else (4, 5, 6, 7) if j == 3 else ()):
                    skip(HIGH[m] if j == 1 else LOW[m - 4])
                    act.wait_ge(s_mg, m + 1)
                    hi(r1_hi[:, m, :], merged[:, m, :])
            for b in HIGH:
                skip(b)
            for j in range(4):
                ahead(S_OUT + j, (S_OUT + j) % RING)
            act.wait_ge(s_mgs, 8)
            act.dma_start(region(fp, RR, 4096), ple_spill).then_inc(s_pler, 16)
            def split_turned(k0, banks, gain):
                for n, b in enumerate(banks):
                    filled(b)
                    hi(xt_hi[:, k0 + n, :], ps[b][:, :], scale=gain[:, k0 + n:k0 + n + 1])

            def row_squares(first_sum):
                for t in range(NT):
                    if t or first_sum:
                        act.wait_ge(s_ss, first_sum + t)
                    act.activation(squares2, xs[:, t, :], ACT.Square, accum_out=ss[:, t:t + 1]).then_inc(s_ss, 1)

            for j in range(4):
                if j == 3:
                    split_turned(0, HIGH, mlp_g)
                ahead(S_OUT + 4 + j, j)
            for b in LOW:
                skip(b)
            for j in range(4):
                ahead(S_UP0 + j, (S_UP0 + j) % RING)
                if j == 1:
                    split_turned(4, LOW, mlp_g)
                if j == 2:
                    row_squares(NT)

            def relus(banks):
                for m, b in enumerate(banks):
                    filled(b)
                    drained(b, act.activation(stage[:, m, :], ps[b][:, :], ACT.Relu))

            hid_m = Mark(s_hid)

            def split_hidden(dst):
                for m in range(4):
                    act.wait_ge(s_hid, hid_m.up())
                    hi(dst[:, m, :], stage[:, m, :])

            relus(HIGH)
            mlp_marks = {fill[b]: 2 for b in LOW}
            mlp_marks.update({fill[b]: 1 for b in HIGH})
            mlp_marks.update({ahi: 4, hid_m: 4})
            with counted(act, NF - 1, mlp_marks) as f:
                ahead_in(S_MLP, f, 8, 0, 0)
                act.wait_ge(s_fill[3], fill[3].value)
                split_hidden(r1_hi)
                for j in range(1, 4):
                    ahead_in(S_MLP, f, 8, j, j)
                act.wait_ge(s_hids, f * 4 + 4)
                relus(LOW)
                for j in range(4, 8):
                    ahead_in(S_MLP, f, 8, j, j % RING)
                for b in HIGH + LOW:
                    skip(b)
            split_hidden(xt_hi[:, 4:8, :])
            act.dma_start(fin_g, fin_gain.partition_broadcast(P)).then_inc(s_fin, 16)
            for j in range(4):
                if j == 3:
                    for b in HIGH:
                        skip(b)
                    split_turned(0, HIGH, ple_g)
                ahead(S_DOWN7 + j, j)
            for b in LOW:
                skip(b)
            for j in range(4):
                ahead(S_PG + j, j)
                if j == 1:
                    split_turned(4, LOW, ple_g)
                if j == 2:
                    row_squares(2 * NT)
            ahead(S_PG + 4, 0)
            act.wait_ge(s_rs, 1)
            def gate_of(c, t, b):
                filled(b)
                drained(b, act.activation(sig[:, c, t, :], ps[b][:, :], ACT.Sigmoid, scale=rstd[:, t:t + 1]))

            def half_squares(c, t):
                act.wait_ge(s_xf, NT * c + t + 1)
                act.wait_ge(s_ss, 3 * NT + NT * c + t)
                act.activation(squares2[:, 0:C], xs[:, t, c * C:(c + 1) * C], ACT.Square,
                               accum_out=ss2[:, 2 * t + c:2 * t + c + 1]).then_inc(s_ss, 1)

            for t in range(NT):
                gate_of(0, t, HIGH[t])
            for t in range(NT):
                half_squares(0, t)
            for t in range(NT):
                gate_of(1, t, LOW[t])
                half_squares(1, t)
            for t in range(NT):
                act.wait_ge(s_fo, t + 1)
                act.dma_start(out[t * P:(t + 1) * P, :], out_sb[:, t, :]).then_inc(s_out, 16)
            act.wait_ge(s_out, 16 * NT)

        @block.vector
        def _(dve):
            fill = [Mark(s_fill[b]) for b in range(8)]
            ahi = Mark(s_ahi)
            steps = Mark(s_dve)
            roped = Mark(s_rope)

            def filled(b):
                dve.wait_ge(s_fill[b], fill[b].up())

            def skip(b):
                fill[b].up()

            def step(ins):
                ins.then_inc(s_dve, 1)
                steps.up()

            def settle():
                dve.wait_ge(s_dve, steps.value)

            def carry_waits():
                step(dve.memset(small[:, 152:153], 0.0))

            def lo(dst, src, hi_part):
                dve.wait_ge(s_ahi, ahi.up())
                return dve.tensor_tensor(dst, src, f32(hi_part), ALU.subtract)

            def rsqrt(dst, src):
                n = dst.shape[-1]
                t = nwt[:, 0:n]
                step(dve.tensor_scalar(dst.bitcast(I32), src.bitcast(I32), -0.5, 1597463007.0, ALU.mult, ALU.add))
                settle()
                for _ in range(3):
                    step(dve.tensor_tensor(t, dst, dst, ALU.mult))
                    settle()
                    step(dve.scalar_tensor_tensor(t, t, -0.5, src, ALU.mult, ALU.mult))
                    settle()
                    step(dve.scalar_tensor_tensor(dst, t, 1.5, dst, ALU.add, ALU.mult))
                    settle()

            def rope(o1, o2, x1, x2, cos, sin, shape):
                n = 1
                for v in shape[1:]:
                    n *= v
                def buf(k):
                    v = rope_tmp[:, k * n:(k + 1) * n]
                    if len(shape) == 4:
                        return v.rearrange("p (t h d) -> p t h d", t=shape[1], h=shape[2])
                    return v.rearrange("p (t d) -> p t d", t=shape[1])
                a, b = buf(0), buf(1)

                def first():
                    step(dve.tensor_tensor(a, x1, sin, ALU.mult))
                    step(dve.tensor_tensor(b, x2, sin, ALU.mult))
                    step(dve.tensor_tensor(o1, x1, cos, ALU.mult))
                    step(dve.tensor_tensor(o2, x2, cos, ALU.mult))

                def last():
                    step(dve.tensor_tensor(o1, o1, b, ALU.subtract))
                    return dve.tensor_tensor(o2, o2, a, ALU.add)
                return first, last

            def head_steps(dst, v, gain):
                half = HD // 2
                dv = dst.rearrange("p t (h d) -> p t h d", h=2)
                hv = v.rearrange("p t (h d) -> p t h d", h=2)
                c = cos_a.unsqueeze(2).to_broadcast([P, NT, 2, half])
                s = sin_a.unsqueeze(2).to_broadcast([P, NT, 2, half])

                def mean_squares():
                    dve.wait_ge(s_rope, roped.value)
                    step(dve.tensor_tensor(q_sq, v, v, ALU.mult))
                    settle()
                    step(dve.tensor_reduce(hss, q_sq.rearrange("p t (h d) -> p (t h) d", h=2), AX.X, ALU.add))
                    settle()
                    step(dve.tensor_scalar(hss, hss, 1.0 / HD, NORM_EPS, ALU.mult, ALU.add))
                    settle()

                def scale():
                    r = hr.rearrange("p (t h) -> p t h", h=2).unsqueeze(3).to_broadcast([P, NT, 2, HD])
                    step(dve.tensor_tensor(hv, hv, r, ALU.mult))
                    settle()
                    g = gain.unsqueeze(1).unsqueeze(1).to_broadcast([P, NT, 2, HD])
                    step(dve.tensor_tensor(hv, hv, g, ALU.mult))
                    settle()

                first, last = rope(dv[:, :, :, 0:half], dv[:, :, :, half:HD], hv[:, :, :, 0:half],
                                   hv[:, :, :, half:HD], c, s, [P, NT, 2, half])

                def rotate():
                    settle()
                    last().then_inc(s_rope, 1)
                    roped.up()
                return mean_squares, lambda: rsqrt(hr, hss), scale, first, rotate

            for k, b in ((0, 4), (1, 5)):
                filled(b)
                lo(pt_lo[:, k, :], ps[b][:, :], pt_hi[:, k, :]).then_inc(s_drain[b], 1)
            dve.wait_ge(s_tab, 16 * 6)
            step(dve.tensor_scalar(lt[:, 2, :], dec, -1.0, None, ALU.mult))
            settle()
            dve.tensor_tensor(lt[:, 0, :], dec, lt[:, 2, :], ALU.min).then_inc(s_dexp, 1)

            def split_turned(dst_lo, dst_hi, k0, banks, gain):
                for n, b in enumerate(banks):
                    filled(b)
                    dve.wait_ge(s_ahi, ahi.up())
                    dve.scalar_tensor_tensor(dst_lo[:, k0 + n, :], ps[b][:, :], gain[:, k0 + n:k0 + n + 1],
                                             f32(dst_hi[:, k0 + n, :]), ALU.mult, ALU.subtract)\
                       .then_inc(s_drain[b], 1)
            dve.wait_ge(s_tab, 16 * 6)
            split_turned(r1_lo, r1_hi, 0, HIGH, mix_g)
            for t in range(NT):
                filled(t)
                if t % 2:
                    dve.tensor_copy(ple_w[:, t, 0:C], ps[t][:, :]).then_inc(s_drain[t], 1)
            split_turned(r1_lo, r1_hi, 4, HIGH, mix_g)
            dve.wait_ge(s_ss, NT)
            step(dve.tensor_scalar(inv_ms, ss, 1.0 / D, NORM_EPS, ALU.mult, ALU.add))
            settle()
            rsqrt(row_r, inv_ms)
            dve.nop().then_inc(s_rr, 1)

            dve.wait_ge(s_du, 1)
            u_, w_, s_, q_ = lt[:, 1, :], lt[:, 2, :], lt[:, 3, :], lt[:, 4, :]
            step(dve.tensor_scalar(w_, u_, 2.0, None, ALU.add))
            settle()
            step(dve.reciprocal(w_, w_))
            settle()
            step(dve.tensor_tensor(s_, u_, w_, ALU.mult))
            settle()
            step(dve.tensor_tensor(w_, s_, s_, ALU.mult))
            settle()
            step(dve.tensor_scalar(q_, w_, 1.0 / 17, None, ALU.mult))
            settle()
            for n in (15, 13, 11, 9, 7, 5, 3):
                step(dve.scalar_tensor_tensor(q_, q_, 1.0 / n, w_, ALU.add, ALU.mult))
                settle()
            step(dve.scalar_tensor_tensor(q_, q_, 1.0, s_, ALU.add, ALU.mult))
            step(dve.tensor_scalar(w_, dec, 0.0, None, ALU.min))
            settle()
            step(dve.scalar_tensor_tensor(lg, q_, -2.0, w_, ALU.mult, ALU.add))
            settle()
            step(dve.tensor_scalar(lg[:, RH:2 * RH], lg[:, RH:2 * RH], -1.0, None, ALU.mult))

            for t in range(NT):
                filled(t)
                dve.wait_ge(s_act, t + 1)
                dve.wait_ge(s_ahi, ahi.up())
                dve.scalar_tensor_tensor(v_st[:, :, t, HD:P], ps[t][:, P:2 * P].rearrange("p (g d) -> p g d", g=KV),
                                         row_r[:, t:t + 1], f32(v_st[:, :, t, 0:HD]), ALU.mult, ALU.subtract)\
                    .then_inc(s_drain[t], 1)
            for part in head_steps(k_rot, k_raw, kg):
                part()
            skip(2)
            filled(3)
            dve.wait_ge(s_act, NT + 2)
            for g, rows, other in ((0, slice(0, HD), slice(HD, P)), (1, slice(HD, P), slice(0, HD))):
                dve.wait_ge(s_ahi, ahi.up())
                step(dve.tensor_tensor(k_st[rows, g, 1, :], ps[3][rows, :], f32(k_st[rows, g, 0, :]), ALU.subtract))
                ins = dve.tensor_tensor(k_st[other, g, 1, :], ps[3][rows, :], f32(k_st[rows, g, 0, :]), ALU.subtract)
                if g == 0:
                    step(ins)
            ins.then_inc(s_drain[3], 1)
            for t in range(NT):
                b = HIGH[t]
                filled(b)
                if t % 2:
                    dve.tensor_scalar(q_raw[:, t, :], ps[b][:, :], row_r[:, t:t + 1], None, ALU.mult)\
                       .then_inc(s_drain[b], 1)
            for b in HIGH:
                dve.wait_ge(s_drain[b], fill[b].value)
            parts = head_steps(q_rot, q_raw[:, :, 0:P], qg)
            for part in parts:
                part()
            for t in range(NT):
                filled(t)
                if t % 2:
                    dve.tensor_copy(ple_w[:, t, C:2 * C], ps[t][:, :]).then_inc(s_drain[t], 1)

            otmp_m = Mark(s_otmp)

            def soft():
                n0 = []
                for qt in range(NT):
                    b = HIGH[qt]
                    filled(b)
                    step(dve.tensor_reduce(mx[:, qt:qt + 1], ps[b][:, :], AX.X, ALU.max))
                    settle()
                    dve.tensor_scalar(nb[:, qt:qt + 1], mx[:, qt:qt + 1], -(HD ** -0.5), None, ALU.mult)\
                       .then_inc(s_shift, 1)
                    n0.append(fill[b].value)
                for qt in range(NT):
                    dve.wait_ge(s_drain[HIGH[qt]], n0[qt])
                    step(dve.reciprocal(rden[:, qt:qt + 1], den[:, qt:qt + 1]))
                    settle()
                    dve.tensor_scalar(prob[:, qt, :], prob[:, qt, :], rden[:, qt:qt + 1], None, ALU.mult)\
                       .then_inc(s_prob, 1)

            def split_probs():
                for kt in range(NT):
                    b = HIGH[kt]
                    filled(b)
                    lo(prt_lo[:, kt, :], ps[b][:, :], prt_hi[:, kt, :]).then_inc(s_drain[b], 1)

            def join(pair, rows):
                filled(7)
                dve.wait_ge(s_otmp, otmp_m.up())
                dve.tensor_tensor(ot[rows, bass.ds(pair, 1), :].rearrange("p a n -> p (a n)"),
                                  ps[7][0:HD, :], otmp_a[0:HD, :], ALU.add).then_inc(s_drain[7], 1)

            def drain_ret(c):
                for t in range(NT):
                    filled(t)
                    if t % 2:
                        dve.tensor_scalar(ret[:, bass.ds(c, 1), t, :].rearrange("p a n -> p (a n)"), ps[t][:, :],
                                          row_r[:, t:t + 1], None, ALU.mult).then_inc(s_drain[t], 1)

            def attention(g, pair, last):
                filled(4)
                dve.wait_ge(s_ahi, ahi.up())
                step(dve.tensor_tensor(q_st[HD:P, 0, :], ps[4][0:HD, :], f32(q_st[0:HD, 0, :]), ALU.subtract))
                dve.wait_ge(s_ahi, ahi.up())
                settle()
                dve.tensor_tensor(q_st[0:HD, 1, :], ps[4][HD:P, :], f32(q_st[HD:P, 1, :]), ALU.subtract)\
                   .then_inc(s_drain[4], 1)
                if last:
                    parts = [lambda: None] * 5
                else:
                    parts = head_steps(q_rot, q_raw[:, :, bass.ds((pair + 1) * P, P)], qg)
                soft()
                parts[0]()
                split_probs()
                parts[1]()
                join(pair, slice(0, HD))
                parts[2]()
                soft()
                parts[3]()
                split_probs()
                parts[4]()
                drain_ret(pair)
                join(pair, slice(HD, P))

            HEADS_STEPS = 3 + 10 + 2 + 5
            at_marks = {fill[0]: 1, fill[1]: 1, fill[2]: 1, fill[3]: 1, fill[4]: 5, fill[5]: 4, fill[6]: 4,
                        fill[7]: 6, ahi: 10, otmp_m: 2, roped: 1, steps: 1 + 16 + HEADS_STEPS}
            with counted(dve, 2, at_marks) as i:
                attention(0, i, False)
            attention(1, 2, False)
            attention(1, 3, True)

            for b in LOW:
                dve.wait_ge(s_drain[b], fill[b].value)
            dve.wait_ge(s_drain[7], fill[7].value)
            dve.wait_ge(s_dlt, 16)
            mask_m = Mark(s_mask)
            half = RHD // 2

            def rotate_heads(u):
                dve.wait_ge(s_sct, u * NT)
                for c in (0, 1):
                    v = ret[:, c, :, :]
                    first, last = rope(r_rot[:, c, :, 0:half], r_rot[:, c, :, half:RHD], v[:, :, bass.ds(u * P, half)],
                                       v[:, :, bass.ds(u * P + half, half)], cos_r, sin_r, [P, NT, half])
                    first()
                    settle()
                    last().then_inc(s_rope, 1)
                    dve.wait_ge(s_rope, roped.up())

            def decays(u):
                diag = slice((NT - 1) * P, NT * P)
                step(dve.tensor_scalar(mask[:, diag], delta[:, diag], 0.0, lg[:, bass.ds(u, 1)], ALU.max, ALU.mult))
                step(dve.tensor_scalar(mtmp, delta[:, diag], 0.0, lg[:, bass.ds(u + RH, 1)], ALU.min, ALU.mult))
                settle()
                dve.tensor_tensor(mask[:, diag], mask[:, diag], mtmp, ALU.add).then_inc(s_mexp, 1)

            def head(u):
                hc = bass.ds(u * P, P)
                lo(rv_st[:, :, P:2 * P], ret[:, 2, :, hc], rv_st[:, :, 0:P]).then_inc(s_vst, 1)
                for b, dst in ((4, rq_t), (5, rk_t)):
                    filled(b)
                    lo(dst[:, 1, :], ps[b][:, :], dst[:, 0, :]).then_inc(s_drain[b], 1)
                dve.wait_ge(s_mask, mask_m.up())

                def finish(jt):
                    lo(prt_lo[:, jt, :], sc_f[:, jt % 2, :], prt_hi[:, jt, :]).then_inc(s_sct, 1)
                for jt, b in enumerate((6, 7, 4, 5)):
                    filled(b)
                    if jt >= 2:
                        dve.wait_ge(s_sct, u * 4 + jt - 1)
                    dve.scalar_tensor_tensor(sc_f[:, jt % 2, :], ps[b][:, :], RHD ** -0.5,
                                             mask[:, (NT - 1 - jt) * P:(NT - 1 - jt) * P + C], ALU.mult, ALU.mult)\
                       .then_inc(s_drain[b], 1)
                    if jt >= 1:
                        finish(jt - 1)
                finish(3)
                for b in (6, 7):
                    filled(b)
                    dve.wait_ge(s_otmp, otmp_m.up())
                    dve.tensor_tensor(ret[:, 0, 2 * (b - 6):2 * (b - 6) + 2, hc],
                                      ps[b][:, :].rearrange("p (e s n) -> p e s n", e=2, s=2)[:, :, 0, :],
                                      otmp[:, (b - 6) * 256:(b - 5) * 256].rearrange("p (e n) -> p e n", e=2),
                                      ALU.add).then_inc(s_drain[b], 1)
                for b in (6, 7):
                    dve.wait_ge(s_drain[b], fill[b].value)
                carry_waits()
                for m in LOW:
                    skip(m)

            def group_norm(u):
                hc = bass.ds(u * P, P)
                for t in range(NT):
                    step(dve.bn_stats(bst[:, t, :], ret[:, 0, t, hc]))
                settle()
                carry_waits()
                for t in range(NT):
                    step(dve.bn_aggr(mv[:, t, :], bst[:, t, :]))
                settle()
                step(dve.tensor_scalar(rvar, mv[:, :, 1], GN_EPS, None, ALU.add))
                settle()
                rsqrt(rstd, rvar)
                for t in range(NT):
                    step(dve.tensor_scalar(ret[:, 0, t, hc], ret[:, 0, t, hc], mv[:, t, 0:1], rstd[:, t:t + 1],
                                           ALU.subtract, ALU.mult))
                settle()
                gb = rg_g[:, hc].unsqueeze(1).to_broadcast([P, NT, RHD])
                step(dve.tensor_tensor(ret[:, 0, :, hc], ret[:, 0, :, hc], gb, ALU.mult))
                settle()
                step(dve.tensor_tensor(ret[:, 0, :, hc], ret[:, 0, :, hc], ret[:, 3, :, hc], ALU.mult))

            re_marks = {fill[0]: 1, fill[1]: 1, fill[2]: 1, fill[3]: 1, fill[4]: 2, fill[5]: 2, fill[6]: 2,
                        fill[7]: 2, ahi: 7, otmp_m: 2, mask_m: 1, roped: 2,
                        steps: 2 + 10 + 4 + 4 + 2 + 1 + 10 + 4 + 2}
            def scale_gates(u):
                for b in LOW:
                    dve.wait_ge(s_drain[b], fill[b].value)
                g = gate[:, bass.ds(u * 4, 4), :]
                dve.tensor_tensor(g, g, scale_t.unsqueeze(1).to_broadcast([P, 4, C]), ALU.mult).then_inc(s_gr, 1)

            decays(0)
            rotate_heads(0)
            head(0)
            with counted(dve, RH - 1, re_marks) as i:
                rotate_heads(i + 1)
                decays(i + 1)
                group_norm(i)
                scale_gates(i)
                head(i + 1)

            for k in range(4):
                lo(at_lo[:, k, :], ot[:, k, :], at_hi[:, k, :]).then_inc(s_osp, 1)
            scale_gates(RH - 1)
            group_norm(RH - 1)
            settle()
            for t in range(NT):
                dve.wait_ge(s_rgs, t + 1)
                dve.tensor_tensor(ret[:, 0, t, :], ret[:, 0, t, :], ret[:, 1, t, :], ALU.mult).then_inc(s_ry, 1)
            def attn_branch(ms):
                for m in ms:
                    b = m
                    filled(b)
                    dve.wait_ge(s_gs, m + 1)
                    dve.tensor_tensor(gate[:, m, :], ps[b][:, :], gate[:, m, :], ALU.mult).then_inc(s_drain[b], 1)

            attn_branch(range(8))
            for k in range(4):
                filled(LOW[k])
                lo(ry_lo[:, k, :], ps[LOW[k]][:, :], ry_hi[:, k, :]).then_inc(s_drain[LOW[k]], 1)
            for b in LOW + HIGH:
                dve.wait_ge(s_drain[b], fill[b].value)

            def merge(m, b):
                filled(b)
                dve.wait_ge(s_gs, 8 + m + 1)
                dve.tensor_tensor(gate[:, 8 + m, :], ps[b][:, :], gate[:, 8 + m, :], ALU.mult)\
                   .then_inc(s_drain[b], 1)
                dve.wait_ge(s_drain[b], fill[b].value)
                dve.tensor_tensor(merged[:, m, :], gate[:, m, :], gate[:, 8 + m, :], ALU.add).then_inc(s_mg, 1)

            def merge_lo(m):
                lo(r1_lo[:, m, :], merged[:, m, :], r1_hi[:, m, :]).then_inc(s_mgs, 1)
            for m in range(8):
                merge(m, m % 4 + (4 if m < 4 else 0))
                if m:
                    merge_lo(m - 1)
            merge_lo(7)

            def add_columns(c, banks):
                for t in range(NT):
                    b = banks[t]
                    filled(b)
                    xc = xs[:, t, c * C:(c + 1) * C]
                    dve.tensor_tensor(xc, xc, ps[b][:, :], ALU.add).then_inc(s_drain[b], 1)

            dve.wait_ge(s_xr, 16)
            add_columns(0, HIGH)
            split_turned(xt_lo, xt_hi, 0, HIGH, mlp_g)
            add_columns(1, LOW)
            split_turned(xt_lo, xt_hi, 4, LOW, mlp_g)
            dve.wait_ge(s_ss, 2 * NT)
            step(dve.tensor_scalar(inv_ms, ss, 1.0 / D, NORM_EPS, ALU.mult, ALU.add))
            settle()
            step(dve.reciprocal(inv_ms, inv_ms))
            settle()

            def square(banks):
                for m, b in enumerate(banks):
                    skip(b)
                    dve.wait_ge(s_drain[b], fill[b].value)
                    dve.tensor_tensor(stage[:, m, :], stage[:, m, :], stage[:, m, :], ALU.mult).then_inc(s_hid, 1)

            def split_hidden(d_lo, d_hi):
                for m in range(4):
                    lo(d_lo[:, m, :], stage[:, m, :], d_hi[:, m, :]).then_inc(s_hids, 1)

            def add_scaled(c, banks):
                for t in range(NT):
                    b = banks[t]
                    filled(b)
                    xc = xs[:, t, c * C:(c + 1) * C]
                    dve.scalar_tensor_tensor(xc, ps[b][:, :], inv_ms[:, t:t + 1], xc, ALU.mult, ALU.add)\
                       .then_inc(s_drain[b], 1)

            square(HIGH)
            mlp_marks = {fill[b]: 2 for b in LOW}
            mlp_marks.update({fill[b]: 1 for b in HIGH})
            mlp_marks.update({ahi: 4})
            with counted(dve, NF - 1, mlp_marks) as f:
                split_hidden(r1_lo, r1_hi)
                square(LOW)
                add_scaled(0, HIGH)
                add_scaled(1, LOW)
            split_hidden(xt_lo[:, 4:8, :], xt_hi[:, 4:8, :])
            add_scaled(0, HIGH)
            split_turned(xt_lo, xt_hi, 0, HIGH, ple_g)
            add_scaled(1, LOW)
            split_turned(xt_lo, xt_hi, 4, LOW, ple_g)
            dve.wait_ge(s_ss, 3 * NT)
            step(dve.tensor_scalar(inv_ms, ss, 1.0 / D, NORM_EPS, ALU.mult, ALU.add))
            settle()
            rsqrt(rstd, inv_ms)
            dve.nop().then_inc(s_rs, 1)
            dve.wait_ge(s_pler, 16)
            dve.wait_ge(s_fin, 16)

            def embed(c, t, b):
                skip(b)
                dve.wait_ge(s_drain[b], fill[b].value)
                xc = xs[:, t, c * C:(c + 1) * C]
                sg = sig[:, c, t, :]
                step(dve.tensor_tensor(sg, sg, ple_r[:, t, c * C:(c + 1) * C], ALU.mult))
                settle()
                dve.tensor_tensor(xc, xc, sg, ALU.add).then_inc(s_xf, 1)

            for t in range(NT):
                embed(0, t, HIGH[t])
            for t in range(NT):
                embed(1, t, LOW[t])
                dve.wait_ge(s_ss, 4 * NT + t + 1)
                it = inv_ms[:, t:t + 1]
                step(dve.tensor_tensor(it, ss2[:, 2 * t:2 * t + 1], ss2[:, 2 * t + 1:2 * t + 2], ALU.add))
                settle()
                step(dve.tensor_scalar(it, it, 1.0 / D, NORM_EPS, ALU.mult, ALU.add))
                settle()
                rsqrt(row_r[:, t:t + 1], it)
                dve.wait_ge(s_xf, NT + t + 1)
                dve.scalar_tensor_tensor(out_sb[:, t, :], xs[:, t, :], row_r[:, t:t + 1], fin_g, ALU.mult, ALU.mult)\
                   .then_inc(s_fo, 1)


def shape_tables():
    import numpy as np

    def rope(head_dim):
        n = head_dim // 4
        freqs = np.float32(10000.0) ** (-np.arange(n, dtype=np.float32) / np.float32(n))
        pos = np.arange(SEQ)
        row, col = (pos // 64).astype(np.float32), (pos % 64).astype(np.float32)
        ang = np.concatenate([row[:, None] * freqs, col[:, None] * freqs], axis=-1).astype(np.float32)
        tiles = lambda a: a.reshape(NT, P, -1).transpose(1, 0, 2).reshape(P, -1)
        return tiles(np.cos(ang)), tiles(np.sin(ang))

    tables = np.concatenate([np.eye(P, dtype=np.float32), *rope(HD), *rope(RHD)], axis=1).astype(np.float32)
    delta = (np.arange(DELTA)[None, :] - (NT - 1) * P - np.arange(P)[:, None]).astype(np.float32)
    return tables, delta


def slabs_of(w, width):
    per = SLAB // width
    k = w.shape[0] // P
    return w.reshape(k // per, per, P, width).transpose(0, 2, 1, 3).reshape(k // per, P, SLAB)


def pack(w_in, w_attn_o, w_ret_o, w_out, w_up, w_down, w_ple_gate, w_ple):
    import numpy as np

    a = NH * HD
    kv = 2 * KV * HD
    cols = lambda w, c: slabs_of(w[:, c:c + C], C)
    parts = [cols(w_ple, 0), slabs_of(w_in[:, a:a + kv], kv), cols(w_in, 0), cols(w_ple, C)]
    parts += [cols(w_in, a + kv + n * C) for n in range(8)]
    parts += [cols(w, n * C) for w in (w_attn_o, w_ret_o, w_out) for n in range(2)]
    parts += [cols(w_up, 0)]
    for f in range(NF):
        if f + 1 < NF:
            parts.append(cols(w_up, (f + 1) * C))
        parts += [cols(w_down[f * C:(f + 1) * C], n * C) for n in range(2)]
    parts += [cols(w_ple_gate, n * C) for n in range(2)]
    return np.concatenate(parts)


def kernel(**inputs):
    import numpy as np
    import concourse.bacc as bacc
    from concourse.bass_utils import run_bass_kernel_spmd

    a = {k: np.asarray(v) for k, v in inputs.items()}
    tables, delta = shape_tables()
    norms = np.concatenate([a[n][0].reshape(KD, P).T for n in ("mix_norm", "mlp_norm", "ple_norm")], axis=1)
    arrays = {
        "slabs": pack(*(a[n][0] for n in ("w_in", "w_attn_o", "w_ret_o", "w_out", "w_up", "w_down",
                                          "w_ple_gate", "w_ple"))),
        "x": a["x"][0], "p": a["p"][0, 0], "tables": tables, "delta": delta, "norms": norms,
        "q_gain": a["attn_q_norm"][0], "k_gain": a["attn_k_norm"][0], "ret_gain": a["ret_norm_gain"][0],
        "final_gain": a["final_norm"], "decay": a["ret_decay_logit"][0].reshape(-1),
    }
    arrays = {f"in_{k}": np.ascontiguousarray(v) for k, v in arrays.items()}
    nc = bacc.Bacc("TRN2", target_bir_lowering=False, num_devices=1)
    args = [nc.dram_tensor(k, v.shape, F32, kind="ExternalInput").ap() for k, v in arrays.items()]
    args.append(nc.dram_tensor("ple_spill", [P, 4096], F32).ap())
    args.append(nc.dram_tensor("out_x", [SEQ, D], F32, kind="ExternalOutput").ap())
    build(nc, *args)
    r = run_bass_kernel_spmd(nc, [arrays], core_ids=[0])
    return r.results[0]["out_x"].reshape(1, SEQ, D)
```

```python
from contextlib import ExitStack, contextmanager

import concourse.bass as bass
from concourse import mybir

ALU = mybir.AluOpType
ACT = mybir.ActivationFunctionType
AX = mybir.AxisListType
F32 = mybir.dt.float32
F32R = mybir.dt.float32r
I32 = mybir.dt.int32

P = 128
D = 1024
SEQ = 512
PLE = 256
FF = 4 * D
C = 512
NT = SEQ // P
KD = D // P
HD = 64
NH = 8
KV = 2
RHD = 128
RH = 4
NORM_EPS = 1e-6
GN_EPS = 1e-5
RING = 4
SLAB = 1024

S_PLE0 = 0
S_AKV = S_PLE0 + 1
S_AQ = S_AKV + 2
S_PLE1 = S_AQ + 4
S_RET = S_PLE1 + 1
S_GATE = S_RET + 16
S_AO = S_GATE + 16
S_RO = S_AO + 4
S_OUT = S_RO + 4
S_UP0 = S_OUT + 8
S_MLP = S_UP0 + 4
S_DOWN7 = S_MLP + 7 * 8
S_PG = S_DOWN7 + 4
SLABS = S_PG + 8
NF = FF // C

T_ID = 0
T_CA = T_ID + P
T_SA = T_CA + NT * HD // 2
T_CR = T_SA + NT * HD // 2
T_SR = T_CR + NT * RHD // 2
T_END = T_SR + NT * RHD // 2
PIECES = ((0, 0, 0, C), (1, 1, 0, C), (2, 2, 0, C), (3, 3, 0, C // 2), (3, 4, C // 2, C))
WARM_UP = 10
DELTA = SEQ + (NT - 1) * P


class Mark:

    def __init__(self, sem):
        self.sem, self.base, self.local = sem, 0, 0

    @property
    def value(self):
        return self.base + self.local

    def up(self):
        self.local += 1
        return self.value


@contextmanager
def counted(engine, count, marks):
    start = {m: m.value for m in marks}
    with engine.Fori(0, count) as i:
        for m, per in marks.items():
            m.base, m.local = i * per + start[m], 0
        yield i
        for m, per in marks.items():
            assert m.local == per, (m.sem, m.local, per)
    for m, per in marks.items():
        m.base, m.local = start[m] + count * per, 0


def build(nc, slabs, x_in, p_in, tables, delta_in, norms, q_gain, k_gain, ret_gain, fin_gain,
          decay, ple_spill, out):
    ctx = ExitStack()
    with ctx:
        sem = lambda name: ctx.enter_context(nc.semaphore(name))
        sb = lambda n, w, dt=F32: ctx.enter_context(nc.sbuf_tensor(n, [P, w], dt))

        ops = sb("ops", 24576, F32R)
        fp = sb("fp", 4096 + 8192 + 8192 + 2048 + 2048 + 896)
        tab = sb("tab", T_END)
        gains = sb("gains", 24 + HD + HD + RH * RHD + 2 * RH)
        rope_tmp = sb("rope_tmp", 512)
        mtmp = sb("mtmp", P)[:, :]
        scale_t = sb("scale_t", C)[:, :]
        small = sb("small", 256)
        ps = [ctx.enter_context(nc.psum_tensor(f"bank{b}", [P, C], F32)) for b in range(8)]

        def region(t, a, n):
            return t[:, a:a + n]

        w_hi = region(ops, 0, 4096).rearrange("p (s n) -> p s n", s=RING)
        w_lo = region(ops, 4096, 4096).rearrange("p (s n) -> p s n", s=RING)
        R1, R2 = 8192, 16384
        r1_hi = region(ops, R1, 4096).rearrange("p (k n) -> p k n", n=C)
        r1_lo = region(ops, R1 + 4096, 4096).rearrange("p (k n) -> p k n", n=C)
        xt_hi = region(ops, R2, 4096).rearrange("p (k n) -> p k n", n=C)
        xt_lo = region(ops, R2 + 4096, 4096).rearrange("p (k n) -> p k n", n=C)
        pt_hi = region(ops, R2 + 4096, 1024).rearrange("p (k n) -> p k n", n=C)
        pt_lo = region(ops, R2 + 5120, 1024).rearrange("p (k n) -> p k n", n=C)
        q_st = region(ops, R2, 1024).rearrange("p (h n) -> p h n", h=2)
        k_st = region(ops, R2 + 1024, 2048).rearrange("p (g s n) -> p g s n", g=KV, s=2)
        v_st = region(ops, R2 + 3072, 1024).rearrange("p (g t n) -> p g t n", g=KV, t=NT)
        prt_hi = region(ops, R2 + 4096, 2048).rearrange("p (k n) -> p k n", n=C)
        prt_lo = region(ops, R2 + 6144, 2048).rearrange("p (k n) -> p k n", n=C)
        rq_t = region(ops, R2, 1024).rearrange("p (s n) -> p s n", s=2)
        rk_t = region(ops, R2 + 1024, 1024).rearrange("p (s n) -> p s n", s=2)
        rv_st = region(ops, R2 + 2048, 1024).rearrange("p (t n) -> p t n", t=NT)
        at_hi, at_lo = prt_hi, prt_lo
        ry_hi = region(ops, R2, 2048).rearrange("p (k n) -> p k n", n=C)
        ry_lo = region(ops, R2 + 2048, 2048).rearrange("p (k n) -> p k n", n=C)

        f32 = lambda ap: ap.bitcast(F32)

        raw = region(fp, 0, 4096).rearrange("p (s n) -> p s n", s=RING)
        RR, GG = 4096, 12288
        ret = region(fp, RR, 8192).rearrange("p (c t n) -> p c t n", c=4, t=NT)
        x0 = region(fp, RR, 4096).rearrange("p (t n) -> p t n", t=NT)
        ple_w = region(fp, RR + 4096, 4096).rearrange("p (t n) -> p t n", t=NT)
        merged = region(fp, RR, 4096).rearrange("p (m n) -> p m n", n=C)
        xs = region(fp, RR + 4096, 4096).rearrange("p (t n) -> p t n", t=NT)
        ple_r = region(fp, RR, 4096).rearrange("p (t n) -> p t n", t=NT)
        gate = region(fp, GG, 8192).rearrange("p (m n) -> p m n", n=C)
        q_raw = region(fp, GG, 2048).rearrange("p (t n) -> p t n", t=NT)
        k_raw = region(fp, GG + 2048, 512).rearrange("p (t n) -> p t n", t=NT)
        p_sb = region(fp, GG + 4096, 1024).rearrange("p (t n) -> p t n", t=NT)
        squares = region(fp, GG + 5120, 1024)
        otmp_a = squares[:, 0:C]
        q_sq = region(fp, GG + 6144, 512).rearrange("p (t n) -> p t n", t=NT)
        q_rot = region(fp, GG + 6656, 512).rearrange("p (t n) -> p t n", t=NT)
        k_rot = region(fp, GG + 7168, 512).rearrange("p (t n) -> p t n", t=NT)
        stage = region(fp, GG, 2048).rearrange("p (m n) -> p m n", n=C)
        fin_g = region(fp, GG + 2048, 1024)
        squares2 = region(fp, GG + 3072, 1024)
        out_sb = region(fp, 0, 4096).rearrange("p (t n) -> p t n", t=NT)
        sig = region(fp, GG + 4096, 4096).rearrange("p (t n) -> p t n", t=NT)
        PP = GG + 8192
        prob = region(fp, PP, 2048).rearrange("p (t n) -> p t n", t=NT)
        sc_f = region(fp, PP, 1024).rearrange("p (b n) -> p b n", b=2)
        r_rot = region(fp, PP, 1024).rearrange("p (c t n) -> p c t n", c=2, t=NT)
        delta = region(fp, PP + 1024, DELTA)
        ot = region(fp, PP + 2048, 2048).rearrange("p (k n) -> p k n", n=C)
        mask = region(fp, PP + 4096, DELTA)
        ident = tab[:, T_ID:T_ID + P]
        cos_a = tab[:, T_CA:T_SA].rearrange("p (t d) -> p t d", t=NT)
        sin_a = tab[:, T_SA:T_CR].rearrange("p (t d) -> p t d", t=NT)
        cos_r = tab[:, T_CR:T_SR].rearrange("p (t d) -> p t d", t=NT)
        sin_r = tab[:, T_SR:T_END].rearrange("p (t d) -> p t d", t=NT)
        mix_g, mlp_g, ple_g = gains[:, 0:8], gains[:, 8:16], gains[:, 16:24]
        qg = gains[:, 24:88]
        kg = gains[:, 88:152]
        rg_g = gains[:, 152:664]
        dec = gains[:, 664:672]
        ss = small[:, 0:4]
        rstd = small[:, 4:8]
        inv_ms = small[:, 8:12]
        hss = small[:, 12:20]
        hr = small[:, 20:28]
        nwt = small[:, 28:44]
        mx = small[:, 44:48]
        nb = small[:, 48:52]
        den = small[:, 52:56]
        rden = small[:, 56:60]
        lg = small[:, 60:68]
        lt = small[:, 68:116].rearrange("p (a n) -> p a n", n=8)
        bst = small[:, 116:140].rearrange("p (t n) -> p t n", t=NT)
        mv = small[:, 140:148].rearrange("p (t n) -> p t n", t=NT)
        rvar = small[:, 148:152]
        zero = small[:, 152:153]
        warm_out = small[:, 166:167]
        row_r = small[:, 153:157]
        ss2 = small[:, 157:166]
        otmp = rope_tmp[:, :]

        s_slab = [sem(f"slab_landed{n}") for n in range(RING)]
        s_hi = sem("slab_hi_made")
        s_lo = sem("slab_lo_made")
        s_slab0a = sem("slab0_first_half_landed")
        s_hi0a = sem("slab0_first_half_hi_made")
        s_lo0a = sem("slab0_first_half_lo_made")
        s_used = sem("slab_used")
        s_fill = [sem(f"bank{b}_filled") for b in range(8)]
        s_drain = [sem(f"bank{b}_drained") for b in range(8)]
        s_ahi = sem("operand_hi_made")
        s_p = [sem(f"p_half{k}_landed") for k in range(2)]
        s_x = [sem(f"x_landed{t}") for t in range(NT)]
        s_tab = sem("tables_landed")
        s_dlt = sem("delta_landed")
        s_xr = sem("residual_landed")
        s_spill = sem("ple_spilled")
        s_pler = sem("ple_reloaded")
        s_fin = sem("final_gain_landed")
        s_out = sem("out_stored")
        s_ss = sem("squares_summed")
        s_rr = sem("row_rms_ready")
        s_gr = sem("gates_scaled")
        s_id = sem("identity_landed")
        s_norms = sem("norm_gains_landed")
        s_warm = sem("warm_up_input")
        s_rope = sem("roped")
        s_shift = sem("row_max_ready")
        s_prob = sem("probs_ready")
        s_otmp = sem("lo_half_copied")
        s_vst = sem("v_split")
        s_sct = sem("scores_split")
        s_mexp = sem("mask_exponent")
        s_mask = sem("mask_ready")
        s_dexp = sem("decay_exponent")
        s_du = sem("decay_exp_done")
        s_osp = sem("attention_out_split")
        s_rgs = sem("ret_gate_sigmoid")
        s_gs = sem("gate_sigmoid")
        s_ry = sem("ret_out_ready")
        s_mg = sem("merged_summed")
        s_mgs = sem("merged_split")
        s_xf = sem("x_final")
        s_hid = sem("hidden_squared")
        s_hids = sem("hidden_split")
        s_rs = sem("row_scale_ready")
        s_fo = sem("final_ready")
        s_foa = sem("final_low_columns_ready")
        s_xg = sem("final_gain_applied")
        s_fg = sem("final_gain_scaled")
        s_rf = sem("final_rms_ready")
        s_dve = sem("dve_steps")
        s_kcopy = sem("k_copied")

        LOW = [0, 1, 2, 3]
        HIGH = [4, 5, 6, 7]

        block = ctx.enter_context(nc.Block())

        @block.sync
        def _(sp):
            pv = p_in.rearrange("(t p) n -> p t n", p=P)
            sp.dma_start(p_sb[:, :, 0:P], pv[:, :, 0:P]).then_inc(s_p[0], 16)
            sp.dma_start(raw[:, 0, 0:C], slabs[0][:, 0:C]).then_inc(s_slab0a, 16)
            sp.dma_start(p_sb[:, :, P:2 * P], pv[:, :, P:2 * P]).then_inc(s_p[1], 16)
            sp.dma_start(raw[:, 0, C:2 * C], slabs[0][:, C:2 * C]).then_inc(s_slab[0], 16)
            for t in range(NT):
                if t == NT - 1:
                    sp.dma_start(raw[:, 1, :], slabs[1]).then_inc(s_slab[1], 16)
                sp.dma_start(x0[:, t, :], x_in[t * P:(t + 1) * P, :]).then_inc(s_x[t], 16)
            for n in range(2, RING):
                sp.dma_start(raw[:, n, :], slabs[n]).then_inc(s_slab[n], 16)
            sp.dma_start(dec, decay.partition_broadcast(P)).then_inc(s_tab, 16)
            sp.dma_start(tab[:, T_CA:T_END], tables[:, T_CA:T_END]).then_inc(s_tab, 16)
            sp.dma_start(kg, k_gain.partition_broadcast(P)).then_inc(s_tab, 16)
            sp.dma_start(qg, q_gain.partition_broadcast(P)).then_inc(s_tab, 16)
            sp.dma_start(rg_g, ret_gain.partition_broadcast(P)).then_inc(s_tab, 16)
            with sp.Fori(1, SLABS // RING) as i:
                for n in range(RING):
                    sp.wait_ge(s_lo, (i - 1) * RING + n + 1)
                    sp.dma_start(raw[:, n, :], slabs[bass.ds(i * RING + n, 1)].rearrange("a p n -> (a p) n"))\
                      .then_inc(s_slab[n], 16)
            for t in range(NT):
                sp.wait_ge(s_foa, t + 1)
                sp.wait_ge(s_fo, t + 1)
                sp.dma_start(out[t * P:(t + 1) * P, :], out_sb[:, t, :]).then_inc(s_out, 16)
            sp.wait_ge(s_out, 16 * NT)

        @block.gpsimd
        def _(pool):
            def make_lo(s, n):
                pool.wait_ge(s_hi, s + 1)
                pool.tensor_tensor(w_lo[:, n, :], raw[:, n, :], f32(w_hi[:, n, :]), ALU.subtract).then_inc(s_lo, 1)

            pool.wait_ge(s_hi0a, 1)
            pool.tensor_tensor(w_lo[:, 0, 0:C], raw[:, 0, 0:C], f32(w_hi[:, 0, 0:C]), ALU.subtract)\
                .then_inc(s_lo0a, 1)
            pool.wait_ge(s_hi, 1)
            pool.tensor_tensor(w_lo[:, 0, C:2 * C], raw[:, 0, C:2 * C], f32(w_hi[:, 0, C:2 * C]), ALU.subtract)\
                .then_inc(s_lo, 1)
            for n in range(1, RING):
                make_lo(n, n)
            with pool.Fori(1, SLABS // RING) as i:
                for n in range(RING):
                    make_lo(i * RING + n, n)
            pool.wait_ge(s_fg, 1)
            pool.wait_ge(s_lo, SLABS)
            for t in range(NT):
                pool.wait_ge(s_xf, t + 1)
                pool.tensor_tensor(out_sb[:, t, 0:C], xs[:, t, 0:C], fin_g[:, 0:C], ALU.mult).then_inc(s_xg, 1)

        @block.tensor
        def _(pe):
            fill = [Mark(s_fill[b]) for b in range(8)]

            def begin(b):
                n = fill[b].up()
                if not (isinstance(n, int) and n == 1):
                    pe.wait_ge(s_drain[b], n - 1)

            def slab_start(s):
                pe.wait_ge(s_lo, s + 1)
                return not (isinstance(s, int) and s == 0)

            def three(bank, a_hi, a_lo, b_hi, b_lo, first, last, used, done):
                m = pe.matmul(bank, a_hi, b_hi, start=first, stop=False)
                if used:
                    m.then_inc(s_used, 1)
                pe.matmul(bank, a_hi, b_lo, start=False, stop=False)
                m = pe.matmul(bank, a_lo, b_hi, start=False, stop=last)
                if done is not None:
                    m.then_inc(s_fill[done], 1)

            def tile(s, j, kk, banks, x_hi, x_lo, k, k_end, tokens, n=C, wait=None):
                used = slab_start(s) if (kk == 0 if wait is None else wait) else False
                cols = slice(kk * n, (kk + 1) * n)
                first, last = k == 0, k == k_end - 1
                for m, b in enumerate(banks):
                    if first:
                        begin(b)
                    wc = slice(kk * n + m * P, kk * n + (m + 1) * P)
                    xc = slice(m * P, (m + 1) * P)
                    done = b if last else None
                    if tokens:
                        three(ps[b][:, 0:n], x_hi[:, k, xc], x_lo[:, k, xc], w_hi[:, j, cols], w_lo[:, j, cols],
                              first, last, used and m == 0, done)
                    else:
                        three(ps[b][:, :], w_hi[:, j, wc], w_lo[:, j, wc], x_hi[:, k, :], x_lo[:, k, :],
                              first, last, used and m == 0, done)

            def slab(s, j, banks, x_hi, x_lo, k0, k_end, tokens, n=C):
                for kk in range(SLAB // n):
                    tile(s, j, kk, banks, x_hi, x_lo, k0 + kk, k_end, tokens, n)

            def turn(b, src):
                begin(b)
                for n in range(4):
                    m = pe.transpose(ps[b][:, n * P:(n + 1) * P], src(n), ident)
                m.then_inc(s_fill[b], 1)

            def turn_x(src, k0, banks):
                for n, b in enumerate(banks):
                    turn(b, lambda t, k=k0 + n: src[:, t, k * P:(k + 1) * P])

            pe.wait_ge(s_warm, 1)
            for _ in range(WARM_UP):
                pe.matmul(ps[7][:, 0:P], mtmp, mtmp, start=True, stop=True)

            pe.wait_ge(s_id, 16)
            for k in range(2):
                pe.wait_ge(s_p[k], 16)
                turn_x(p_sb, k, [HIGH[k]])
            for k in range(2):
                pe.wait_ge(s_drain[HIGH[k]], 1)
                if k == 0:
                    pe.wait_ge(s_lo0a, 1)
                tile(S_PLE0, 0, k, LOW, pt_hi, pt_lo, k, 2, True, wait=k == 1)

            for t in range(NT):
                pe.wait_ge(s_x[t], 16)
            turn_x(x0, 0, HIGH)
            for k in range(KD):
                b = HIGH[k % 4]
                pe.wait_ge(s_drain[b], fill[b].value)
                if k < 4:
                    turn_x(x0, 4 + k, [b])
                tile(S_AKV + k // 4, (S_AKV + k // 4) % RING, k % 4, LOW, r1_hi, r1_lo, k, KD, True, n=2 * KV * HD)
            for j in range(4):
                if j == 3:
                    begin(2)
                    for t in range(NT):
                        m = pe.matmul(ps[2][:, t * P:(t + 1) * P], row_r[:, t:t + 1].to_broadcast([P, P]), ident,
                                      start=True, stop=True)
                    m.then_inc(s_fill[2], 1)
                    pe.wait_ge(s_rope, 1)
                    turn(3, lambda t: k_rot[:, t, :])
                slab(S_AQ + j, (S_AQ + j) % RING, HIGH, r1_hi, r1_lo, 2 * j, KD, True)
            slab(S_PLE1, S_PLE1 % RING, LOW, pt_hi, pt_lo, 0, 2, True)

            prob_m = Mark(s_prob)

            def scores(e, g):
                for qt in range(NT):
                    b = HIGH[qt]
                    begin(b)
                    lhs = q_st[:, e, qt * P:(qt + 1) * P]
                    pe.matmul(ps[b][:, :], lhs, k_st[:, g, 0, :], start=True, stop=False)
                    pe.matmul(ps[b][:, :], lhs, k_st[:, g, 1, :], start=False, stop=True).then_inc(s_fill[b], 1)

            def turn_probs():
                for kt in range(NT):
                    b = HIGH[kt]
                    begin(b)
                    for qt in range(NT):
                        if kt == 0:
                            pe.wait_ge(s_prob, prob_m.up())
                        m = pe.transpose(ps[b][:, qt * P:(qt + 1) * P], prob[:, qt, kt * P:(kt + 1) * P], ident)
                    m.then_inc(s_fill[b], 1)

            def values(g):
                ready = [fill[HIGH[kt]].value for kt in range(NT)]
                begin(7)
                for kt in range(NT):
                    if kt < 3:
                        pe.wait_ge(s_drain[HIGH[kt]], ready[kt])
                    pe.matmul(ps[7][:, :], v_st[:, g, kt, :], prt_hi[:, kt, :], start=(kt == 0), stop=False)
                    m = pe.matmul(ps[7][:, :], v_st[:, g, kt, :], prt_lo[:, kt, :], start=False, stop=(kt == 3))
                m.then_inc(s_fill[7], 1)

            rope_m = Mark(s_rope)
            rope_m.local = 1

            def attention(s0, pair, g):
                def half(n):
                    j = n // 2
                    tile(s0 + j, j, n % 2, LOW, r1_hi, r1_lo, n, KD, True)
                half(0)
                pe.wait_ge(s_rope, rope_m.up())
                turn(4, lambda t: q_rot[:, t, :])
                q_ready = fill[4].value
                half(1)
                pe.wait_ge(s_drain[4], q_ready)
                scores(0, g)
                half(2)
                half(3)
                turn_probs()
                half(4)
                values(g)
                scores(1, g)
                half(5)
                half(6)
                turn_probs()
                half(7)
                values(g)

            at_marks = {fill[0]: 1, fill[1]: 1, fill[2]: 1, fill[3]: 1, fill[4]: 5, fill[5]: 4, fill[6]: 4,
                        fill[7]: 6, prob_m: 8, rope_m: 1}
            for g in range(KV):
                with counted(pe, 2, at_marks) as i:
                    attention(S_RET + 8 * g + i * 4, 2 * g + i, g)

            vst_m, sct_m = Mark(s_vst), Mark(s_sct)
            rr_m = Mark(s_rope)
            rr_m.local = rope_m.value
            re_marks = {fill[0]: 1, fill[1]: 1, fill[2]: 1, fill[3]: 1, fill[4]: 2, fill[5]: 2, fill[6]: 2,
                        fill[7]: 2, vst_m: 1, sct_m: 4, rr_m: 2}
            with counted(pe, RH, re_marks) as u:
                s0 = S_GATE + u * 4

                def half(n):
                    tile(s0 + n // 2, n // 2, n % 2, LOW, r1_hi, r1_lo, n, KD, False)
                half(0)
                half(1)
                half(2)
                for b, c in ((4, 0), (5, 1)):
                    pe.wait_ge(s_rope, rr_m.up())
                    turn(b, lambda t, c=c: r_rot[:, c, t, :])
                ready = [fill[4].value, fill[5].value]
                half(3)
                pe.wait_ge(s_drain[4], ready[0])
                pe.wait_ge(s_drain[5], ready[1])
                for jt, b in enumerate((6, 7, 4, 5)):
                    begin(b)
                    kc = slice(jt * P, (jt + 1) * P)
                    three(ps[b][:, :], rk_t[:, 0, kc], rk_t[:, 1, kc], rq_t[:, 0, :], rq_t[:, 1, :],
                          True, True, False, b)
                half(4)
                half(5)
                pe.wait_ge(s_vst, vst_m.up())
                for b in (6, 7):
                    begin(b)
                    for e in range(2):
                        it = 2 * (b - 6) + e
                        for jt in range(NT):
                            if it == 0:
                                pe.wait_ge(s_sct, sct_m.up())
                            ic = slice(it * P, (it + 1) * P)
                            o = ps[b][:, e * 256:(e + 1) * 256]
                            pe.matmul(o, prt_hi[:, jt, ic], rv_st[:, jt, :], start=(jt == 0), stop=False)
                            m = pe.matmul(o, prt_lo[:, jt, ic], rv_st[:, jt, :], start=False, stop=(jt == 3))
                    m.then_inc(s_fill[b], 1)
                half(6)
                half(7)

            def project(s, banks, x_hi, x_lo, k_end, tokens, ready=None):
                for j in range(k_end // 2):
                    if ready:
                        ready(2 * j)
                    slab(s + j, (s + j) % RING, banks, x_hi, x_lo, 2 * j, k_end, tokens)

            project(S_AO, LOW, at_hi, at_lo, 4, False, lambda k: pe.wait_ge(s_osp, k + 2))
            project(S_AO + 2, HIGH, at_hi, at_lo, 4, False)
            pe.wait_ge(s_ry, NT)
            for k in range(4):
                turn(LOW[k], lambda t, k=k: ret[:, 0, t, k * P:(k + 1) * P])
            for k in range(4):
                pe.wait_ge(s_drain[LOW[k]], fill[LOW[k]].value)
                tile(S_RO + k // 2, (S_RO + k // 2) % RING, k % 2, HIGH, ry_hi, ry_lo, k, 4, False)
            project(S_RO + 2, LOW, ry_hi, ry_lo, 4, False)

            project(S_OUT, HIGH, r1_hi, r1_lo, KD, True, lambda k: pe.wait_ge(s_mgs, k + 2))

            def chunk_and_turn(s, x_hi, x_lo, k_end):
                for j in range(k_end // 2):
                    if j == k_end // 2 - 1:
                        for b in HIGH:
                            pe.wait_ge(s_drain[b], fill[b].value)
                        turn_x(xs, 0, HIGH)
                    slab(s + j, (s + j) % RING, LOW, x_hi, x_lo, 2 * j, k_end, True)

            def chunk_from_turns(s, tokens):
                for j in range(4):
                    for n in (2 * j, 2 * j + 1):
                        if n == 2:
                            for b in LOW:
                                pe.wait_ge(s_drain[b], fill[b].value)
                            turn_x(xs, 4, LOW)
                        if n == 0:
                            for b in HIGH:
                                pe.wait_ge(s_drain[b], fill[b].value)
                        if n >= 4:
                            pe.wait_ge(s_drain[LOW[n - 4]], fill[LOW[n - 4]].value)
                        tile(s + j, j, n % 2, HIGH, xt_hi, xt_lo, n, KD, tokens)

            chunk_and_turn(S_OUT + 4, r1_hi, r1_lo, KD)
            chunk_from_turns(S_UP0, False)

            hid_m = Mark(s_hids)

            def down(s, slot, banks, first, h_hi=r1_hi, h_lo=r1_lo):
                for j in range(2):
                    if first:
                        for _ in range(2):
                            hid_m.up()
                        pe.wait_ge(s_hids, hid_m.value)
                    slab(s + j, slot + j, banks, h_hi, h_lo, 2 * j, 4, True)

            mlp_marks = {hid_m: 4}
            for b in LOW:
                mlp_marks[fill[b]] = 2
            for b in HIGH:
                mlp_marks[fill[b]] = 1
            with counted(pe, NF - 1, mlp_marks) as f:
                s0 = S_MLP + f * 8
                for j in range(4):
                    slab(s0 + j, j, LOW, xt_hi, xt_lo, 2 * j, KD, False)
                down(s0 + 4, 0, HIGH, True)
                down(s0 + 6, 2, LOW, False)
            down(S_DOWN7, 0, HIGH, True, xt_hi[:, 4:8, :], xt_lo[:, 4:8, :])
            chunk_and_turn(S_DOWN7 + 2, xt_hi[:, 4:8, :], xt_lo[:, 4:8, :], 4)

            chunk_from_turns(S_PG, True)
            for n, (t, b, c0, c1) in enumerate(PIECES):
                begin(b)
                for k in range(KD):
                    j = k // 2
                    used = slab_start(S_PG + 4 + j) if n == 0 and k % 2 == 0 else False
                    cols = slice(k % 2 * C + c0, k % 2 * C + c1)
                    tc = slice(t * P, (t + 1) * P)
                    three(ps[b][:, 0:c1 - c0], xt_hi[:, k, tc], xt_lo[:, k, tc], w_hi[:, j, cols], w_lo[:, j, cols],
                          k == 0, k == KD - 1, used, b if k == KD - 1 else None)

        @block.scalar
        def _(act):
            fill = [Mark(s_fill[b]) for b in range(8)]
            ahi = Mark(s_ahi)

            def ahead(s, slot):
                s3, n = s + 3, (slot + 3) % RING
                turn_of = s3 // RING + 1 if isinstance(s3, int) else None
                act.wait_ge(s_slab[n], 16 * turn_of)
                if not (isinstance(s, int) and s < 1):
                    act.wait_ge(s_used, s)
                act.activation(w_hi[:, n, :], raw[:, n, :], ACT.Copy).then_inc(s_hi, 1)

            def ahead_in(base, i, per, j, slot):
                n = (slot + 3) % RING
                q = (base + j + 3) // RING + 1
                act.wait_ge(s_slab[n], (i * (per // RING) + q) * 16)
                act.wait_ge(s_used, i * per + (base + j))
                act.activation(w_hi[:, n, :], raw[:, n, :], ACT.Copy).then_inc(s_hi, 1)

            def filled(b):
                act.wait_ge(s_fill[b], fill[b].up())

            def skip(b):
                fill[b].up()

            def hi(dst, src, scale=1.0):
                ahi.up()
                return act.activation(dst, src, ACT.Copy, scale=scale).then_inc(s_ahi, 1)

            def drained(b, ins):
                ins.then_inc(s_drain[b], 1)

            act.dma_start(ident, tables[:, T_ID:T_ID + P]).then_inc(s_id, 16)
            act.dma_start(gains[:, 0:24], norms).then_inc(s_norms, 16)
            act.wait_ge(s_warm, 2)
            act.activation(warm_out, zero, ACT.Copy)

            def first_hi(n):
                act.wait_ge(s_slab[n], 16)
                act.activation(w_hi[:, n, :], raw[:, n, :], ACT.Copy).then_inc(s_hi, 1)

            def x_squares(t):
                act.wait_ge(s_x[t], 16)
                if t:
                    act.wait_ge(s_ss, t)
                act.activation(squares, x0[:, t, :], ACT.Square, accum_out=ss[:, t:t + 1]).then_inc(s_ss, 1)

            def turned_hi(k):
                filled(HIGH[k % 4])
                hi(r1_hi[:, k, :], ps[HIGH[k % 4]][:, :], scale=mix_g[:, k:k + 1])

            act.wait_ge(s_slab0a, 16)
            act.activation(w_hi[:, 0, 0:C], raw[:, 0, 0:C], ACT.Copy).then_inc(s_hi0a, 1)
            act.wait_ge(s_slab[0], 16)
            act.activation(w_hi[:, 0, C:2 * C], raw[:, 0, C:2 * C], ACT.Copy).then_inc(s_hi, 1)
            for k in range(2):
                filled(HIGH[k])
                hi(pt_hi[:, k, :], ps[HIGH[k]][:, :])
            for t in range(NT - 1):
                x_squares(t)
            act.wait_ge(s_norms, 16)
            first_hi(1)
            for t in range(NT):
                filled(t)
                if t % 2 == 0:
                    drained(t, act.copy(ple_w[:, t, 0:C], ps[t][:, :]))
            for k in range(4):
                turned_hi(k)
            first_hi(2)
            for k in range(4, KD):
                turned_hi(k)
            x_squares(NT - 1)
            ahead(0, 0)
            act.wait_ge(s_dexp, 1)
            act.activation(lt[:, 1, :], lt[:, 0, :], ACT.Exp).then_inc(s_du, 1)
            for j in range(2):
                ahead(S_AKV + j, (S_AKV + j) % RING)
            act.wait_ge(s_rr, 1)
            for t in range(NT):
                filled(t)
                act.activation(k_raw[:, t, :], ps[t][:, 0:P], ACT.Copy, scale=row_r[:, t:t + 1]).then_inc(s_kcopy, 1)
                hi(v_st[:, :, t, 0:HD], ps[t][:, P:2 * P].rearrange("p (g d) -> p g d", g=KV), scale=row_r[:, t:t + 1])
            for j in range(3):
                ahead(S_AQ + j, (S_AQ + j) % RING)
            filled(2)
            drained(2, act.copy(scale_t, ps[2][:, :]))
            filled(3)
            hi(k_st[0:HD, 0, 0, :], ps[3][0:HD, :])
            hi(k_st[HD:P, 1, 0, :], ps[3][HD:P, :])
            act.copy(k_st[HD:P, 0, 0, :], ps[3][0:HD, :]).then_inc(s_kcopy, 1)
            act.copy(k_st[0:HD, 1, 0, :], ps[3][HD:P, :]).then_inc(s_kcopy, 1)
            ahead(S_AQ + 3, (S_AQ + 3) % RING)
            for t in range(NT):
                b = HIGH[t]
                filled(b)
                if t != 2:
                    drained(b, act.activation(q_raw[:, t, :], ps[b][:, :], ACT.Copy, scale=row_r[:, t:t + 1]))
            ahead(S_PLE1, S_PLE1 % RING)
            for t in range(NT):
                filled(t)
                drained(t, act.copy(ple_w[:, t, C:2 * C], ps[t][:, :]))
            for t in range(NT):
                act.wait_ge(s_drain[t], fill[t].value)
            act.dma_start(ple_spill, region(fp, RR + 4096, 4096)).then_inc(s_spill, 16)

            shift_m = Mark(s_shift)

            def soft():
                for qt in range(NT):
                    b = HIGH[qt]
                    filled(b)
                    act.wait_ge(s_shift, shift_m.up())
                    drained(b, act.activation(prob[:, qt, :], ps[b][:, :], ACT.Exp, bias=nb[:, qt:qt + 1],
                                              scale=HD ** -0.5, accum_out=den[:, qt:qt + 1]))

            def split_probs():
                for kt in range(NT):
                    filled(HIGH[kt])
                    hi(prt_hi[:, kt, :], ps[HIGH[kt]][:, :])

            def low_half():
                filled(7)
                act.copy(otmp_a[0:HD, :], ps[7][HD:P, :]).then_inc(s_otmp, 1)

            def drain_ret(c):
                for t in range(NT):
                    filled(t)
                    if t % 2 == 0:
                        drained(t, act.activation(ret[:, bass.ds(c, 1), t, :].rearrange("p a n -> p (a n)"),
                                                  ps[t][:, :], ACT.Copy, scale=row_r[:, t:t + 1]))

            at_marks = {fill[0]: 1, fill[1]: 1, fill[2]: 1, fill[3]: 1, fill[4]: 5, fill[5]: 4, fill[6]: 4,
                        fill[7]: 6, ahi: 10, shift_m: 8}
            for g in range(KV):
                if g:
                    act.wait_ge(s_spill, 16)
                with counted(act, 2, at_marks) as i:
                    base = S_RET + 8 * g
                    filled(4)
                    hi(q_st[0:HD, 0, :], ps[4][0:HD, :])
                    hi(q_st[HD:P, 1, :], ps[4][HD:P, :])
                    ahead_in(base, i, 4, 0, 0)
                    soft()
                    ahead_in(base, i, 4, 1, 1)
                    split_probs()
                    low_half()
                    ahead_in(base, i, 4, 2, 2)
                    soft()
                    ahead_in(base, i, 4, 3, 3)
                    split_probs()
                    drain_ret(2 * g + i)
                    low_half()

            act.dma_start(delta, delta_in).then_inc(s_dlt, 16)
            mexp_m = Mark(s_mexp)
            re_marks = {fill[0]: 1, fill[1]: 1, fill[2]: 1, fill[3]: 1, fill[4]: 2, fill[5]: 2, fill[6]: 2,
                        fill[7]: 2, ahi: 7, mexp_m: 1}

            def ret_head(u, i=None):
                def ahead_of(j):
                    if i is None:
                        ahead(S_GATE + j, j)
                    else:
                        ahead_in(S_GATE + 4, i, 4, j, j)
                ahead_of(0)
                hi(rv_st[:, :, 0:P], ret[:, 2, :, bass.ds(u * P, P)])
                act.wait_ge(s_mexp, mexp_m.up())
                diag = (NT - 1) * P
                act.activation(mask[:, 0:diag], delta[:, 0:diag], ACT.Exp, scale=lg[:, bass.ds(u + RH, 1)])
                act.activation(mask[:, diag + P:DELTA], delta[:, diag + P:DELTA], ACT.Exp, scale=lg[:, bass.ds(u, 1)])
                act.activation(mask[:, diag:diag + P], mask[:, diag:diag + P], ACT.Exp).then_inc(s_mask, 1)
                ahead_of(1)
                for b, dst in ((4, rq_t), (5, rk_t)):
                    filled(b)
                    hi(dst[:, 0, :], ps[b][:, :])
                for jt, b in enumerate((6, 7, 4, 5)):
                    skip(b)
                    act.wait_ge(s_drain[b], fill[b].value)
                    hi(prt_hi[:, jt, :], sc_f[:, jt % 2, :])
                ahead_of(2)
                ahead_of(3)
                for b in (6, 7):
                    filled(b)
                    act.copy(otmp[:, (b - 6) * 256:(b - 5) * 256].rearrange("p (e n) -> p e n", e=2),
                             ps[b][:, :].rearrange("p (e s n) -> p e s n", e=2, s=2)[:, :, 1, :]).then_inc(s_otmp, 1)

            def drain_gates(u):
                for m in LOW:
                    filled(m)
                    g = gate[:, u * 4 + m, :] if isinstance(u, int) else \
                        gate[:, bass.ds(u * 4 + m, 1), :].rearrange("p a n -> p (a n)")
                    drained(m, act.copy(g, ps[m][:, :]))

            ret_head(0)
            with counted(act, RH - 1, re_marks) as i:
                drain_gates(i)
                ret_head(i + 1, i)

            for k in range(4):
                hi(at_hi[:, k, :], ot[:, k, :])
            drain_gates(RH - 1)
            for t in range(NT):
                act.activation(ret[:, 1, t, :], ret[:, 3, t, :], ACT.Sigmoid).then_inc(s_rgs, 1)
            for j in range(2):
                ahead(S_AO + j, (S_AO + j) % RING)
                act.wait_ge(s_gr, j + 1)
                for m in range(4 * j, 4 * j + 4):
                    act.activation(gate[:, m, :], gate[:, m, :], ACT.Sigmoid).then_inc(s_gs, 1)
            for b in LOW + HIGH:
                skip(b)
            ahead(S_AO + 2, (S_AO + 2) % RING)
            act.wait_ge(s_gr, 4)
            for m in range(8, 12):
                act.activation(gate[:, m, :], gate[:, m, :], ACT.Sigmoid).then_inc(s_gs, 1)
            ahead(S_AO + 3, (S_AO + 3) % RING)
            for m in range(12, 16):
                act.activation(gate[:, m, :], gate[:, m, :], ACT.Sigmoid).then_inc(s_gs, 1)
            for k in range(4):
                filled(LOW[k])
                hi(ry_hi[:, k, :], ps[LOW[k]][:, :])
            act.wait_ge(s_rgs, NT)
            act.wait_ge(s_ry, NT)
            act.dma_start(xs, x_in.rearrange("(t p) n -> p t n", p=P)).then_inc(s_xr, 16)
            for j in range(4):
                ahead(S_RO + j, (S_RO + j) % RING)
                for m in ((0, 1, 2, 3) if j == 1 else (4, 5, 6, 7) if j == 3 else ()):
                    skip(HIGH[m] if j == 1 else LOW[m - 4])
                    act.wait_ge(s_mg, m + 1)
                    hi(r1_hi[:, m, :], merged[:, m, :])
            for b in HIGH:
                skip(b)
            for j in range(4):
                ahead(S_OUT + j, (S_OUT + j) % RING)
            act.wait_ge(s_mgs, 8)
            act.dma_start(region(fp, RR, 4096), ple_spill).then_inc(s_pler, 16)

            def split_turned(k0, banks, gain):
                for n, b in enumerate(banks):
                    filled(b)
                    hi(xt_hi[:, k0 + n, :], ps[b][:, :], scale=gain[:, k0 + n:k0 + n + 1])

            def row_squares(first_sum):
                for t in range(NT):
                    if t or first_sum:
                        act.wait_ge(s_ss, first_sum + t)
                    act.activation(squares2, xs[:, t, :], ACT.Square, accum_out=ss[:, t:t + 1]).then_inc(s_ss, 1)

            for j in range(4):
                if j == 3:
                    split_turned(0, HIGH, mlp_g)
                ahead(S_OUT + 4 + j, j)
            for b in LOW:
                skip(b)
            for j in range(4):
                ahead(S_UP0 + j, (S_UP0 + j) % RING)
                if j == 1:
                    split_turned(4, LOW, mlp_g)
                if j == 2:
                    row_squares(NT)

            def relus(banks):
                for m, b in enumerate(banks):
                    filled(b)
                    drained(b, act.activation(stage[:, m, :], ps[b][:, :], ACT.Relu))

            hid_m = Mark(s_hid)

            def split_hidden(dst):
                for m in range(4):
                    act.wait_ge(s_hid, hid_m.up())
                    hi(dst[:, m, :], stage[:, m, :])

            relus(HIGH)
            mlp_marks = {fill[b]: 2 for b in LOW}
            mlp_marks.update({fill[b]: 1 for b in HIGH})
            mlp_marks.update({ahi: 4, hid_m: 4})
            with counted(act, NF - 1, mlp_marks) as f:
                ahead_in(S_MLP, f, 8, 0, 0)
                act.wait_ge(s_fill[3], fill[3].value)
                split_hidden(r1_hi)
                for j in range(1, 4):
                    ahead_in(S_MLP, f, 8, j, j)
                act.wait_ge(s_hids, f * 4 + 4)
                relus(LOW)
                for j in range(4, 8):
                    ahead_in(S_MLP, f, 8, j, j % RING)
                for b in HIGH + LOW:
                    skip(b)
            split_hidden(xt_hi[:, 4:8, :])
            act.dma_start(fin_g, fin_gain.partition_broadcast(P)).then_inc(s_fin, 16)
            for j in range(4):
                if j == 3:
                    for b in HIGH:
                        skip(b)
                    split_turned(0, HIGH, ple_g)
                ahead(S_DOWN7 + j, j)
            for b in LOW:
                skip(b)
            for j in range(4):
                ahead(S_PG + j, j)
                if j == 1:
                    split_turned(4, LOW, ple_g)
                if j == 2:
                    row_squares(2 * NT)

            def gate_of(t, b, c0, c1):
                filled(b)
                drained(b, act.activation(sig[:, t, c0:c1], ps[b][:, 0:c1 - c0], ACT.Sigmoid, scale=rstd[:, t:t + 1]))

            def part_squares(n, t, c0, c1):
                act.wait_ge(s_xf, n + 1)
                act.wait_ge(s_ss, 3 * NT + n)
                act.activation(squares2[:, 0:c1 - c0], xs[:, t, c0:c1], ACT.Square, accum_out=ss2[:, n:n + 1])\
                   .then_inc(s_ss, 1)

            act.wait_ge(s_rs, 1)
            for t in range(NT):
                if t == 2:
                    ahead(S_PG + 4, 0)
                gate_of(t, HIGH[t], 0, C)
            for t in range(NT):
                part_squares(t, t, 0, C)

            def final_low(t):
                act.wait_ge(s_xg, t + 1)
                act.wait_ge(s_rf, t + 1)
                act.activation(out_sb[:, t, 0:C], out_sb[:, t, 0:C], ACT.Copy, scale=row_r[:, t:t + 1])\
                   .then_inc(s_foa, 1)

            for n, (t, b, c0, c1) in enumerate(PIECES):
                gate_of(t, b, C + c0, C + c1)
                if c0 == 0 and t:
                    final_low(t - 1)
                part_squares(NT + n, t, C + c0, C + c1)
            final_low(NT - 1)


        @block.vector
        def _(dve):
            fill = [Mark(s_fill[b]) for b in range(8)]
            ahi = Mark(s_ahi)
            steps = Mark(s_dve)
            roped = Mark(s_rope)

            def filled(b):
                dve.wait_ge(s_fill[b], fill[b].up())

            def skip(b):
                fill[b].up()

            def step(ins):
                ins.then_inc(s_dve, 1)
                steps.up()

            def settle():
                dve.wait_ge(s_dve, steps.value)

            def carry_waits():
                step(dve.memset(zero, 0.0))

            def lo(dst, src, hi_part):
                dve.wait_ge(s_ahi, ahi.up())
                return dve.tensor_tensor(dst, src, f32(hi_part), ALU.subtract)

            def rsqrt(dst, src):
                n = dst.shape[-1]
                t = nwt[:, 0:n]
                step(dve.tensor_scalar(dst.bitcast(I32), src.bitcast(I32), -0.5, 1597463007.0, ALU.mult, ALU.add))
                settle()
                for _ in range(3):
                    step(dve.tensor_tensor(t, dst, dst, ALU.mult))
                    settle()
                    step(dve.scalar_tensor_tensor(t, t, -0.5, src, ALU.mult, ALU.mult))
                    settle()
                    step(dve.scalar_tensor_tensor(dst, t, 1.5, dst, ALU.add, ALU.mult))
                    settle()

            def rope(o1, o2, x1, x2, cos, sin, shape):
                n = 1
                for v in shape[1:]:
                    n *= v
                def buf(k):
                    v = rope_tmp[:, k * n:(k + 1) * n]
                    if len(shape) == 4:
                        return v.rearrange("p (t h d) -> p t h d", t=shape[1], h=shape[2])
                    return v.rearrange("p (t d) -> p t d", t=shape[1])
                a, b = buf(0), buf(1)

                def first():
                    step(dve.tensor_tensor(a, x1, sin, ALU.mult))
                    step(dve.tensor_tensor(b, x2, sin, ALU.mult))
                    step(dve.tensor_tensor(o1, x1, cos, ALU.mult))
                    step(dve.tensor_tensor(o2, x2, cos, ALU.mult))

                def last():
                    step(dve.tensor_tensor(o1, o1, b, ALU.subtract))
                    return dve.tensor_tensor(o2, o2, a, ALU.add)
                return first, last

            def head_steps(dst, v, gain):
                half = HD // 2
                dv = dst.rearrange("p t (h d) -> p t h d", h=2)
                hv = v.rearrange("p t (h d) -> p t h d", h=2)
                c = cos_a.unsqueeze(2).to_broadcast([P, NT, 2, half])
                s = sin_a.unsqueeze(2).to_broadcast([P, NT, 2, half])

                def mean_squares():
                    dve.wait_ge(s_rope, roped.value)
                    step(dve.tensor_tensor(q_sq, v, v, ALU.mult))
                    settle()
                    step(dve.tensor_reduce(hss, q_sq.rearrange("p t (h d) -> p (t h) d", h=2), AX.X, ALU.add))
                    settle()
                    step(dve.tensor_scalar(hss, hss, 1.0 / HD, NORM_EPS, ALU.mult, ALU.add))
                    settle()

                def scale():
                    r = hr.rearrange("p (t h) -> p t h", h=2).unsqueeze(3).to_broadcast([P, NT, 2, HD])
                    step(dve.tensor_tensor(hv, hv, r, ALU.mult))
                    settle()
                    g = gain.unsqueeze(1).unsqueeze(1).to_broadcast([P, NT, 2, HD])
                    step(dve.tensor_tensor(hv, hv, g, ALU.mult))
                    settle()

                first, last = rope(dv[:, :, :, 0:half], dv[:, :, :, half:HD], hv[:, :, :, 0:half],
                                   hv[:, :, :, half:HD], c, s, [P, NT, 2, half])

                def rotate():
                    settle()
                    last().then_inc(s_rope, 1)
                    roped.up()
                return mean_squares, lambda: rsqrt(hr, hss), scale, first, rotate

            dve.memset(mtmp, 0.0).then_inc(s_warm, 1)
            dve.memset(zero, 0.0).then_inc(s_warm, 1)
            for k, b in ((0, 4), (1, 5)):
                filled(b)
                lo(pt_lo[:, k, :], ps[b][:, :], pt_hi[:, k, :]).then_inc(s_drain[b], 1)
            def split_turned(dst_lo, dst_hi, k0, banks, gain):
                for n, b in enumerate(banks):
                    filled(b)
                    dve.wait_ge(s_ahi, ahi.up())
                    dve.scalar_tensor_tensor(dst_lo[:, k0 + n, :], ps[b][:, :], gain[:, k0 + n:k0 + n + 1],
                                             f32(dst_hi[:, k0 + n, :]), ALU.mult, ALU.subtract)\
                       .then_inc(s_drain[b], 1)
            dve.wait_ge(s_norms, 16)
            for t in range(NT):
                filled(t)
                if t % 2:
                    dve.tensor_copy(ple_w[:, t, 0:C], ps[t][:, :]).then_inc(s_drain[t], 1)
            split_turned(r1_lo, r1_hi, 0, HIGH, mix_g)
            dve.wait_ge(s_tab, 16 * 5)
            step(dve.tensor_scalar(lt[:, 2, :], dec, -1.0, None, ALU.mult))
            settle()
            dve.tensor_tensor(lt[:, 0, :], dec, lt[:, 2, :], ALU.min).then_inc(s_dexp, 1)
            split_turned(r1_lo, r1_hi, 4, HIGH, mix_g)
            dve.wait_ge(s_ss, NT)
            step(dve.tensor_scalar(inv_ms, ss, 1.0 / D, NORM_EPS, ALU.mult, ALU.add))
            settle()
            rsqrt(row_r, inv_ms)
            dve.nop().then_inc(s_rr, 1)

            dve.wait_ge(s_du, 1)
            u_, w_, s_, q_ = lt[:, 1, :], lt[:, 2, :], lt[:, 3, :], lt[:, 4, :]
            step(dve.tensor_scalar(w_, u_, 2.0, None, ALU.add))
            settle()
            step(dve.reciprocal(w_, w_))
            settle()
            step(dve.tensor_tensor(s_, u_, w_, ALU.mult))
            settle()
            step(dve.tensor_tensor(w_, s_, s_, ALU.mult))
            settle()
            step(dve.tensor_scalar(q_, w_, 1.0 / 17, None, ALU.mult))
            settle()
            for n in (15, 13, 11, 9, 7, 5, 3):
                step(dve.scalar_tensor_tensor(q_, q_, 1.0 / n, w_, ALU.add, ALU.mult))
                settle()
            step(dve.scalar_tensor_tensor(q_, q_, 1.0, s_, ALU.add, ALU.mult))
            step(dve.tensor_scalar(w_, dec, 0.0, None, ALU.min))
            settle()
            step(dve.scalar_tensor_tensor(lg, q_, -2.0, w_, ALU.mult, ALU.add))
            settle()
            step(dve.tensor_scalar(lg[:, RH:2 * RH], lg[:, RH:2 * RH], -1.0, None, ALU.mult))

            for t in range(NT):
                filled(t)
                dve.wait_ge(s_kcopy, t + 1)
                dve.wait_ge(s_ahi, ahi.up())
                dve.scalar_tensor_tensor(v_st[:, :, t, HD:P], ps[t][:, P:2 * P].rearrange("p (g d) -> p g d", g=KV),
                                         row_r[:, t:t + 1], f32(v_st[:, :, t, 0:HD]), ALU.mult, ALU.subtract)\
                    .then_inc(s_drain[t], 1)
            for part in head_steps(k_rot, k_raw, kg):
                part()
            skip(2)
            filled(3)
            dve.wait_ge(s_kcopy, NT + 2)
            for g, rows, other in ((0, slice(0, HD), slice(HD, P)), (1, slice(HD, P), slice(0, HD))):
                dve.wait_ge(s_ahi, ahi.up())
                step(dve.tensor_tensor(k_st[rows, g, 1, :], ps[3][rows, :], f32(k_st[rows, g, 0, :]), ALU.subtract))
                ins = dve.tensor_tensor(k_st[other, g, 1, :], ps[3][rows, :], f32(k_st[rows, g, 0, :]), ALU.subtract)
                if g == 0:
                    step(ins)
            ins.then_inc(s_drain[3], 1)
            for t in range(NT):
                b = HIGH[t]
                filled(b)
                if t == 2:
                    dve.tensor_scalar(q_raw[:, t, :], ps[b][:, :], row_r[:, t:t + 1], None, ALU.mult)\
                       .then_inc(s_drain[b], 1)
            for b in HIGH:
                dve.wait_ge(s_drain[b], fill[b].value)
            parts = head_steps(q_rot, q_raw[:, :, 0:P], qg)
            for part in parts:
                part()
            for b in LOW:
                skip(b)

            otmp_m = Mark(s_otmp)

            def soft():
                n0 = []
                for qt in range(NT):
                    b = HIGH[qt]
                    filled(b)
                    step(dve.tensor_reduce(mx[:, qt:qt + 1], ps[b][:, :], AX.X, ALU.max))
                    settle()
                    dve.tensor_scalar(nb[:, qt:qt + 1], mx[:, qt:qt + 1], -(HD ** -0.5), None, ALU.mult)\
                       .then_inc(s_shift, 1)
                    n0.append(fill[b].value)
                for qt in range(NT):
                    dve.wait_ge(s_drain[HIGH[qt]], n0[qt])
                    step(dve.reciprocal(rden[:, qt:qt + 1], den[:, qt:qt + 1]))
                    settle()
                    dve.tensor_scalar(prob[:, qt, :], prob[:, qt, :], rden[:, qt:qt + 1], None, ALU.mult)\
                       .then_inc(s_prob, 1)

            def split_probs():
                for kt in range(NT):
                    b = HIGH[kt]
                    filled(b)
                    lo(prt_lo[:, kt, :], ps[b][:, :], prt_hi[:, kt, :]).then_inc(s_drain[b], 1)

            def join(pair, rows):
                filled(7)
                dve.wait_ge(s_otmp, otmp_m.up())
                dve.tensor_tensor(ot[rows, bass.ds(pair, 1), :].rearrange("p a n -> p (a n)"),
                                  ps[7][0:HD, :], otmp_a[0:HD, :], ALU.add).then_inc(s_drain[7], 1)

            def drain_ret(c):
                for t in range(NT):
                    filled(t)
                    if t % 2:
                        dve.tensor_scalar(ret[:, bass.ds(c, 1), t, :].rearrange("p a n -> p (a n)"), ps[t][:, :],
                                          row_r[:, t:t + 1], None, ALU.mult).then_inc(s_drain[t], 1)

            def rotate_head(u, c):
                half = RHD // 2
                v = ret[:, c, :, :]
                first, last = rope(r_rot[:, c, :, 0:half], r_rot[:, c, :, half:RHD], v[:, :, bass.ds(u * P, half)],
                                   v[:, :, bass.ds(u * P + half, half)], cos_r, sin_r, [P, NT, half])
                first()
                settle()
                last().then_inc(s_rope, 1)
                dve.wait_ge(s_rope, roped.up())

            def attention(g, pair, last):
                filled(4)
                dve.wait_ge(s_ahi, ahi.up())
                step(dve.tensor_tensor(q_st[HD:P, 0, :], ps[4][0:HD, :], f32(q_st[0:HD, 0, :]), ALU.subtract))
                dve.wait_ge(s_ahi, ahi.up())
                settle()
                dve.tensor_tensor(q_st[0:HD, 1, :], ps[4][HD:P, :], f32(q_st[HD:P, 1, :]), ALU.subtract)\
                   .then_inc(s_drain[4], 1)
                if last:
                    parts = [lambda: None] * 5
                else:
                    parts = head_steps(q_rot, q_raw[:, :, bass.ds((pair + 1) * P, P)], qg)
                soft()
                parts[0]()
                split_probs()
                parts[1]()
                join(pair, slice(0, HD))
                soft()
                parts[2]()
                split_probs()
                if last:
                    for b in LOW:
                        dve.wait_ge(s_drain[b], fill[b].value)
                    rotate_head(0, 0)
                drain_ret(pair)
                parts[3]()
                join(pair, slice(HD, P))
                parts[4]()

            HEADS_STEPS = 3 + 10 + 2 + 5
            at_marks = {fill[0]: 1, fill[1]: 1, fill[2]: 1, fill[3]: 1, fill[4]: 5, fill[5]: 4, fill[6]: 4,
                        fill[7]: 6, ahi: 10, otmp_m: 2, roped: 1, steps: 1 + 16 + HEADS_STEPS}
            with counted(dve, 2, at_marks) as i:
                attention(0, i, False)
            attention(1, 2, False)
            attention(1, 3, True)

            rotate_head(0, 1)
            for b in LOW:
                dve.wait_ge(s_drain[b], fill[b].value)
            dve.wait_ge(s_dlt, 16)
            mask_m = Mark(s_mask)

            def decays(u):
                diag = slice((NT - 1) * P, NT * P)
                step(dve.tensor_scalar(mask[:, diag], delta[:, diag], 0.0, lg[:, bass.ds(u, 1)], ALU.max, ALU.mult))
                step(dve.tensor_scalar(mtmp, delta[:, diag], 0.0, lg[:, bass.ds(u + RH, 1)], ALU.min, ALU.mult))
                settle()
                dve.tensor_tensor(mask[:, diag], mask[:, diag], mtmp, ALU.add).then_inc(s_mexp, 1)

            def head(u, before=None):
                hc = bass.ds(u * P, P)
                ahi.up()
                for b, dst in ((4, rq_t), (5, rk_t)):
                    filled(b)
                    lo(dst[:, 1, :], ps[b][:, :], dst[:, 0, :]).then_inc(s_drain[b], 1)
                dve.tensor_tensor(rv_st[:, :, P:2 * P], ret[:, 2, :, hc], f32(rv_st[:, :, 0:P]), ALU.subtract)\
                   .then_inc(s_vst, 1)
                dve.wait_ge(s_mask, mask_m.up())

                def finish(jt):
                    lo(prt_lo[:, jt, :], sc_f[:, jt % 2, :], prt_hi[:, jt, :]).then_inc(s_sct, 1)
                for jt, b in enumerate((6, 7, 4, 5)):
                    filled(b)
                    if jt >= 2:
                        dve.wait_ge(s_sct, u * 4 + jt - 1)
                    dve.scalar_tensor_tensor(sc_f[:, jt % 2, :], ps[b][:, :], RHD ** -0.5,
                                             mask[:, (NT - 1 - jt) * P:(NT - 1 - jt) * P + C], ALU.mult, ALU.mult)\
                       .then_inc(s_drain[b], 1)
                    if jt >= 1:
                        finish(jt - 1)
                finish(3)
                if before is not None:
                    gain_and_gate(before)
                    scale_gates(before)
                for b in (6, 7):
                    filled(b)
                    dve.wait_ge(s_otmp, otmp_m.up())
                    dve.tensor_tensor(ret[:, 0, 2 * (b - 6):2 * (b - 6) + 2, hc],
                                      ps[b][:, :].rearrange("p (e s n) -> p e s n", e=2, s=2)[:, :, 0, :],
                                      otmp[:, (b - 6) * 256:(b - 5) * 256].rearrange("p (e n) -> p e n", e=2),
                                      ALU.add).then_inc(s_drain[b], 1)
                for b in (6, 7):
                    dve.wait_ge(s_drain[b], fill[b].value)
                carry_waits()
                for m in LOW:
                    skip(m)

            def group_norm(u):
                hc = bass.ds(u * P, P)
                for t in range(NT):
                    step(dve.bn_stats(bst[:, t, :], ret[:, 0, t, hc]))
                settle()
                carry_waits()
                for t in range(NT):
                    step(dve.bn_aggr(mv[:, t, :], bst[:, t, :]))
                settle()
                step(dve.tensor_scalar(rvar, mv[:, :, 1], GN_EPS, None, ALU.add))
                settle()
                rsqrt(rstd, rvar)
                for t in range(NT):
                    step(dve.tensor_scalar(ret[:, 0, t, hc], ret[:, 0, t, hc], mv[:, t, 0:1], rstd[:, t:t + 1],
                                           ALU.subtract, ALU.mult))

            def gain_and_gate(u):
                hc = bass.ds(u * P, P)
                settle()
                gb = rg_g[:, hc].unsqueeze(1).to_broadcast([P, NT, RHD])
                step(dve.tensor_tensor(ret[:, 0, :, hc], ret[:, 0, :, hc], gb, ALU.mult))
                settle()
                step(dve.tensor_tensor(ret[:, 0, :, hc], ret[:, 0, :, hc], ret[:, 3, :, hc], ALU.mult))

            re_marks = {fill[0]: 1, fill[1]: 1, fill[2]: 1, fill[3]: 1, fill[4]: 2, fill[5]: 2, fill[6]: 2,
                        fill[7]: 2, ahi: 7, otmp_m: 2, mask_m: 1, roped: 2,
                        steps: 2 + 10 + 4 + 4 + 2 + 1 + 10 + 4 + 2}

            def scale_gates(u):
                for b in LOW:
                    dve.wait_ge(s_drain[b], fill[b].value)
                g = gate[:, bass.ds(u * 4, 4), :]
                dve.tensor_tensor(g, g, scale_t.unsqueeze(1).to_broadcast([P, 4, C]), ALU.mult).then_inc(s_gr, 1)

            decays(0)
            head(0)
            with counted(dve, RH - 1, re_marks) as i:
                dve.wait_ge(s_sct, (i + 1) * NT)
                rotate_head(i + 1, 0)
                rotate_head(i + 1, 1)
                decays(i + 1)
                group_norm(i)
                head(i + 1, i)

            for k in range(4):
                lo(at_lo[:, k, :], ot[:, k, :], at_hi[:, k, :]).then_inc(s_osp, 1)
            scale_gates(RH - 1)
            group_norm(RH - 1)
            gain_and_gate(RH - 1)
            settle()
            for t in range(NT):
                dve.wait_ge(s_rgs, t + 1)
                dve.tensor_tensor(ret[:, 0, t, :], ret[:, 0, t, :], ret[:, 1, t, :], ALU.mult).then_inc(s_ry, 1)

            def attn_branch(ms):
                for m in ms:
                    b = m
                    filled(b)
                    dve.wait_ge(s_gs, m + 1)
                    dve.tensor_tensor(gate[:, m, :], ps[b][:, :], gate[:, m, :], ALU.mult).then_inc(s_drain[b], 1)

            attn_branch(range(8))
            for k in range(4):
                filled(LOW[k])
                lo(ry_lo[:, k, :], ps[LOW[k]][:, :], ry_hi[:, k, :]).then_inc(s_drain[LOW[k]], 1)
            for b in LOW + HIGH:
                dve.wait_ge(s_drain[b], fill[b].value)

            def merge(m, b):
                filled(b)
                dve.wait_ge(s_gs, 8 + m + 1)
                dve.tensor_tensor(gate[:, 8 + m, :], ps[b][:, :], gate[:, 8 + m, :], ALU.mult)\
                   .then_inc(s_drain[b], 1)
                dve.wait_ge(s_drain[b], fill[b].value)
                dve.tensor_tensor(merged[:, m, :], gate[:, m, :], gate[:, 8 + m, :], ALU.add).then_inc(s_mg, 1)

            def merge_lo(m):
                lo(r1_lo[:, m, :], merged[:, m, :], r1_hi[:, m, :]).then_inc(s_mgs, 1)
            for m in range(8):
                merge(m, m % 4 + (4 if m < 4 else 0))
                if m:
                    merge_lo(m - 1)
            merge_lo(7)

            def add_columns(c, banks):
                for t in range(NT):
                    b = banks[t]
                    filled(b)
                    xc = xs[:, t, c * C:(c + 1) * C]
                    dve.tensor_tensor(xc, xc, ps[b][:, :], ALU.add).then_inc(s_drain[b], 1)

            dve.wait_ge(s_xr, 16)
            add_columns(0, HIGH)
            split_turned(xt_lo, xt_hi, 0, HIGH, mlp_g)
            add_columns(1, LOW)
            split_turned(xt_lo, xt_hi, 4, LOW, mlp_g)
            dve.wait_ge(s_ss, 2 * NT)
            step(dve.tensor_scalar(inv_ms, ss, 1.0 / D, NORM_EPS, ALU.mult, ALU.add))
            settle()
            step(dve.reciprocal(inv_ms, inv_ms))
            settle()

            def square(banks):
                for m, b in enumerate(banks):
                    skip(b)
                    dve.wait_ge(s_drain[b], fill[b].value)
                    dve.tensor_tensor(stage[:, m, :], stage[:, m, :], stage[:, m, :], ALU.mult).then_inc(s_hid, 1)

            def split_hidden(d_lo, d_hi):
                for m in range(4):
                    lo(d_lo[:, m, :], stage[:, m, :], d_hi[:, m, :]).then_inc(s_hids, 1)

            def add_scaled(c, banks):
                for t in range(NT):
                    b = banks[t]
                    filled(b)
                    xc = xs[:, t, c * C:(c + 1) * C]
                    dve.scalar_tensor_tensor(xc, ps[b][:, :], inv_ms[:, t:t + 1], xc, ALU.mult, ALU.add)\
                       .then_inc(s_drain[b], 1)

            square(HIGH)
            split_hidden(r1_lo, r1_hi)
            square(LOW)
            add_scaled(0, HIGH)
            mlp_marks = {fill[b]: 2 for b in LOW}
            mlp_marks.update({fill[b]: 1 for b in HIGH})
            mlp_marks.update({ahi: 4})
            with counted(dve, NF - 2, mlp_marks) as f:
                add_scaled(1, LOW)
                split_hidden(r1_lo, r1_hi)
                square(LOW)
                add_scaled(0, HIGH)
            split_hidden(xt_lo[:, 4:8, :], xt_hi[:, 4:8, :])
            add_scaled(1, LOW)
            add_scaled(0, HIGH)
            split_turned(xt_lo, xt_hi, 0, HIGH, ple_g)
            add_scaled(1, LOW)
            split_turned(xt_lo, xt_hi, 4, LOW, ple_g)
            dve.wait_ge(s_ss, 3 * NT)
            step(dve.tensor_scalar(inv_ms, ss, 1.0 / D, NORM_EPS, ALU.mult, ALU.add))
            settle()
            rsqrt(rstd, inv_ms)
            dve.nop().then_inc(s_rs, 1)
            dve.wait_ge(s_pler, 16)
            dve.wait_ge(s_fin, 16)

            step(dve.tensor_scalar(fin_g, fin_g, 9.0 / 64, None, ALU.mult))
            settle()
            dve.nop().then_inc(s_fg, 1)

            def gated(t, b, c0, c1):
                skip(b)
                dve.wait_ge(s_drain[b], fill[b].value)
                sg = sig[:, t, c0:c1]
                step(dve.tensor_tensor(sg, sg, ple_r[:, t, c0:c1], ALU.mult))

            def embed(t, c0, c1, n):
                xc = xs[:, t, c0:c1]
                dve.wait_ge(s_dve, steps.value - n)
                dve.tensor_tensor(xc, xc, sig[:, t, c0:c1], ALU.add).then_inc(s_xf, 1)

            def final_rsqrt(dst, src):
                y, h, q, src2 = nwt[:, 0:1], nwt[:, 1:2], nwt[:, 2:3], nwt[:, 3:4]
                step(dve.tensor_scalar(y.bitcast(I32), src.bitcast(I32), -0.5, 1597463007.0, ALU.mult, ALU.add))
                step(dve.tensor_scalar(src2, src, 9.0 / 64, None, ALU.mult))
                settle()
                for x, y_next in ((src, nwt[:, 4:5]), (src2, dst)):
                    step(dve.scalar_tensor_tensor(h, y, x, y, ALU.mult, ALU.mult))
                    settle()
                    step(dve.scalar_tensor_tensor(q, h, -10.0 / 3, h, ALU.add, ALU.mult))
                    settle()
                    last = dve.scalar_tensor_tensor(y_next, q, 5.0, y, ALU.add, ALU.mult)
                    if y_next is not dst:
                        step(last)
                        settle()
                    y = y_next
                return last

            for t in range(NT):
                gated(t, HIGH[t], 0, C)
                if t:
                    embed(t - 1, 0, C, 1)
            embed(NT - 1, 0, C, 0)
            dve.wait_ge(s_ss, 4 * NT)
            step(dve.tensor_scalar(inv_ms, ss2[:, 0:NT], 1.0 / D, NORM_EPS, ALU.mult, ALU.add))
            for n, (t, b, c0, c1) in enumerate(PIECES):
                gated(t, b, C + c0, C + c1)
                embed(t, C + c0, C + c1, 0)
                dve.wait_ge(s_ss, 4 * NT + n + 1)
                it = inv_ms[:, t:t + 1]
                step(dve.scalar_tensor_tensor(it, ss2[:, NT + n:NT + n + 1], 1.0 / D, it, ALU.mult, ALU.add))
                if c1 < C:
                    continue
                settle()
                final_rsqrt(row_r[:, t:t + 1], it).then_inc(s_rf, 1)
                dve.wait_ge(s_rf, t + 1)
                dve.wait_ge(s_xf, NT + n + 1)
                dve.scalar_tensor_tensor(out_sb[:, t, C:D], xs[:, t, C:D], row_r[:, t:t + 1], fin_g[:, C:D],
                                         ALU.mult, ALU.mult).then_inc(s_fo, 1)


def shape_tables():
    import numpy as np

    def rope(head_dim):
        n = head_dim // 4
        freqs = np.float32(10000.0) ** (-np.arange(n, dtype=np.float32) / np.float32(n))
        pos = np.arange(SEQ)
        row, col = (pos // 64).astype(np.float32), (pos % 64).astype(np.float32)
        ang = np.concatenate([row[:, None] * freqs, col[:, None] * freqs], axis=-1).astype(np.float32)
        tiles = lambda a: a.reshape(NT, P, -1).transpose(1, 0, 2).reshape(P, -1)
        return tiles(np.cos(ang)), tiles(np.sin(ang))

    tables = np.concatenate([np.eye(P, dtype=np.float32), *rope(HD), *rope(RHD)], axis=1).astype(np.float32)
    delta = (np.arange(DELTA)[None, :] - (NT - 1) * P - np.arange(P)[:, None]).astype(np.float32)
    return tables, delta


def slabs_of(w, width):
    per = SLAB // width
    k = w.shape[0] // P
    return w.reshape(k // per, per, P, width).transpose(0, 2, 1, 3).reshape(k // per, P, SLAB)


def pack(w_in, w_attn_o, w_ret_o, w_out, w_up, w_down, w_ple_gate, w_ple):
    import numpy as np

    a = NH * HD
    kv = 2 * KV * HD
    cols = lambda w, c: slabs_of(w[:, c:c + C], C)
    parts = [cols(w_ple, 0), slabs_of(w_in[:, a:a + kv], kv), cols(w_in, 0), cols(w_ple, C)]
    parts += [cols(w_in, a + kv + n * C) for n in range(8)]
    parts += [cols(w, n * C) for w in (w_attn_o, w_ret_o, w_out) for n in range(2)]
    parts += [cols(w_up, 0)]
    for f in range(NF):
        if f + 1 < NF:
            parts.append(cols(w_up, (f + 1) * C))
        parts += [cols(w_down[f * C:(f + 1) * C], n * C) for n in range(2)]
    parts += [cols(w_ple_gate, n * C) for n in range(2)]
    return np.concatenate(parts)


def kernel(**inputs):
    import numpy as np
    import concourse.bacc as bacc
    from concourse.bass_utils import run_bass_kernel_spmd

    a = {k: np.asarray(v) for k, v in inputs.items()}
    tables, delta = shape_tables()
    norms = np.concatenate([a[n][0].reshape(KD, P).T for n in ("mix_norm", "mlp_norm", "ple_norm")], axis=1)
    arrays = {
        "slabs": pack(*(a[n][0] for n in ("w_in", "w_attn_o", "w_ret_o", "w_out", "w_up", "w_down",
                                          "w_ple_gate", "w_ple"))),
        "x": a["x"][0], "p": a["p"][0, 0], "tables": tables, "delta": delta, "norms": norms,
        "q_gain": a["attn_q_norm"][0], "k_gain": a["attn_k_norm"][0], "ret_gain": a["ret_norm_gain"][0],
        "final_gain": a["final_norm"], "decay": a["ret_decay_logit"][0].reshape(-1),
    }
    arrays = {f"in_{k}": np.ascontiguousarray(v) for k, v in arrays.items()}
    nc = bacc.Bacc("TRN2", target_bir_lowering=False, num_devices=1)
    args = [nc.dram_tensor(k, v.shape, F32, kind="ExternalInput").ap() for k, v in arrays.items()]
    args.append(nc.dram_tensor("ple_spill", [P, 4096], F32).ap())
    args.append(nc.dram_tensor("out_x", [SEQ, D], F32, kind="ExternalOutput").ap())
    build(nc, *args)
    r = run_bass_kernel_spmd(nc, [arrays], core_ids=[0])
    return r.results[0]["out_x"].reshape(1, SEQ, D)
```
